# Optimizing a Trainium2 kernel written in Bass

```python
import math
import jax
import jax.numpy as jnp
from jax import lax
import numpy as np
import jax, jax.numpy as jnp

D_MODEL = 1024
BATCH = 1
SEQ = 256
DEPTH = 2

GRID_W = 64
CTX_LEN = 256
HEAD_DIM = 64
MIX_WIDTH = 1024
N_MOD = 9
FFN_HIDDEN = 2816
NORM_EPS = 1e-6
FOURIER_GROUPS = 4
FOURIER_WIDTH = FOURIER_GROUPS * HEAD_DIM
GLA_HEADS = 6
GLA_DK = 64
GLA_DV = 128
GLA_GATE_RANK = 16
GLA_TAU = 16.0
GLA_CHUNK = 64
CONV_GROUPS = 4
CONV_WIDTH = CONV_GROUPS * HEAD_DIM
CONV_TAPS = 3
DIFF_HEADS = 6
DIFF_DV = 2 * HEAD_DIM
Q_BLOCK = 128
ROPE_THETA = 10000.0
ROPE_AXIS_DIM = HEAD_DIM // 2
N_EVEN = (DEPTH + 1) // 2
N_ODD = DEPTH // 2
EVEN_SPLITS = (FOURIER_WIDTH, GLA_HEADS * GLA_DK, GLA_HEADS * GLA_DK, GLA_HEADS * GLA_DV, GLA_HEADS * GLA_DV, GLA_GATE_RANK, GLA_GATE_RANK)
EVEN_IN = sum(EVEN_SPLITS)
ODD_SPLITS = (CONV_WIDTH, CONV_WIDTH, CONV_WIDTH, DIFF_HEADS * 2 * HEAD_DIM, DIFF_HEADS * 2 * HEAD_DIM, DIFF_HEADS * DIFF_DV)
ODD_IN = sum(ODD_SPLITS)


def _split(z, sizes):
    idx = [int(i) for i in np.cumsum(sizes)[:-1]]
    return jnp.split(z, idx, axis=-1)

def _rmsnorm(x, g):
    xf = x.astype(jnp.float32)
    y = xf * lax.rsqrt(jnp.mean(xf * xf, axis=-1, keepdims=True) + NORM_EPS)
    return (y * g.astype(jnp.float32)).astype(x.dtype)

def _modulation(cond, w, b):
    m = jax.nn.silu(cond) @ w + b
    return jnp.split(m[..., None, :], N_MOD, axis=-1)

def _prenorm(h, gain, shift, scale):
    return _rmsnorm(h, gain) * (1.0 + scale) + shift

def _swiglu(h, w_in, w_out):
    g, u = jnp.split(h @ w_in, 2, axis=-1)
    return (jax.nn.silu(g) * u) @ w_out

def _axial_rope_tables(rows):
    row = jnp.repeat(jnp.arange(rows), GRID_W).astype(jnp.float32)
    col = jnp.tile(jnp.arange(GRID_W), rows).astype(jnp.float32)
    n = ROPE_AXIS_DIM // 2
    inv = ROPE_THETA ** (-jnp.arange(n, dtype=jnp.float32) / n)
    ang = jnp.concatenate([row[:, None] * inv, col[:, None] * inv], axis=-1)
    return jnp.cos(ang), jnp.sin(ang)

def _axial_rope(x, cos, sin):
    n = ROPE_AXIS_DIM // 2
    def rot(part, cs, sn):
        p1, p2 = jnp.split(part, 2, axis=-1)
        return jnp.concatenate([p1 * cs - p2 * sn, p1 * sn + p2 * cs], axis=-1)
    bc = lambda t: t[:, None, None, :]
    xr = rot(x[..., :ROPE_AXIS_DIM], bc(cos[:, :n]), bc(sin[:, :n]))
    xc = rot(x[..., ROPE_AXIS_DIM:], bc(cos[:, n:]), bc(sin[:, n:]))
    return jnp.concatenate([xr, xc], axis=-1).astype(x.dtype)

def _fourier_mix(z):
    bn, t, _ = z.shape
    zf = z.astype(jnp.float32).reshape(bn, t, FOURIER_GROUPS, HEAD_DIM)
    y = jnp.fft.fft2(zf, axes=(1, 3), norm='ortho').real
    return y.reshape(bn, t, FOURIER_WIDTH).astype(z.dtype)

def _gla_chunked(q, k, v, logg, s0):
    bn, h, t, dk = q.shape
    dv = v.shape[-1]
    n = t // GLA_CHUNK
    def chunks(a):
        return jnp.moveaxis(a.reshape(bn, h, n, GLA_CHUNK, a.shape[-1]), 2, 0)
    b = jnp.cumsum(chunks(logg), axis=-2)
    mask = jnp.tril(jnp.ones((GLA_CHUNK, GLA_CHUNK), dtype=bool))
    def step(s, inp):
        qc, kc, vc, bc = inp
        bl = bc[..., -1:, :]
        qd = qc * jnp.exp(bc)
        kd = kc * jnp.exp(-bc)
        att = jnp.where(mask, jnp.einsum('bhid,bhjd->bhij', qd, kd), 0.0)
        o = jnp.einsum('bhid,bhdv->bhiv', qd, s) + jnp.einsum('bhij,bhjv->bhiv', att, vc)
        s = s * jnp.exp(bl)[..., 0, :, None] + jnp.einsum('bhjd,bhjv->bhdv', kc * jnp.exp(bl - bc), vc)
        return s, o
    s, o = lax.scan(step, s0, (chunks(q), chunks(k), chunks(v), b))
    return jnp.moveaxis(o, 0, 2).reshape(bn, h, t, dv), s

def _even_mixer(z, s0_f, s0_b, gate_w, gate_b, gla_g):
    bn, t, _ = z.shape
    z_f, zq, zk, zv, zr, zgf, zgb = _split(z, EVEN_SPLITS)
    y_f = _fourier_mix(z_f)
    def heads(a, d):
        return a.astype(jnp.float32).reshape(bn, t, GLA_HEADS, d).transpose(0, 2, 1, 3)
    q = heads(zq, GLA_DK) * (GLA_DK ** -0.5)
    k = heads(zk, GLA_DK)
    v = heads(zv, GLA_DV)
    gw = gate_w.astype(jnp.float32)
    gb = gate_b.astype(jnp.float32)
    logg_f = heads(jax.nn.log_sigmoid(zgf.astype(jnp.float32) @ gw[0] + gb[0]), GLA_DK) / GLA_TAU
    logg_b = heads(jax.nn.log_sigmoid(zgb.astype(jnp.float32) @ gw[1] + gb[1]), GLA_DK) / GLA_TAU
    flip = lambda a: jnp.flip(a, axis=2)
    o_f, s_f = _gla_chunked(q, k, v, logg_f, s0_f)
    o_b, s_b = _gla_chunked(flip(q), flip(k), flip(v), flip(logg_b), s0_b)
    o = (o_f + flip(o_b)).transpose(0, 2, 1, 3)
    o = _rmsnorm(o, gla_g) * jax.nn.silu(zr.astype(jnp.float32).reshape(bn, t, GLA_HEADS, GLA_DV))
    y_g = o.reshape(bn, t, GLA_HEADS * GLA_DV).astype(z.dtype)
    return jnp.concatenate([y_f, y_g], axis=-1), s_f, s_b

def _short_conv(zb, zc, zx, w, b):
    u = zc * zx
    t = u.shape[1]
    up = jnp.pad(u, ((0, 0), (1, 1), (0, 0)))
    y = up[:, 0:t] * w[0] + up[:, 1:t + 1] * w[1] + up[:, 2:t + 2] * w[2] + b
    return zb * y

def _odd_parts(z):
    bn, t, _ = z.shape
    zb, zc, zx, q, k, v = _split(z, ODD_SPLITS)
    q = q.reshape(bn, t, DIFF_HEADS, 2, HEAD_DIM)
    k = k.reshape(bn, t, DIFF_HEADS, 2, HEAD_DIM)
    v = v.reshape(bn, t, DIFF_HEADS, DIFF_DV)
    return zb, zc, zx, q, k, v

def _diff_attn(q, k, v, lam):
    s = jnp.einsum('bqhsd,bkhsd->bhsqk', q, k, preferred_element_type=jnp.float32) * (HEAD_DIM ** -0.5)
    p = jax.nn.softmax(s, axis=-1)
    a = p[:, :, 0] - lam * p[:, :, 1]
    return jnp.einsum('bhqk,bkhv->bqhv', a, v.astype(jnp.float32))

def _diff_attn_blocked(q, k, v, lam):
    bn, t = q.shape[:2]
    nb = t // Q_BLOCK
    qb = jnp.moveaxis(q.reshape(bn, nb, Q_BLOCK, DIFF_HEADS, 2, HEAD_DIM), 1, 0)
    o = lax.map(lambda blk: _diff_attn(blk, k, v, lam), qb)
    return jnp.moveaxis(o, 0, 1).reshape(bn, t, DIFF_HEADS, DIFF_DV)

def _subln(o, g, lam_init, dtype):
    bn, t = o.shape[:2]
    return (_rmsnorm(o, g) * (1.0 - lam_init)).reshape(bn, t, DIFF_HEADS * DIFF_DV).astype(dtype)

def _odd_mixer(zl, zc, cos, sin, conv_w, conv_b, lam, lam_init, dnorm, with_ctx_out):
    lat = _odd_parts(zl)
    cx = _odd_parts(zc)
    ql = _axial_rope(lat[3], cos, sin)
    kl = _axial_rope(lat[4], cos, sin)
    k_all = jnp.concatenate([kl, cx[4]], axis=1)
    v_all = jnp.concatenate([lat[5], cx[5]], axis=1)
    att_l = _diff_attn_blocked(ql, k_all, v_all, lam)
    y_l = jnp.concatenate([_short_conv(lat[0], lat[1], lat[2], conv_w, conv_b),
                           _subln(att_l, dnorm, lam_init, zl.dtype)], axis=-1)
    if not with_ctx_out:
        return y_l, None
    att_c = _diff_attn(cx[3], cx[4], cx[5], lam)
    y_c = jnp.concatenate([_short_conv(cx[0], cx[1], cx[2], conv_w, conv_b),
                           _subln(att_c, dnorm, lam_init, zc.dtype)], axis=-1)
    return y_l, y_c

def first_inputs(seed: int = 0) -> dict:
    key = jax.random.key(seed)
    ks = jax.random.split(key, 28)
    nrm = lambda k, shape, s: jax.random.normal(k, shape, jnp.float32) * s
    gain = lambda k, shape: 1.0 + 0.05 * jax.random.normal(k, shape, jnp.float32)
    D = D_MODEL
    return {
        'x': nrm(ks[0], (BATCH, SEQ, D), 1.0),
        'c': nrm(ks[1], (BATCH, D), 1.0),
        'ctx': nrm(ks[2], (BATCH, CTX_LEN, D), 1.0),
        'c_ctx': nrm(ks[3], (D,), 1.0),
        'ada_w': nrm(ks[4], (DEPTH, D, N_MOD * D), 0.5 * D ** -0.5),
        'ada_b': nrm(ks[5], (DEPTH, N_MOD * D), 0.01),
        'norm_ffn1': gain(ks[6], (DEPTH, D)),
        'norm_mix': gain(ks[7], (DEPTH, D)),
        'norm_ffn2': gain(ks[8], (DEPTH, D)),
        'ffn1_w_in': nrm(ks[9], (DEPTH, D, 2 * FFN_HIDDEN), D ** -0.5),
        'ffn1_w_out': nrm(ks[10], (DEPTH, FFN_HIDDEN, D), FFN_HIDDEN ** -0.5),
        'ffn2_w_in': nrm(ks[11], (DEPTH, D, 2 * FFN_HIDDEN), D ** -0.5),
        'ffn2_w_out': nrm(ks[12], (DEPTH, FFN_HIDDEN, D), FFN_HIDDEN ** -0.5),
        'mix_w_out': nrm(ks[13], (DEPTH, MIX_WIDTH, D), MIX_WIDTH ** -0.5),
        'even_w_in': nrm(ks[14], (N_EVEN, D, EVEN_IN), D ** -0.5),
        'gla_gate_w': nrm(ks[15], (N_EVEN, 2, GLA_GATE_RANK, GLA_HEADS * GLA_DK), GLA_GATE_RANK ** -0.5),
        'gla_gate_b': nrm(ks[16], (N_EVEN, 2, GLA_HEADS * GLA_DK), 0.1),
        'gla_norm': gain(ks[17], (N_EVEN, GLA_DV)),
        'odd_w_in': nrm(ks[18], (N_ODD, D, ODD_IN), D ** -0.5),
        'conv_w': nrm(ks[19], (N_ODD, CONV_TAPS, CONV_WIDTH), CONV_TAPS ** -0.5),
        'conv_b': nrm(ks[20], (N_ODD, CONV_WIDTH), 0.01),
        'lambda_q1': nrm(ks[21], (N_ODD, HEAD_DIM), 0.1),
        'lambda_k1': nrm(ks[22], (N_ODD, HEAD_DIM), 0.1),
        'lambda_q2': nrm(ks[23], (N_ODD, HEAD_DIM), 0.1),
        'lambda_k2': nrm(ks[24], (N_ODD, HEAD_DIM), 0.1),
        'diff_norm': gain(ks[25], (N_ODD, DIFF_DV)),
        'final_norm': gain(ks[26], (D,)),
    }

def first_block(x, c, ctx, c_ctx, ada_w, ada_b, norm_ffn1, norm_mix, norm_ffn2, ffn1_w_in, ffn1_w_out,
              ffn2_w_in, ffn2_w_out, mix_w_out, even_w_in, gla_gate_w, gla_gate_b, gla_norm, odd_w_in,
              conv_w, conv_b, lambda_q1, lambda_k1, lambda_q2, lambda_k2, diff_norm, final_norm):
    bn = x.shape[0]
    rows = x.shape[1] // GRID_W
    cos, sin = _axial_rope_tables(rows)
    h, hc = x, ctx
    for layer in range(DEPTH):
        last = layer == DEPTH - 1
        sh1, sc1, g1, shm, scm, gm, sh2, sc2, g2 = _modulation(c, ada_w[layer], ada_b[layer])
        csh1, csc1, cg1, cshm, cscm, cgm, csh2, csc2, cg2 = _modulation(c_ctx, ada_w[layer], ada_b[layer])
        h = h + 0.5 * g1 * _swiglu(_prenorm(h, norm_ffn1[layer], sh1, sc1), ffn1_w_in[layer], ffn1_w_out[layer])
        hc = hc + 0.5 * cg1 * _swiglu(_prenorm(hc, norm_ffn1[layer], csh1, csc1), ffn1_w_in[layer], ffn1_w_out[layer])
        if layer % 2 == 0:
            i = layer // 2
            w_in = even_w_in[i]
            zl = _prenorm(h, norm_mix[layer], shm, scm) @ w_in
            zc = _prenorm(hc, norm_mix[layer], cshm, cscm) @ w_in
            s0 = jnp.zeros((bn, GLA_HEADS, GLA_DK, GLA_DV), jnp.float32)
            mix_c, s_f, s_b = _even_mixer(zc, s0, s0, gla_gate_w[i], gla_gate_b[i], gla_norm[i])
            mix_l, _, _ = _even_mixer(zl, s_f, s_b, gla_gate_w[i], gla_gate_b[i], gla_norm[i])
        else:
            i = layer // 2
            w_in = odd_w_in[i]
            zl = _prenorm(h, norm_mix[layer], shm, scm) @ w_in
            zc = _prenorm(hc, norm_mix[layer], cshm, cscm) @ w_in
            lam_init = 0.8 - 0.6 * math.exp(-0.3 * layer)
            lam = (jnp.exp(jnp.sum(lambda_q1[i].astype(jnp.float32) * lambda_k1[i].astype(jnp.float32)))
                   - jnp.exp(jnp.sum(lambda_q2[i].astype(jnp.float32) * lambda_k2[i].astype(jnp.float32)))
                   + lam_init)
            mix_l, mix_c = _odd_mixer(zl, zc, cos, sin, conv_w[i], conv_b[i], lam, lam_init, diff_norm[i],
                                      not last)
        h = h + gm * (mix_l @ mix_w_out[layer])
        h = h + 0.5 * g2 * _swiglu(_prenorm(h, norm_ffn2[layer], sh2, sc2), ffn2_w_in[layer], ffn2_w_out[layer])
        if not last:
            hc = hc + cgm * (mix_c @ mix_w_out[layer])
            hc = hc + 0.5 * cg2 * _swiglu(_prenorm(hc, norm_ffn2[layer], csh2, csc2), ffn2_w_in[layer], ffn2_w_out[layer])
    return _rmsnorm(h, final_norm)


N_MIXERS = 2
RET_QK_DIM = 256
RET_HEADS = D_MODEL // RET_QK_DIM
RET_V_DIM = 2 * RET_QK_DIM
RET_QK = RET_HEADS * RET_QK_DIM
RET_V = RET_HEADS * RET_V_DIM
RET_CHUNK = 128
ROPE_BASE = 10000.0
DILATED_PAIRS = ((128, 1), (512, 4), (2048, 16))
ATT_GROUPS = 3
ATT_HEAD_DIM = 64
ATT_HEADS = D_MODEL // ATT_HEAD_DIM
ATT_GROUP_W = ATT_HEADS * ATT_HEAD_DIM
BAND_BLOCK = 128
NUM_BUCKETS = 32
MAX_DISTANCE = 2048
D_FF = ((8 * D_MODEL + 3 * 256 - 1) // (3 * 256)) * 256
DEEPNORM_ALPHA = (2 * DEPTH) ** 0.25
DEEPNORM_BETA = (8 * DEPTH) ** -0.25
LN_EPS = 1e-5
GN_EPS = 1e-5


def _layer_norm(x, g, b):
    xf = x.astype(jnp.float32)
    mu = jnp.mean(xf, axis=-1, keepdims=True)
    var = jnp.mean(jnp.square(xf - mu), axis=-1, keepdims=True)
    y = (xf - mu) * lax.rsqrt(var + LN_EPS) * g.astype(jnp.float32) + b.astype(jnp.float32)
    return y.astype(x.dtype)

def _rope(x):
    B, T, H, d = x.shape
    inv = 1.0 / (ROPE_BASE ** jnp.linspace(0.0, 1.0, d // 2, dtype=jnp.float32))
    ang = jnp.arange(T, dtype=jnp.float32)[:, None] * inv[None, :]
    c = jnp.cos(ang)[None, :, None, :]
    s = jnp.sin(ang)[None, :, None, :]
    xp = x.reshape(B, T, H, d // 2, 2)
    a, b = xp[..., 0], xp[..., 1]
    return jnp.stack([a * c - b * s, a * s + b * c], axis=-1).reshape(B, T, H, d)

def retention(x, w_in, w_out):
    B, T, _ = x.shape
    H, dk, dv, C = RET_HEADS, RET_QK_DIM, RET_V_DIM, RET_CHUNK
    N = T // C
    proj = x @ w_in
    q, k, v, gate = jnp.split(proj, [RET_QK, 2 * RET_QK, 2 * RET_QK + RET_V], axis=-1)
    q = _rope(q.reshape(B, T, H, dk).astype(jnp.float32))
    k = _rope(k.reshape(B, T, H, dk).astype(jnp.float32)) * (dk ** -0.5)
    v = v.reshape(B, T, H, dv).astype(jnp.float32)

    def to_chunks(t):
        return t.reshape(B, N, C, H, t.shape[-1]).transpose(1, 0, 3, 2, 4)

    qc, kc, vc = to_chunks(q), to_chunks(k), to_chunks(v)
    log_gamma = jnp.log(1.0 - 2.0 ** (-5.0 - jnp.arange(H, dtype=jnp.float32)))
    idx = jnp.arange(C, dtype=jnp.float32)
    diff = idx[:, None] - idx[None, :]
    intra = jnp.where(diff[None] >= 0,
                      jnp.exp(jnp.maximum(diff, 0.0)[None] * log_gamma[:, None, None]), 0.0)
    xi = jnp.exp((idx[None, :] + 1.0) * log_gamma[:, None])[..., None]
    zeta = jnp.exp((C - 1.0 - idx[None, :]) * log_gamma[:, None])[..., None]
    gamma_c = jnp.exp(C * log_gamma)[:, None, None]

    def body(state, inp):
        qi, ki, vi = inp
        s = jnp.einsum('bhid,bhjd->bhij', qi, ki) * intra
        inner = jnp.einsum('bhij,bhje->bhie', s, vi)
        cross = jnp.einsum('bhid,bhde->bhie', qi * xi, state)
        state = gamma_c * state + jnp.einsum('bhjd,bhje->bhde', ki * zeta, vi)
        return state, inner + cross

    state0 = jnp.zeros((B, H, dk, dv), jnp.float32)
    _, y = lax.scan(body, state0, (qc, kc, vc))
    y = y.transpose(1, 0, 3, 2, 4).reshape(B, T, H, dv)
    mu = jnp.mean(y, axis=-1, keepdims=True)
    var = jnp.mean(jnp.square(y - mu), axis=-1, keepdims=True)
    y = ((y - mu) * lax.rsqrt(var + GN_EPS)).reshape(B, T, RET_V).astype(x.dtype)
    return (jax.nn.silu(gate) * y) @ w_out

def _t5_bucket(dist):
    max_exact = NUM_BUCKETS // 2
    d_f = jnp.maximum(dist, 1).astype(jnp.float32)
    large = max_exact + (jnp.log(d_f / max_exact) / math.log(MAX_DISTANCE / max_exact)
                         * (NUM_BUCKETS - max_exact)).astype(jnp.int32)
    large = jnp.minimum(large, NUM_BUCKETS - 1)
    return jnp.where(dist < max_exact, dist, large)

def _dilated_group(q, k, v, bias_table, window, dil):
    B, H, T, hd = q.shape
    blk = BAND_BLOCK
    steps = window // dil
    L = T // dil
    nb = -(-L // blk)
    Lp = nb * blk

    def to_blocks(t):
        t = t.reshape(B, H, L, dil, hd).transpose(0, 1, 3, 2, 4)
        t = jnp.pad(t, ((0, 0), (0, 0), (0, 0), (0, Lp - L), (0, 0)))
        return t.reshape(B, H, dil, nb, blk, hd)

    def band(t):
        prev = jnp.pad(t, ((0, 0), (0, 0), (0, 0), (1, 0), (0, 0), (0, 0)))[:, :, :, :-1]
        return jnp.concatenate([prev, t], axis=4)

    qb = to_blocks(q)
    kw = band(to_blocks(k))
    vw = band(to_blocks(v))
    qi = jnp.arange(blk)[:, None]
    kj = jnp.arange(2 * blk)[None, :]
    delta = qi + blk - kj
    band_ok = (delta >= 0) & (delta <= steps)
    key_ok = (jnp.arange(nb)[:, None, None] * blk - blk + kj[None]) >= 0
    mask = band_ok[None] & key_ok
    bucket = _t5_bucket(jnp.maximum(delta, 0) * dil)
    bias = bias_table[:, bucket].astype(jnp.float32)

    s = jnp.einsum('bhrnqd,bhrnkd->bhrnqk', qb, kw).astype(jnp.float32) * (hd ** -0.5)
    s = s + bias[None, :, None, None]
    s = jnp.where(mask[None, None, None], s, -jnp.inf)
    m = jnp.max(s, axis=-1, keepdims=True)
    e = jnp.exp(s - m)
    den = jnp.sum(e, axis=-1, keepdims=True)
    p = e / den
    lse = (m + jnp.log(den))[..., 0]
    o = jnp.einsum('bhrnqk,bhrnkd->bhrnqd', p.astype(v.dtype), vw)
    o = o.reshape(B, H, dil, Lp, hd)[:, :, :, :L].transpose(0, 1, 3, 2, 4).reshape(B, H, T, hd)
    lse = lse.reshape(B, H, dil, Lp)[..., :L].transpose(0, 1, 3, 2).reshape(B, H, T)
    return o, lse

def dilated_attention(x, w_in, w_out, rel_bias):
    B, T, _ = x.shape
    proj = (x @ w_in).reshape(B, T, 3, ATT_GROUPS, ATT_HEADS, ATT_HEAD_DIM)
    proj = proj.transpose(2, 3, 0, 4, 1, 5)
    outs, lses = [], []
    for g, (window, dil) in enumerate(DILATED_PAIRS):
        o, lse = _dilated_group(proj[0, g], proj[1, g], proj[2, g],
                                rel_bias[g * ATT_HEADS:(g + 1) * ATT_HEADS], window, dil)
        outs.append(o)
        lses.append(lse)
    w = jax.nn.softmax(jnp.stack(lses, axis=0), axis=0)
    o = jnp.sum(w[..., None] * jnp.stack(outs, axis=0).astype(jnp.float32), axis=0)
    o = o.transpose(0, 2, 1, 3).reshape(B, T, ATT_GROUP_W).astype(x.dtype)
    return o @ w_out

def swiglu_ffn(x, w_up, w_down):
    gate, up = jnp.split(x @ w_up, 2, axis=-1)
    return (jax.nn.silu(gate) * up) @ w_down

def second_inputs(seed: int = 0) -> dict:
    key = jax.random.key(seed)
    ks = jax.random.split(key, 10)
    n_ret = (DEPTH + 1) // 2
    n_att = DEPTH // 2
    f32 = jnp.float32
    x = jax.random.normal(ks[0], (BATCH, SEQ, D_MODEL), f32)
    ret_w_in = jax.random.normal(ks[1], (n_ret, D_MODEL, 2 * RET_QK + 2 * RET_V), f32) * D_MODEL ** -0.5
    ret_w_out = jax.random.normal(ks[2], (n_ret, RET_V, D_MODEL), f32) * (RET_V ** -0.5 * DEEPNORM_BETA)
    attn_w_in = jax.random.normal(ks[3], (n_att, D_MODEL, 3 * ATT_GROUPS * ATT_GROUP_W), f32) * D_MODEL ** -0.5
    attn_w_out = jax.random.normal(ks[4], (n_att, ATT_GROUP_W, D_MODEL), f32) * (ATT_GROUP_W ** -0.5 * DEEPNORM_BETA)
    rel_bias = jax.random.normal(ks[5], (ATT_GROUPS * ATT_HEADS, NUM_BUCKETS), f32) * 0.2
    ffn_w_up = jax.random.normal(ks[6], (DEPTH, D_MODEL, 2 * D_FF), f32) * D_MODEL ** -0.5
    ffn_w_down = jax.random.normal(ks[7], (DEPTH, D_FF, D_MODEL), f32) * (D_FF ** -0.5 * DEEPNORM_BETA)
    ln_gain = 1.0 + 0.02 * jax.random.normal(ks[8], (DEPTH, 2, D_MODEL), f32)
    ln_bias = 0.02 * jax.random.normal(ks[9], (DEPTH, 2, D_MODEL), f32)
    return {"x": x, "ret_w_in": ret_w_in, "ret_w_out": ret_w_out,
            "attn_w_in": attn_w_in, "attn_w_out": attn_w_out, "rel_bias": rel_bias,
            "ffn_w_up": ffn_w_up, "ffn_w_down": ffn_w_down,
            "ln_gain": ln_gain, "ln_bias": ln_bias}

def second_block(x, ret_w_in, ret_w_out, attn_w_in, attn_w_out, rel_bias,
              ffn_w_up, ffn_w_down, ln_gain, ln_bias):
    for i in range(DEPTH):
        j = i // N_MIXERS
        if i % N_MIXERS == 0:
            mix = retention(x, ret_w_in[j], ret_w_out[j])
        else:
            mix = dilated_attention(x, attn_w_in[j], attn_w_out[j], rel_bias)
        x = _layer_norm(DEEPNORM_ALPHA * x + mix, ln_gain[i, 0], ln_bias[i, 0])
        x = _layer_norm(DEEPNORM_ALPHA * x + swiglu_ffn(x, ffn_w_up[i], ffn_w_down[i]),
                        ln_gain[i, 1], ln_bias[i, 1])
    return x


def setup_inputs(seed=0):
    out = dict(first_inputs(seed))
    for name, value in second_inputs(seed + 1).items():
        if name != "x":
            out[name + "_2"] = value
    return out


def reference(
    x, c, ctx, c_ctx, ada_w, ada_b, norm_ffn1, norm_mix, norm_ffn2, ffn1_w_in, ffn1_w_out,
    ffn2_w_in, ffn2_w_out, mix_w_out, even_w_in, gla_gate_w, gla_gate_b, gla_norm, odd_w_in,
    conv_w, conv_b, lambda_q1, lambda_k1, lambda_q2, lambda_k2, diff_norm, final_norm,
    ret_w_in_2, ret_w_out_2, attn_w_in_2, attn_w_out_2, rel_bias_2, ffn_w_up_2, ffn_w_down_2,
    ln_gain_2, ln_bias_2,
):
    x = first_block(
        x, c, ctx, c_ctx, ada_w, ada_b, norm_ffn1, norm_mix, norm_ffn2, ffn1_w_in, ffn1_w_out,
        ffn2_w_in, ffn2_w_out, mix_w_out, even_w_in, gla_gate_w, gla_gate_b, gla_norm, odd_w_in,
        conv_w, conv_b, lambda_q1, lambda_k1, lambda_q2, lambda_k2, diff_norm, final_norm,
    )
    return second_block(
        x, ret_w_in_2, ret_w_out_2, attn_w_in_2, attn_w_out_2, rel_bias_2, ffn_w_up_2,
        ffn_w_down_2, ln_gain_2, ln_bias_2,
    )


_drawn_inputs = setup_inputs


def setup_inputs(seed=0):
    import zlib

    import numpy as np

    out = dict(_drawn_inputs(seed))
    spreads = {}
    factors = {'ada_b': 2.928,
     'norm_ffn1': 4.454,
     'norm_ffn2': 4.954,
     'gla_gate_b': 6.765,
     'gla_norm': 5.666,
     'conv_b': 187.438,
     'lambda_q1': 8.0,
     'lambda_k1': 8.0,
     'lambda_q2': 3.47,
     'diff_norm': 25.463,
     'rel_bias_2': 5.267}
    for name, (base, spread) in spreads.items():
        noise = np.random.default_rng([zlib.crc32(name.encode()), seed]).standard_normal(out[name].shape)
        drawn = base * np.exp(spread * noise) if base else spread * noise
        out[name] = jnp.asarray(drawn.astype(out[name].dtype))
    for name, factor in factors.items():
        out[name] = (out[name] * factor).astype(out[name].dtype)
    return out
```

```python
import math
from contextlib import ExitStack

import numpy as np
import concourse.bass as bass
from concourse import mybir

P = 128
F32 = mybir.dt.float32
F32R = mybir.dt.float32r
ALU = mybir.AluOpType
ACT = mybir.ActivationFunctionType
AX = mybir.AxisListType.X

D = 1024
KC = D // P
T = 256
TB = T // P
FFN = 2816
FC = FFN // P
HALVES = ((0, 12), (12, 10))
EPS_RMS = 1e-6
EPS_LN = 1e-5
MODS = 9
GLA_HEADS, GLA_DK, GLA_DV, GLA_CHUNK, GLA_TAU = 6, 64, 128, 64, 16.0
NCH = 2 * T // GLA_CHUNK
DIFF_HEADS, HD = 6, 64
LAM_INIT = 0.8 - 0.6 * math.exp(-0.3)
RET_HEADS, RET_DK, RET_DV = 4, 256, 512
ATT_HEADS, ATT_GROUPS = 16, 3
DILATED = ((128, 1), (512, 4), (2048, 16))
NUM_BUCKETS, MAX_DISTANCE = 32, 2048
ALPHA = 4 ** 0.25
NEG = -1e30

SMALL = [("cond", 2 * KC), ("ada_b", 2 * MODS * KC), ("norm_ffn1", 2 * KC), ("norm_mix", 2 * KC),
         ("norm_ffn2", 2 * KC), ("final_norm", KC), ("gate_b", 6), ("gla_norm", 1), ("conv_w", 6),
         ("conv_b", 2), ("lambdas", 4), ("diff_norm", 1), ("ln_gain", 4 * KC), ("ln_bias", 4 * KC),
         ("rel_bias", 48)]
SMALL_AT = {}
_at = 0
for _name, _n in SMALL:
    SMALL_AT[_name] = (_at, _at + _n)
    _at += _n
SMALL_N = _at

XN, MID, TEMPS, WORK = 0, 32768, 93568, 107904
UNIT = 2048
NRAW, NSPLIT = 4, 3


class Engine:

    def __init__(self, sem):
        self.sem, self.count, self.steps, self.first = sem, 0, [], []

    def do(self, op, *after, signal=True):
        waits = [t for t in (*self.first, *after) if t is not None]
        self.first = []
        self.steps.append([waits, op, signal])
        if signal:
            self.count += 1
            return (self.sem, self.count)
        return None

    def last(self):
        if not self.steps:
            return None
        if not self.steps[-1][2]:
            self.steps[-1][2] = True
            self.count += 1
        return (self.sem, self.count)

    def emit(self, eng):
        seen = {}
        for waits, op, signal in self.steps:
            need = {}
            for sem, value in waits:
                if value > max(seen.get(sem.name, 0), need.get(sem.name, (None, 0))[1]):
                    need[sem.name] = (sem, value)
            for name, (sem, value) in need.items():
                eng.wait_ge(sem, value)
                seen[name] = value
            ins = op(eng)
            if signal:
                ins.then_inc(self.sem, 1)


class Banks:

    def __init__(self, tiles):
        self.tiles, self.order, self.readers = tiles, list(range(len(tiles))), [()] * len(tiles)

    def take(self):
        b = self.order.pop(0)
        return b, self.tiles[b], self.readers[b]

    def free(self, b, *readers):
        self.readers[b] = readers
        self.order.append(b)


class Unit:
    pass


class Recorder:

    def __init__(self, hi, lo, raw):
        self.plan, self.tiles = [], (hi, lo, raw)

    def take(self, w, k0, kn, c0, cn, split=True):
        self.plan.append((w, k0, kn, c0, cn, split))
        u = Unit()
        u.hi, u.lo, u.raw = (t[:, 0, 0:kn * cn].rearrange("p (k c) -> p k c", k=kn) for t in self.tiles)
        u.ready = ()
        return u

    def done(self, unit, token):
        pass


class Weights:

    def __init__(self, plan, hi, lo, raw, sync, sems, act, dve, pool):
        self.plan, self.hi, self.lo, self.raw = plan, hi, lo, raw
        self.sync, self.sems, self.act, self.dve, self.pool = sync, sems, act, dve, pool
        self.loaded = self.split = self.taken = 0
        self.raw_free = [()] * NRAW
        self.split_free = [()] * NSPLIT
        self.split_slot = 0
        self.units = []

    def load_tile(self):
        i = self.loaded
        w, k0, kn, c0, cn, split = self.plan[i]
        slot = i % NRAW
        u = Unit()
        u.index, u.slot, u.is_split = i, slot, split
        u.raw = self.raw[:, slot, 0:kn * cn].rearrange("p (k c) -> p k c", k=kn)
        src = w[k0 * P:(k0 + kn) * P, c0:c0 + cn].rearrange("(k p) c -> p k c", p=P)
        self.sync.do(lambda e: e.dma_start(u.raw, src).then_inc(self.sems[slot], 16), *self.raw_free[slot], signal=False)
        u.loaded = (self.sems[slot], 16 * (i // NRAW + 1))
        u.ready = (u.loaded,)
        self.raw_free[slot] = None
        self.units.append(u)
        self.loaded += 1

    def split_tile(self, u):
        s = self.split_slot
        _, k0, kn, c0, cn, _ = self.plan[u.index]
        n = kn * cn
        raw, hi, lo = self.raw[:, u.slot, 0:n], self.hi[:, s, 0:n], self.lo[:, s, 0:n]
        u.hi = hi.rearrange("p (k c) -> p k c", k=kn)
        u.lo = lo.rearrange("p (k c) -> p k c", k=kn)
        a = self.act.do(lambda e: e.activation(hi, raw, ACT.Copy), u.loaded, *self.split_free[s])
        b = self.dve.do(lambda e: e.tensor_tensor(lo, raw, hi.bitcast(F32), ALU.subtract), a, u.loaded,
                        *self.split_free[s])
        u.ready = (a, b)
        self.raw_free[u.slot] = (a, b)
        self.split_free[s] = None
        u.split_slot = s
        self.split_slot = (s + 1) % NSPLIT
        self.split += 1

    def pump(self):
        moved = True
        while moved:
            moved = False
            if self.loaded < len(self.plan) and self.raw_free[self.loaded % NRAW] is not None:
                self.load_tile()
                moved = True
            if self.split < self.loaded:
                u = self.units[self.split]
                if not u.is_split:
                    self.split += 1
                    moved = True
                elif self.split_free[self.split_slot] is not None:
                    self.split_tile(u)
                    moved = True

    def take(self, w, k0, kn, c0, cn, split=True):
        self.pump()
        u = self.units[self.taken]
        assert self.taken < self.split and self.plan[self.taken][1:] == (k0, kn, c0, cn, split)
        self.taken += 1
        return u

    def done(self, u, token):
        if u.is_split:
            self.split_free[u.split_slot] = (token,)
        else:
            self.raw_free[u.slot] = (token,)
        self.pump()


class Program:
    def __init__(self, nc, io, handles, engines, stream):
        self.nc, self.io, self.h = nc, io, handles
        self.pe, self.act_e, self.dve, self.pool, self.sync = engines
        self.w = stream
        self.banks = Banks(handles["psum"])
        self.ada_next = 0
        self.loads = 0
        self.mod_ready = {}

    def mm(self, out, lhsT, rhs, start, stop, *after, signal=False, loose=False):
        return self.pe.do(lambda e: e.matmul(out, lhsT, rhs, start=start, stop=stop,
                                             skip_group_check=loose), *after, signal=signal)

    def transpose(self, out, in_, *after, signal=False):
        ident = self.h["ident"]
        return self.pe.do(lambda e: e.transpose(out, in_, ident[:, :]), *after, signal=signal)

    def act(self, out, in_, func, *after, scale=1.0, bias=0.0, accum=None):
        if accum is None:
            return self.act_e.do(lambda e: e.activation(out, in_, func, bias=bias, scale=scale), *after)
        return self.act_e.do(lambda e: e.activation(out, in_, func, bias=bias, scale=scale,
                                                    accum_out=accum), *after)

    def tt(self, out, a, b, op, *after, eng=None):
        return (eng or self.dve).do(lambda e: e.tensor_tensor(out, a, b, op), *after)

    def ts(self, out, a, s1, s2, op0, op1, *after, eng=None):
        if s2 is None:
            return (eng or self.dve).do(lambda e: e.tensor_scalar(out, a, s1, None, op0), *after)
        return (eng or self.dve).do(lambda e: e.tensor_scalar(out, a, s1, s2, op0, op1), *after)

    def stt(self, out, a, s, b, op0, op1, *after):
        return self.dve.do(lambda e: e.scalar_tensor_tensor(out, a, s, b, op0, op1), *after)

    def recip(self, out, a, *after):
        return self.dve.do(lambda e: e.reciprocal(out, a), *after)

    def rmax(self, out, a, *after):
        return self.dve.do(lambda e: e.tensor_reduce(out, a, AX, ALU.max, negate=True), *after)

    def copy(self, out, a, *after):
        return self.dve.do(lambda e: e.tensor_copy(out, a), *after)

    def load(self, dst, src, *after):
        sem = self.h["load_sems"][self.loads]
        self.loads += 1
        self.sync.do(lambda e: e.dma_start(dst, src).then_inc(sem, 16), *after, signal=False)
        return (sem, 16)

    def place(self, name, at, shape, dtype=F32):
        key = (name, at)
        if key not in self.h["placed"]:
            self.h["placed"][key] = self.nc.alloc_sbuf_tensor_at(name, shape, dtype, offset=self.h["work"] + at)
        return self.h["placed"][key]

    def barrier(self):
        tokens = [e.last() for e in (self.pe, self.act_e, self.dve, self.pool)]
        for e in (self.pe, self.act_e, self.dve, self.pool):
            e.first = list(tokens)
        return tokens

    def small(self, name, a=0, b=None):
        s, e = SMALL_AT[name]
        return self.h["small"][:, s + a:(e if b is None else s + b)]

    def product3(self, out, a_hi, a_lo, b_hi, b_lo, start, stop, *after, signal=False):
        self.mm(out, a_hi, b_hi, start, False, *after)
        self.mm(out, a_hi, b_lo, False, False)
        return self.mm(out, a_lo, b_hi, False, stop, signal=signal)

    def project(self, u, c, x, n, bank, after, ks=range(KC), k0=0, start=True, stop=True, cols=0):
        ks = list(ks)
        for i, k in enumerate(ks):
            t = self.product3(bank[:, 0:n], u.hi[:, k - k0, c:c + P], u.lo[:, k - k0, c:c + P],
                              x.hi[:, k, cols:cols + n], x.lo[:, k, cols:cols + n],
                              start and i == 0, stop and i == len(ks) - 1,
                              *u.ready, *x.ready[k], *(after if i == 0 else ()), signal=i == len(ks) - 1)
        return t

    def project_rows(self, u, cn, x, tb, bank, after):
        for k in range(KC):
            t = self.product3(bank[:, 0:cn], x.hi[:, k, tb * P:(tb + 1) * P], x.lo[:, k, tb * P:(tb + 1) * P],
                              u.hi[:, k, 0:cn], u.lo[:, k, 0:cn], k == 0, k == KC - 1,
                              *u.ready, *x.ready[k], *(after if k == 0 else ()), signal=k == KC - 1)
        return t

    def ada_step(self):
        if self.ada_next >= 2 * MODS * 4:
            return
        i = self.ada_next
        self.ada_next += 1
        layer, c = divmod(i, MODS * 4)
        u = self.w.take(self.io["ada_w"][layer], 0, KC, c * 256, 256, split=False)
        b, bank, free = self.banks.take()
        for j in range(2):
            for k in range(KC):
                t = self.mm(bank[:, 2 * j:2 * j + 2], u.raw[:, k, j * P:(j + 1) * P], self.h["cs"][:, k, :],
                            k == 0, k == KC - 1, *u.ready, self.cs_ready, *free, signal=k == KC - 1)
        at = layer * MODS * KC + 2 * c
        bias = self.small("ada_b", at, at + 2).rearrange("p (j o) -> p j o", o=1).broadcast_to([P, 2, 2])
        e = self.tt(self.h["mod"][:, at:at + 2, :], bank[:, 0:4].rearrange("p (j c) -> p j c", j=2), bias,
                    ALU.add, t, self.small_ready)
        self.mod_ready[i] = e
        self.banks.free(b, e)
        self.w.done(u, t)

    def ada_until(self, layer, part):
        last = (layer * MODS + part + 1) * 4
        while self.ada_next < last:
            self.ada_step()
        return self.mod_ready[last - 1]

    def mod(self, layer, part):
        at = (layer * MODS + part) * KC
        return self.h["mod"][:, at:at + KC, :]

    def square_sum(self, k, src, n, *after):
        h = self.h
        if k == 0:
            self.sum_tok = self.act(h["acc"][:, 0:n], src, ACT.Square, *after, *self.acc_free)
            return
        s = k % 2
        t = self.act(h["sq"][:, s, 0:n], src, ACT.Square, *after, *self.sq_free[s])
        self.sum_tok = self.tt(h["acc"][:, 0:n], h["acc"][:, 0:n], h["sq"][:, s, 0:n], ALU.add, t, self.sum_tok,
                               eng=self.pool)
        self.sq_free[s] = (self.sum_tok,)

    def columns_to_rows(self, stat_bank, stat_ready, ncol, width, eps, banks_out):
        h = self.h
        t = self.act(h["rs"][:, 0:ncol], stat_bank[:, 0:ncol], ACT.Sqrt, stat_ready, *self.rs_free,
                     scale=1.0 / width, bias=h["eps"][:, 0:1] if eps == EPS_RMS else h["eps"][:, 1:2])
        stat_read = t
        t = self.recip(h["rs2"][:, 0:ncol], h["rs"][:, 0:ncol], t, *self.rs_free)
        out = []
        for c in range(ncol):
            s = c % 4
            d = self.ts(h["diag"][:, s, :], h["ident"][:, :], h["rs2"][:, c:c + 1], None, ALU.mult, None, t,
                        *self.diag_free[s])
            bank, at, free = banks_out[c]
            m = self.mm(bank[:, at:at + P], h["ones"][:, :], h["diag"][:, s, :], True, True, d, *free, signal=True)
            self.diag_free[s] = (m,)
            out.append(m)
        self.rs_free = (d,)
        return stat_read, out

    def rms_rows(self, n, width, eps, sum_tok):
        h = self.h
        sb, stat, sfree = self.banks.take()
        for tb in range(n // P):
            t = self.mm(stat[:, tb:tb + 1], h["acc"][:, tb * P:(tb + 1) * P], h["ones"][:, 0:1], True, True,
                        sum_tok, *sfree, signal=True)
        self.acc_free = (t,)
        rb, rows, rfree = self.banks.take()
        read, toks = self.columns_to_rows(stat, t, n // P, width, eps, [(rows, tb * P, rfree) for tb in range(n // P)])
        self.banks.free(sb, read)
        return rb, rows, toks[-1]

    def prenorm(self, hT, n, layer, gain, shift_part, hT_ready, sum_tok):
        h = self.h
        mt = self.ada_until(layer, shift_part + 1)
        g = self.small(gain, layer * KC, (layer + 1) * KC).rearrange("p (k o) -> p k o", o=1).broadcast_to([P, KC, 2])
        a = self.stt(h["coef"][:, :, :], self.mod(layer, shift_part + 1), 1.0, g, ALU.add, ALU.mult, mt, self.small_ready,
                     *self.coef_free)
        rb, rows, rt = self.rms_rows(n, D, EPS_RMS, sum_tok)
        x = self.x
        x.ready = []
        for k in range(KC):
            ready = []
            s = k % 2
            for c in range(n // T):
                cs = slice(c * T, (c + 1) * T)
                t = self.stt(h["tmp"][:, s, cs], hT[:, k, cs], h["coef"][:, k, c:c + 1], rows[:, cs], ALU.mult, ALU.mult,
                             a, rt, *hT_ready, *self.tmp_free[s])
                shift = self.mod(layer, shift_part)[:, k, c:c + 1]
                e = self.act(x.hi[:, k, cs], h["tmp"][:, s, cs], ACT.Identity, t, mt, *self.x_free, bias=shift)
                f = self.stt(x.lo[:, k, cs], h["tmp"][:, s, cs], shift, x.hi[:, k, cs].bitcast(F32), ALU.add, ALU.subtract,
                             e, t, *self.x_free)
                ready += [e, f]
            self.tmp_free[s] = tuple(ready)
            x.ready.append(ready)
        self.banks.free(rb, f)
        self.coef_free = (f,)
        return x

    def split_into(self, hi, lo, src, *after, free=()):
        a = self.act(hi, src, ACT.Copy, *after, *free)
        b = self.tt(lo, src, hi.bitcast(F32), ALU.subtract, a, *after, *free)
        return [a, b]

    def ffn(self, w_in, w_out, x, n, update, between=lambda: None, before_down=lambda half: None):
        h = self.h
        hid_hi = self.place("hid_hi", MID, [P, 12, 2 * T], F32R)
        hid_lo = self.place("hid_lo", MID + 24576, [P, 12, 2 * T], F32R)
        hid_free = ()
        for half, (j0, jn) in enumerate(HALVES):
            ready = []
            for j in range(j0, j0 + jn, 2):
                ug = self.w.take(w_in, 0, KC, j * P, 256)
                gates = []
                for q in range(2):
                    b, bank, free = self.banks.take()
                    t = self.project(ug, q * P, x, n, bank, free)
                    s = q
                    e = self.act(h["sg"][:, s, 0:n], bank[:, 0:n], ACT.Silu, t, *self.sg_free[s])
                    self.banks.free(b, e)
                    gates.append(e)
                self.w.done(ug, t)
                uu = self.w.take(w_in, 0, KC, FFN + j * P, 256)
                for q in range(2):
                    b, bank, free = self.banks.take()
                    t = self.project(uu, q * P, x, n, bank, free)
                    d = self.tt(h["tmp"][:, q, 0:n], bank[:, 0:n], h["sg"][:, q, 0:n], ALU.mult, t, gates[q],
                                *self.tmp_free[q])
                    self.banks.free(b, d)
                    self.sg_free[q] = (d,)
                    r = self.split_into(hid_hi[:, j - j0 + q, 0:n], hid_lo[:, j - j0 + q, 0:n], h["tmp"][:, q, 0:n],
                                        d, free=hid_free)
                    self.tmp_free[q] = tuple(r)
                    ready.append(r)
                self.w.done(uu, t)
                between()
            if half == 1:
                self.x_free = (t,)
            before_down(half)
            hid = Unit()
            hid.hi, hid.lo, hid.ready = hid_hi, hid_lo, ready
            hk = jn // 2
            for c in range(KC // 2):
                pair = [self.banks.take() for _ in range(2)]
                for part in range(2):
                    u = self.w.take(w_out, j0 + part * hk, hk, c * 256, 256)
                    ends = []
                    for q in range(2):
                        t = self.project(u, q * P, hid, n, pair[q][1], pair[q][2],
                                         ks=range(part * hk, part * hk + hk), k0=part * hk, start=part == 0, stop=part == 1)
                        ends.append(t)
                    self.w.done(u, t)
                for q in range(2):
                    d = update(2 * c + q, pair[q][1], ends[q], half)
                    self.banks.free(pair[q][0], d)
                between()
            hid_free = (t,)

    def gated_update(self, layer, part, factor, n, last_half=1):
        h = self.h
        hT = h["hT"]

        def gate():
            mt = self.ada_until(layer, part)
            self.gate_ready = self.ts(h["gate"][:, :, :], self.mod(layer, part), factor, None, ALU.mult, None, mt,
                                      *self.gate_free)

        def update(k, bank, ready, half):
            ends = []
            for c in range(n // T):
                cs = slice(c * T, (c + 1) * T)
                ends.append(self.stt(hT[:, k, cs], bank[:, cs], h["gate"][:, k, c:c + 1], hT[:, k, cs], ALU.mult, ALU.add,
                                     ready, self.gate_ready, *self.h_ready))
            self.gate_free = (ends[-1],)
            self.h_tok[k] = ends[-1]
            if half == last_half:
                self.square_sum(k, hT[:, k, 0:n], n, *ends)
            return ends[-1]

        return gate, update

    def mix_out(self, w_out, x, n, update, kn=KC):
        for c in range(KC // 2):
            pair = [self.banks.take() for _ in range(2)]
            for k0 in range(0, kn, KC):
                u = self.w.take(w_out, k0, KC, c * 256, 256)
                ends = []
                for q in range(2):
                    t = self.project(u, q * P, x, n, pair[q][1], pair[q][2], ks=range(k0, k0 + KC), k0=k0,
                                     start=k0 == 0, stop=k0 + KC == kn)
                    ends.append(t)
                self.w.done(u, t)
            for q in range(2):
                d = update(2 * c + q, pair[q][1], ends[q], 1)
                self.banks.free(pair[q][0], d)
            self.ada_step()
        self.x_free = (t,)

    def evac(self, dst, bank, t, eng="act", func=ACT.Copy, scale=1.0, *after):
        if eng == "act":
            return self.act(dst, bank, func, t, *after, scale=scale)
        return self.copy(dst, bank, t, *after)

    def even_mixer(self, x):
        h, io, n = self.h, self.io, 2 * T
        w = io["even_w_in"]
        q = self.place("gla_q", MID, [P, 3, n])
        k = self.place("gla_k", MID + 6144, [P, 3, n])
        v = self.place("gla_v", MID + 12288, [P, 4, 768])
        r = self.place("gla_r", MID + 24576, [P, 6, n])
        zf = self.place("gla_zf", MID + 36864, [P, 4, 256])
        zg = self.place("gla_zg", MID + 40960, [P, n])
        gw = self.place("gla_gw", MID + 43008, [P, 2, 384])
        fy = self.place("four_y", MID + 46080, [P, 2, n])
        bar = self.barrier()
        z = self.pool.do(lambda e: e.memset(gw[96:128, :, :], 0.0), *bar)
        gwt = [self.load(gw[96 + 16 * d:112 + 16 * d, d, :], io["gate_w"][d], z, *bar) for d in range(2)]

        qk = []
        for c in range(3):
            u = self.w.take(w, 0, KC, 256 + 256 * c, 256)
            for j in range(2):
                m = 2 * c + j
                b, bank, free = self.banks.take()
                t = self.project(u, j * P, x, n, bank, free)
                dst = q[:, m, :] if m < 3 else k[:, m - 3, :]
                e = self.act(dst, bank[:, :], ACT.Copy, t, scale=GLA_DK ** -0.5 if m < 3 else 1.0)
                self.banks.free(b, e)
                qk.append(e)
            self.w.done(u, t)
            self.ada_step()
        u = self.w.take(w, 0, KC, 2592 - P, P)
        b, bank, free = self.banks.take()
        t = self.project(u, 0, x, n, bank, free)
        self.w.done(u, t)
        zgt = self.act(zg[96:128, :], bank[96:128, :], ACT.Copy, t)
        self.banks.free(b, zgt)

        def rows(c0, dst, c):
            u = self.w.take(w, 0, KC, c0, 256)
            ends = []
            for tb in range(4):
                b, bank, free = self.banks.take()
                t = self.project_rows(u, 256, x, tb, bank, free)
                e = self.copy(dst[:, tb, c:c + 256], bank[:, 0:256], t)
                self.banks.free(b, e)
                ends.append(e)
            self.w.done(u, t)
            self.ada_step()
            return ends
        zft = rows(0, zf, 0)
        vt = [e for c in range(3) for e in rows(1024 + 256 * c, v, 256 * c)]
        rt = []
        for c in range(3):
            u = self.w.take(w, 0, KC, 1792 + 256 * c, 256)
            for j in range(2):
                b, bank, free = self.banks.take()
                t = self.project(u, j * P, x, n, bank, free)
                e = self.act(r[:, 2 * c + j, :], bank[:, :], ACT.Silu, t)
                self.banks.free(b, e)
                rt.append(e)
            self.w.done(u, t)
            self.ada_step()
        bar = self.barrier()

        ft = self.place("four_t", XN, [P, 2, 512])
        fd = self.place("four_d", XN + 8192, [P, 2, 128])
        seg = self.place("seg", XN + 9216, [P, n])
        lim = self.place("lim", XN + 11264, [P, 4, 1, P])
        fa = self.place("four_a", XN + 4096, [P, 2, 512])
        cft = self.load(ft[:, :, :], io["fourier_time"], *bar)
        cfd = self.load(fd[:, :, :], io["fourier_dim"], *bar)
        cseg = self.load(seg[:, :], io["segments"], *bar)
        clim = self.load(lim[:, :, :, :], io["limits"], *bar)

        yt = []
        for c in range(2):
            for part in range(2):
                b, bank, free = self.banks.take()
                for tb in range(2):
                    t = self.mm(bank[:, :], zf[:, 2 * part + tb, c * P:(c + 1) * P], ft[:, tb, :], tb == 0, tb == 1,
                                cft, *free, *zft, signal=True)
                s = (2 * c + part) % 2
                e = self.copy(fa[:, s, :], bank[:, :], t, *(yt[-2:-1]))
                self.banks.free(b, e)
                b, bank, free = self.banks.take()
                self.mm(bank[:, 0:T], fd[:, 0, :], fa[:, s, 0:T], True, False, e, cfd, *free)
                t = self.mm(bank[:, 0:T], fd[:, 1, :], fa[:, s, T:2 * T], False, True, signal=True)
                e = self.act(fy[:, c, part * T:(part + 1) * T], bank[:, 0:T], ACT.Copy, t)
                self.banks.free(b, e)
                yt.append(e)

        spots = [(XN + 13312, 32768 - 13312), (MID + 50176, TEMPS + 10240 - MID - 50176)]
        regions = [list(s) for s in spots]

        def room(n_bytes):
            for reg in regions:
                if reg[1] >= n_bytes:
                    a = reg[0]
                    reg[0] += n_bytes
                    reg[1] -= n_bytes
                    return a
            raise ValueError("work region is full")
        dirs = []
        for d in range(2):
            o = Unit()
            o.ls = self.place(f"gla_ls{d}", room(2048), [P, n])
            o.l = self.place(f"gla_l{d}", room(2048), [P, n])
            o.b = self.place(f"gla_b{d}", room(2048), [P, n])
            o.qd = self.place(f"gla_qd{d}", room(2048), [P, n])
            o.kd = self.place(f"gla_kd{d}", room(2048), [P, n])
            o.ks = self.place(f"gla_ks{d}", room(2048), [P, n])
            o.ksn = self.place(f"gla_ksn{d}", room(2048), [P, 4, P])
            o.st = self.place(f"gla_st{d}", room(3584), [P, 7, P])
            o.dec = self.place(f"gla_dec{d}", room(32), [P, 8])
            o.order = [4, 5, 6, 7, 0, 1, 2, 3] if d == 0 else [7, 6, 5, 4, 3, 2, 1, 0]
            dirs.append(o)
        att = self.place("gla_att", XN, [P, 4, 4, P])
        sbank_b, sbank, sfree = self.banks.take()
        sumsq = []
        prev_pe = ()
        o_read = {}
        att_free = [(), (), (), ()]
        yo = {}
        for m in range(3):
            for d, o in enumerate(dirs):
                b, bank, free = self.banks.take()
                t = self.mm(bank[:, :], gw[96:128, d, m * P:(m + 1) * P], zg[96:128, :], True, True, zgt, *gwt, *free,
                            signal=True)
                gb = self.small("gate_b", d * 3 + m, d * 3 + m + 1)
                t1 = self.ts(o.ls[:, :], bank[:, :], gb, None, ALU.add, None, t, *prev_pe)
                self.banks.free(b, t1)
                t2 = self.stt(o.l[:, :], o.ls[:, :], -1.0, o.ls[:, :], ALU.mult, ALU.min, t1)
                t3 = self.act(o.l[:, :], o.l[:, :], ACT.Exp, t2)
                t4 = self.act(o.l[:, :], o.l[:, :], ACT.Ln, t3, bias=h["one"][:, 0:1])
                t5 = self.stt(o.ls[:, :], o.ls[:, :], 0.0, o.l[:, :], ALU.min, ALU.subtract, t4, t1)
                if d == 0:
                    out, a0, a1 = o.b[:, :], seg[:, :], o.ls[:, :]
                else:
                    out, a0, a1 = o.b[:, ::-1], seg[:, :], o.ls[:, ::-1]
                t6 = self.dve.do(lambda e, out=out, a0=a0, a1=a1: e.tensor_tensor_scan(out, a0, a1, 0.0, ALU.mult, ALU.add),
                                 t5, cseg, *prev_pe)
                ends = o.b[:, :].rearrange("p (c i) -> p c i", i=GLA_CHUNK)[:, :, 63:64] if d == 0 else \
                    o.b[:, :].rearrange("p (c i) -> p c i", i=GLA_CHUNK)[:, :, 0:1]
                inv = 1.0 / GLA_TAU
                o.dec_t = self.act(o.dec[:, :], ends, ACT.Exp, t6, *prev_pe, scale=inv)
                e1 = self.act(o.qd[:, :], o.b[:, :], ACT.Exp, t6, *prev_pe, scale=inv)
                e2 = self.act(o.kd[:, :], o.b[:, :], ACT.Exp, t6, *prev_pe, scale=-inv)
                d1 = self.tt(o.l[:, :].rearrange("p (c i) -> p c i", i=GLA_CHUNK), ends.broadcast_to([P, NCH, GLA_CHUNK]),
                             o.b[:, :].rearrange("p (c i) -> p c i", i=GLA_CHUNK), ALU.subtract, t6, t5)
                e3 = self.act(o.ks[:, :], o.l[:, :], ACT.Exp, d1, *prev_pe, scale=inv)
                o.qd_t = self.tt(o.qd[:, :], o.qd[:, :], q[:, m, :], ALU.mult, e1, *qk)
                o.kd_t = self.tt(o.kd[:, :], o.kd[:, :], k[:, m, :], ALU.mult, e2, *qk)
                o.ks_t = self.tt(o.ks[:, :], o.ks[:, :], k[:, m, :], ALU.mult, e3, *qk)
                b, bank, free = self.banks.take()
                for tb in range(4):
                    t = self.transpose(bank[:, tb * P:(tb + 1) * P], o.ks[:, tb * P:(tb + 1) * P], o.ks_t, *free,
                                       signal=tb == 3)
                kst = self.act(o.ksn[:, :, :], bank[:, :].rearrange("p (a b) -> p a b", a=4), ACT.Copy, t, *prev_pe)
                self.banks.free(b, kst)
                ub = [self.banks.take() for _ in range(2)]
                for c in o.order[:7]:
                    pr, tb = 64 * (c % 2), c // 2
                    for hl in range(2):
                        t = self.mm(ub[c % 2][1][64 * hl:64 * hl + 64, tb * P:(tb + 1) * P],
                                    o.ksn[pr:pr + 64, tb, 64 * hl:64 * hl + 64],
                                    v[pr:pr + 64, tb, (2 * m + hl) * P:(2 * m + hl + 1) * P], True, True,
                                    kst, *vt, *ub[c % 2][2], signal=True)
                st = None
                for s, c in enumerate(o.order[:7]):
                    up = ub[c % 2][1][:, (c // 2) * P:(c // 2 + 1) * P]
                    if s == 0:
                        st = self.copy(o.st[:, 0, :], up, t, *prev_pe)
                    else:
                        st = self.stt(o.st[:, s, :], o.st[:, s - 1, :], o.dec[:, c:c + 1], up, ALU.mult, ALU.add, st, t, o.dec_t)
                o.st_t = st
                for bb in ub:
                    self.banks.free(bb[0], st)
            for d, o in enumerate(dirs):
                for hl in range(2):
                    b, bank, free = self.banks.take()
                    hs = slice(64 * hl, 64 * hl + 64)
                    for tb in range(4):
                        t = self.mm(bank[:, tb * P:(tb + 1) * P], o.kd[hs, tb * P:(tb + 1) * P],
                                    o.qd[hs, tb * P:(tb + 1) * P], True, True, o.kd_t, o.qd_t, *free, signal=tb == 3)
                    i = 2 * d + hl
                    a = att[:, i, :, :]
                    t1 = self.tt(a, bank[:, :].rearrange("p (a b) -> p a b", a=4), lim[:, 2 * d, :, :].broadcast_to([P, 4, P]),
                                 ALU.min, t, clim, *att_free[i])
                    self.banks.free(b, t1)
                    o_read[i] = self.tt(a, a, lim[:, 2 * d + 1, :, :].broadcast_to([P, 4, P]), ALU.max, t1)
            for hl in range(2):
                hd = 2 * m + hl
                hs = slice(64 * hl, 64 * hl + 64)
                b, bank, free = self.banks.take()
                first = True
                for d, o in enumerate(dirs):
                    for tb in range(4):
                        self.mm(bank[:, tb * P:(tb + 1) * P], v[:, tb, hd * P:(hd + 1) * P], att[:, 2 * d + hl, tb, :],
                                first, False, o_read[2 * d + hl], *free, loose=True)
                        first = False
                for d, o in enumerate(dirs):
                    for s, c in enumerate(o.order[1:]):
                        t = self.mm(bank[:, c * 64:(c + 1) * 64], o.st[hs, s, :], o.qd[hs, c * 64:(c + 1) * 64], False,
                                    d == 1 and s == 6, o.st_t, o.qd_t, loose=True, signal=d == 1 and s == 6)
                y1 = self.tt(r[:, hd, :], r[:, hd, :], bank[:, :], ALU.mult, t, *rt)
                sq = h["sq2"]
                y2 = self.act(sq[:, hl, :], bank[:, :], ACT.Square, t, y1, *self.sq2_free[hl])
                self.banks.free(b, y2)
                for tb in range(4):
                    t = self.mm(sbank[:, hd * 4 + tb:hd * 4 + tb + 1], sq[:, hl, tb * P:(tb + 1) * P], h["ones"][:, 0:1],
                                True, True, y2, *sfree, signal=True)
                self.sq2_free[hl] = (t,)
                yo[hd] = y1
            att_free = [(t,)] * 4
            prev_pe = (t,)
        bar = self.barrier()
        xh, xl = self.x.hi, self.x.lo
        self.x.ready = [self.split_into(xh[:, c, :], xl[:, c, :], fy[:, c, :]) for c in range(2)]
        outs, taken = [], []
        for hd in range(6):
            b, bank, free = self.banks.take()
            taken.append((b, bank))
            outs += [(bank, tb * P, free) for tb in range(4)]
            if len(taken) == 6:
                break
        read, toks = self.columns_to_rows(sbank, t, 24, GLA_DV, EPS_RMS, outs)
        self.banks.free(sbank_b, read)
        for hd in range(6):
            y = self.stt(r[:, hd, :], r[:, hd, :], self.small("gla_norm"), taken[hd][1][:, :], ALU.mult, ALU.mult,
                         toks[4 * hd + 3])
            self.banks.free(taken[hd][0], y)
            self.x.ready.append(self.split_into(xh[:, 2 + hd, :], xl[:, 2 + hd, :], r[:, hd, :], y))
        return self.x

    def rope(self, dst, src, cos, sin, rot, n, *after):
        b, bank, free = self.banks.take()
        t = self.mm(bank[:, 0:n], rot, src, True, True, *after, *free, signal=True)
        s = self.rope_i % 2
        self.rope_i += 1
        h = self.h
        t1 = self.tt(h["rt"][:, s, 0:n], bank[:, 0:n], sin, ALU.mult, t, *self.rt_free[s])
        self.banks.free(b, t1)
        t2 = self.tt(dst, src, cos, ALU.mult, t, *after, eng=self.pool)
        t3 = self.tt(dst, dst, h["rt"][:, s, 0:n], ALU.add, t1, t2)
        self.rt_free[s] = (t3,)
        return t3

    def odd_mixer(self, x):
        h, io = self.h, self.io
        w = io["odd_w_in"]
        q = self.place("df_q", MID, [P, 6, T])
        k = self.place("df_k", MID + 6144, [P, 6, 2 * T])
        v = self.place("df_v", MID + 18432, [P, 4, 768])
        z3 = self.place("df_z", MID + 30720, [P, 3, 2, T])
        cs = self.place("df_cs", MID + 36864, [P, 2, T])
        rot = self.place("df_rot", MID + 38912, [P, P])
        raw = self.place("df_raw", MID + 39424, [P, 4, T])
        h["rt"] = self.place("df_rt", MID + 43520, [P, 2, T])
        self.rt_free = [(), ()]
        y = self.place("df_y", MID + 45568, [P, 8, T])
        bar = self.barrier()
        ccs = self.load(cs[:, :, :], io["axial"], *bar)
        crot = self.load(rot[:, :], io["axial_rot"], *bar)

        lam = self.small("lambdas")
        lv = h["lam"]
        t = self.tt(lv[0:64, 0:2], lam[0:64, 0:2], lam[0:64, 2:4], ALU.mult)
        b, bank, free = self.banks.take()
        t = self.mm(bank[:, 0:2], h["ones"][0:64, :], lv[0:64, 0:2], True, True, t, *free, signal=True)
        t = self.act(lv[:, 2:4], bank[:, 0:2], ACT.Exp, t)
        self.banks.free(b, t)
        t = self.tt(lv[:, 4:5], lv[:, 3:4], lv[:, 2:3], ALU.subtract, t)
        lam_t = self.ts(lv[:, 5:6], lv[:, 4:5], -LAM_INIT, None, ALU.add, None, t)

        zt = []
        for c in range(3):
            u = self.w.take(w, 0, KC, 256 * c, 256)
            for j in range(2):
                b, bank, free = self.banks.take()
                t = self.project(u, j * P, x, T, bank, free)
                e = self.act(z3[:, c, j, :], bank[:, 0:T], ACT.Copy, t)
                self.banks.free(b, e)
                zt.append(e)
            self.w.done(u, t)
            self.ada_step()
        qt, kt = [], []
        raw_free = [()] * 4
        i = 0
        for part, dst, toks in ((0, q, qt), (1, k, kt)):
            for c in range(3):
                u = self.w.take(w, 0, KC, 768 + 768 * part + 256 * c, 256)
                for j in range(2):
                    m = 2 * c + j
                    n = T * (1 + part)
                    b, bank, free = self.banks.take()
                    t = self.project(u, j * P, x, n, bank, free)
                    s = i % 4
                    i += 1
                    e = self.act(raw[:, s, :], bank[:, 0:T], ACT.Copy, t, *raw_free[s])
                    if part:
                        e2 = self.act(k[:, m, T:2 * T], bank[:, T:2 * T], ACT.Copy, t)
                        toks.append(e2)
                        self.banks.free(b, e2)
                    else:
                        self.banks.free(b, e)
                    e = self.rope(dst[:, m, 0:T], raw[:, s, :], cs[:, 0, :], cs[:, 1, :], rot[:, :], T, e, ccs, crot)
                    raw_free[s] = (e,)
                    toks.append(e)
                self.w.done(u, t)
                self.ada_step()
        vt = []
        for c in range(3):
            u = self.w.take(w, 0, KC, 2304 + 256 * c, 256)
            for tb in range(4):
                b, bank, free = self.banks.take()
                t = self.project_rows(u, 256, x, tb, bank, free)
                e = self.copy(v[:, tb, 256 * c:256 * c + 256], bank[:, 0:256], t)
                self.banks.free(b, e)
                vt.append(e)
            self.w.done(u, t)
            self.ada_step()

        conv_y = []
        for j in range(2):
            u_ = z3[:, 1, j, :]
            tap = [self.small("conv_w", 2 * a + j, 2 * a + j + 1) for a in range(3)]
            t = self.tt(u_, z3[:, 1, j, :], z3[:, 2, j, :], ALU.mult, *zt)
            t = self.ts(y[:, j, :], u_, tap[1], self.small("conv_b", j, j + 1), ALU.mult, ALU.add, t)
            t = self.stt(y[:, j, 1:T], u_[:, 0:T - 1], tap[0], y[:, j, 1:T], ALU.mult, ALU.add, t)
            t = self.stt(y[:, j, 0:T - 1], u_[:, 1:T], tap[2], y[:, j, 0:T - 1], ALU.mult, ALU.add, t)
            conv_y.append(self.tt(y[:, j, :], y[:, j, :], z3[:, 0, j, :], ALU.mult, t, *zt))
        bar = self.barrier()

        NS = 3
        e_ = self.place("df_e", XN, [P, NS, 2, 2 * T])
        aT = self.place("df_aT", XN + 12288, [P, NS, 4, P])
        sc = self.place("df_sc", XN + 12288 + 6144, [P, 12, 8])
        scale = HD ** -0.5
        sbank_b, sbank, sfree = self.banks.take()
        jobs = [(hd, qb) for hd in range(6) for qb in range(TB)]
        st = {}
        e_free = [()] * NS
        aT_free = [()] * NS
        obank = {}

        def scores(i):
            hd, qb = jobs[i]
            st[i] = []
            for s in range(2):
                b, bank, free = self.banks.take()
                t = self.mm(bank[:, :], q[64 * s:64 * s + 64, hd, qb * P:(qb + 1) * P], k[64 * s:64 * s + 64, hd, :],
                            True, True, *qt, *kt, *free, signal=True)
                c = sc[:, i, :]
                m = self.rmax(c[:, s:s + 1], bank[:, :], t)
                m = self.ts(c[:, 2 + s:3 + s], c[:, s:s + 1], scale, None, ALU.mult, None, m)
                e = self.act(e_[:, i % NS, s, :], bank[:, :], ACT.Exp, t, m, *e_free[i % NS], scale=scale,
                             bias=c[:, 2 + s:3 + s], accum=c[:, 4 + s:5 + s])
                self.banks.free(b, e)
                st[i].append(e)

        def combine(i):
            c = sc[:, i, :]
            a, e1 = e_[:, i % NS, 0, :], e_[:, i % NS, 1, :]
            t = self.recip(c[:, 6:8], c[:, 4:6], *st[i])
            t1 = self.tt(c[:, 7:8], c[:, 7:8], h["lam"][:, 5:6], ALU.mult, t, lam_t)
            t2 = self.ts(a, a, c[:, 6:7], None, ALU.mult, None, t, *st[i])
            t3 = self.stt(a, e1, c[:, 7:8], a, ALU.mult, ALU.add, t1, t2)
            st[i] = t3

        def turn(i):
            b, bank, free = self.banks.take()
            for kb in range(4):
                t = self.transpose(bank[:, kb * P:(kb + 1) * P], e_[:, i % NS, 0, kb * P:(kb + 1) * P], st[i], *free,
                                   signal=kb == 3)
            e_free[i % NS] = (t,)
            e = self.act(aT[:, i % NS, :, :], bank[:, :].rearrange("p (a b) -> p a b", a=4), ACT.Copy, t, *aT_free[i % NS])
            self.banks.free(b, e)
            st[i] = e

        def values(i):
            hd, qb = jobs[i]
            if qb == 0:
                obank[hd] = self.banks.take()
            b, bank, free = obank[hd]
            for kb in range(4):
                t = self.mm(bank[:, qb * P:(qb + 1) * P], v[:, kb, hd * P:(hd + 1) * P], aT[:, i % NS, kb, :], kb == 0,
                            kb == 3, st[i], *vt, *free, signal=kb == 3)
            aT_free[i % NS] = (t,)
            if qb == TB - 1:
                s = hd % 2
                y2 = self.act(h["sq2"][:, s, 0:T], bank[:, 0:T], ACT.Square, t, *self.sq2_free[s])
                y1 = self.copy(y[:, 2 + hd, :], bank[:, 0:T], t, y2)
                self.banks.free(b, y1)
                for tb in range(TB):
                    t = self.mm(sbank[:, hd * TB + tb:hd * TB + tb + 1], h["sq2"][:, s, tb * P:(tb + 1) * P],
                                h["ones"][:, 0:1], True, True, y2, *sfree, signal=True)
                self.sq2_free[s] = (t,)
                self.stat_t = t

        nj = len(jobs)
        for i in range(nj + 2):
            if i < nj:
                scores(i)
            if 0 <= i - 2 < nj:
                values(i - 2)
            if 0 <= i - 1 < nj:
                combine(i - 1)
                turn(i - 1)
        bar = self.barrier()
        xh, xl = self.x.hi, self.x.lo
        self.x.ready = [self.split_into(xh[:, c, 0:T], xl[:, c, 0:T], y[:, c, :]) for c in range(2)]
        outs, taken = [], []
        for hd in range(3):
            b, bank, free = self.banks.take()
            taken.append((b, bank))
            outs += [(bank, tb * P, free) for tb in range(4)]
        read, toks = self.columns_to_rows(sbank, self.stat_t, 12, DIFF_HEADS and 2 * HD, EPS_RMS, outs)
        self.banks.free(sbank_b, read)
        g = self.ts(h["lam"][:, 6:7], self.small("diff_norm"), 1.0 - LAM_INIT, None, ALU.mult, None)
        for hd in range(6):
            rows = taken[hd // 2][1][:, (hd % 2) * T:(hd % 2 + 1) * T]
            t = self.stt(y[:, 2 + hd, :], y[:, 2 + hd, :], h["lam"][:, 6:7], rows, ALU.mult, ALU.mult, g, toks[4 * (hd // 2) + 3])
            if hd % 2:
                self.banks.free(taken[hd // 2][0], t)
            self.x.ready.append(self.split_into(xh[:, 2 + hd, 0:T], xl[:, 2 + hd, 0:T], y[:, 2 + hd, :], t))
        return self.x

    def residual_update(self, first):
        hT = self.h["hT"]

        def update(k, bank, ready, half):
            if half == first:
                t = self.stt(hT[:, k, 0:T], hT[:, k, 0:T], ALPHA, bank[:, 0:T], ALU.mult, ALU.add, ready, *self.h_ready)
            else:
                t = self.tt(hT[:, k, 0:T], hT[:, k, 0:T], bank[:, 0:T], ALU.add, ready, self.h_tok[k])
            self.h_tok[k] = t
            if half == 1:
                acc = self.h["acc"]
                if k == 0:
                    self.sum_tok = self.pool.do(lambda e: e.tensor_copy(acc[:, 0:T], hT[:, 0, 0:T]), t, *self.acc_free)
                else:
                    self.sum_tok = self.tt(acc[:, 0:T], acc[:, 0:T], hT[:, k, 0:T], ALU.add, t, self.sum_tok, eng=self.pool)
            return t
        return update

    def layer_norm(self, which, split=True):
        h, hT = self.h, self.h["hT"]
        b, bank, free = self.banks.take()
        mt = self.mm(bank[:, 0:T], h["mean"][:, :], h["acc"][:, 0:T], True, True, self.sum_tok, *free, signal=True)
        self.acc_free = (mt,)
        d = []
        for k in range(KC):
            t = self.tt(hT[:, k, 0:T], hT[:, k, 0:T], bank[:, 0:T], ALU.subtract, mt, self.h_tok[k])
            self.square_sum(k, hT[:, k, 0:T], T, t)
            d.append(t)
        self.banks.free(b, t)
        rb, rows, rt = self.rms_rows(T, D, EPS_LN, self.sum_tok)
        x = self.x
        x.ready = []
        ready_h = []
        for k in range(KC):
            g = self.small("ln_gain", which * KC + k, which * KC + k + 1)
            bb = self.small("ln_bias", which * KC + k, which * KC + k + 1)
            s = k % 2
            t = self.stt(h["tmp"][:, s, 0:T], hT[:, k, 0:T], g, rows[:, 0:T], ALU.mult, ALU.mult, rt, d[k], *self.tmp_free[s])
            o = self.ts(hT[:, k, 0:T], h["tmp"][:, s, 0:T], bb, None, ALU.add, None, t, eng=self.pool)
            ready_h.append(o)
            if split:
                e = self.act(x.hi[:, k, 0:T], h["tmp"][:, s, 0:T], ACT.Identity, t, *self.x_free, bias=bb)
                f = self.stt(x.lo[:, k, 0:T], h["tmp"][:, s, 0:T], bb, x.hi[:, k, 0:T].bitcast(F32), ALU.add, ALU.subtract,
                             e, t, *self.x_free)
                self.tmp_free[s] = (o, e, f)
                x.ready.append([e, f])
            else:
                self.tmp_free[s] = (o,)
        self.banks.free(rb, t)
        self.h_ready = tuple(ready_h)
        return x

    def retention(self, x):
        h, io = self.h, self.io
        w = io["ret_w_in"]
        q = self.place("rt_q", MID, [P, 8, T])
        k = self.place("rt_k", MID + 8192, [P, 8, T])
        v = self.place("rt_v", MID + 16384, [P, TB, 2048])
        gate = self.place("rt_g", MID + 32768, [P, 16, T])
        cs = self.place("rt_cs", MID + 49152, [P, 2, 2, T])
        raw = self.place("rt_raw", MID + 53248, [P, 2, T])
        rot = self.place("rt_rot", MID + 55296, [P, P])
        h["rt"] = self.place("rt_rt", MID + 57184, [P, 2, T])
        self.rt_free = [(), ()]
        bar = self.barrier()
        ccs = self.load(cs[:, :, :, :], io["ret_rope"], *bar)
        crot = self.load(rot[:, :], io["pair_rot"], *bar)
        qk = []
        raw_free = [(), ()]
        for c in range(8):
            u = self.w.take(w, 0, KC, 256 * c, 256)
            for j in range(2):
                m = 2 * c + j
                b, bank, free = self.banks.take()
                t = self.project(u, j * P, x, T, bank, free)
                e = self.act(raw[:, j, :], bank[:, 0:T], ACT.Copy, t, *raw_free[j])
                self.banks.free(b, e)
                dst = q[:, m, :] if m < 8 else k[:, m - 8, :]
                e = self.rope(dst, raw[:, j, :], cs[:, 0, m % 2, :], cs[:, 1, m % 2, :], rot[:, :], T, e, ccs, crot)
                raw_free[j] = (e,)
                qk.append(e)
            self.w.done(u, t)
        vt = []
        for c in range(8):
            u = self.w.take(w, 0, KC, 2048 + 256 * c, 256)
            for tb in range(TB):
                b, bank, free = self.banks.take()
                t = self.project_rows(u, 256, x, tb, bank, free)
                e = self.copy(v[:, tb, 256 * c:256 * c + 256], bank[:, 0:256], t)
                self.banks.free(b, e)
                vt.append(e)
            self.w.done(u, t)
        gt = []
        for c in range(8):
            u = self.w.take(w, 0, KC, 4096 + 256 * c, 256)
            for j in range(2):
                b, bank, free = self.banks.take()
                t = self.project(u, j * P, x, T, bank, free)
                e = self.act(gate[:, 2 * c + j, :], bank[:, 0:T], ACT.Silu, t)
                self.banks.free(b, e)
                gt.append(e)
            self.w.done(u, t)
        bar = self.barrier()
        dec = self.place("rt_dec", XN, [P, 4, 384])
        S = self.place("rt_S", XN + 6144, [P, 2, 384])
        yb = self.place("rt_y", XN + 9216, [P, 2, 4, T])
        sqr = self.place("rt_sq", XN + 17408, [P, 4, T])
        cdec = self.load(dec[:, :, :], io["decay"], *bar)
        s_free = [(), ()]
        y_free = [(), ()]
        sq_free = ()
        for hd in range(RET_HEADS):
            s = hd % 2
            b, bank, free = self.banks.take()
            for jb, (i0, i1, at) in enumerate(((0, T, 0), (P, T, T))):
                for c in range(2):
                    t = self.mm(bank[:, at:at + i1 - i0], k[:, 2 * hd + c, jb * P:(jb + 1) * P], q[:, 2 * hd + c, i0:i1],
                                c == 0, c == 1, *qk, *free, signal=c == 1)
            st = self.tt(S[:, s, :], bank[:, 0:384], dec[:, hd, :], ALU.mult, t, cdec, *s_free[s])
            self.banks.free(b, st)
            ys = []
            for c in range(4):
                e0 = hd * RET_DV + c * P
                b, bank, free = self.banks.take()
                self.mm(bank[:, 0:T], v[:, 0, e0:e0 + P], S[:, s, 0:T], True, False, st, *vt, *free, loose=True)
                t = self.mm(bank[:, P:T], v[:, 1, e0:e0 + P], S[:, s, T:384], False, True, loose=True, signal=True)
                e = self.act(yb[:, s, c, :], bank[:, 0:T], ACT.Copy, t, *y_free[s])
                self.banks.free(b, e)
                ys.append(e)
            s_free[s] = (t,)
            mb, mbank, mfree = self.banks.take()
            for c in range(4):
                t = self.mm(mbank[:, 0:T], h["ones"][:, :], yb[:, s, c, :], c == 0, c == 3, ys[c], *mfree, signal=c == 3)
            mu = self.act(h["tmp"][:, 0, 0:T], mbank[:, 0:T], ACT.Copy, t, *self.tmp_free[0], scale=1.0 / RET_DV)
            self.banks.free(mb, mu)
            sb_, sbank, sfree = self.banks.take()
            ds = []
            for c in range(4):
                d = self.tt(yb[:, s, c, :], yb[:, s, c, :], h["tmp"][:, 0, 0:T], ALU.subtract, mu, ys[c], t)
                e = self.act(sqr[:, c, :], yb[:, s, c, :], ACT.Square, d, *sq_free)
                ds.append((d, e))
            self.tmp_free[0] = (d,)
            for tb in range(TB):
                for c in range(4):
                    t = self.mm(sbank[:, tb:tb + 1], sqr[:, c, tb * P:(tb + 1) * P], h["ones"][:, 0:1], c == 0, c == 3,
                                ds[c][1], *sfree, signal=c == 3)
            sq_free = (t,)
            rb, rows, rfree = self.banks.take()
            read, toks = self.columns_to_rows(sbank, t, TB, RET_DV, EPS_LN, [(rows, tb * P, rfree) for tb in range(TB)])
            self.banks.free(sb_, read)
            for c in range(4):
                y = self.tt(yb[:, s, c, :], yb[:, s, c, :], rows[:, 0:T], ALU.mult, toks[-1], ds[c][0], ds[c][1])
                f = self.tt(gate[:, hd * 4 + c, :], gate[:, hd * 4 + c, :], yb[:, s, c, :], ALU.mult, y, *gt, eng=self.pool)
            y_free[s] = (f,)
            self.banks.free(rb, y)
        bar = self.barrier()
        r = Unit()
        r.hi = self.place("rt_hi", MID, [P, 16, T], F32R)
        r.lo = self.place("rt_lo", MID + 16384, [P, 16, T], F32R)
        r.ready = [self.split_into(r.hi[:, c, :], r.lo[:, c, :], gate[:, c, :]) for c in range(16)]
        return r

    def dilated(self, x):
        h, io = self.h, self.io
        w = io["attn_w_in"]
        NQ = ATT_GROUPS * 8
        q = self.place("at_q", MID, [P, NQ, T])
        k = self.place("at_k", MID + 24576, [P, NQ, T])
        v = self.place("at_v", MID + 49152, [P, TB, 3072])
        bar = self.barrier()
        qt = []
        for part, dst in ((0, q), (1, k)):
            for c in range(12):
                u = self.w.take(w, 0, KC, 3072 * part + 256 * c, 256)
                for j in range(2):
                    b, bank, free = self.banks.take()
                    t = self.project(u, j * P, x, T, bank, free)
                    e = self.act(dst[:, 2 * c + j, :], bank[:, 0:T], ACT.Copy, t)
                    self.banks.free(b, e)
                    qt.append(e)
                self.w.done(u, t)
        vt = []
        for c in range(12):
            u = self.w.take(w, 0, KC, 6144 + 256 * c, 256)
            for tb in range(TB):
                b, bank, free = self.banks.take()
                t = self.project_rows(u, 256, x, tb, bank, free)
                e = self.copy(v[:, tb, 256 * c:256 * c + 256], bank[:, 0:256], t)
                self.banks.free(b, e)
                vt.append(e)
            self.w.done(u, t)
        bar = self.barrier()
        NB = 2
        bias = self.place("at_bias", XN, [P, NB, 3, T])
        e_ = self.place("at_e", XN + 6144, [P, 2, 3 * T + 3 * P])
        pT = self.place("at_pT", XN + 15360, [P, 9, P])
        o = self.place("at_o", XN + 19968, [P, TB, D])
        sc = self.place("at_sc", XN + 28160, [P, 16, 8])
        wide = self.place("at_wide", XN + 28672, [16, 2, 384])

        oh = self.place("at_onehot", XN, [32, 3, 384])
        mk = self.place("at_mask", XN + 6144, [16, 3, 384])
        coh = self.load(oh[:, :, :], io["onehot"], *bar)
        cmk = self.load(mk[:, :, :], io["dist_mask"], *bar)
        rel = self.small("rel_bias")
        toks = []
        stored = []
        for g in range(3):
            b, bank, free = self.banks.take()
            t = self.mm(bank[0:16, 0:384], rel[0:32, 16 * g:16 * g + 16], oh[:, g, :], True, True, coh, *free, signal=True)
            t = self.tt(wide[:, g % 2, :], bank[0:16, 0:384], mk[:, g, :], ALU.add, t, cmk, *(stored[g - 2:g - 1] if g >= 2 else ()))
            self.banks.free(b, t)
            stored.append(self.load(io["bias_rows"][g], wide[:, g % 2, :], t))
        nbar = self.barrier()
        bias_t = {}
        bias_free = [list(nbar)] * NB

        def fetch(hd):
            s = hd % NB
            src = self.io["bias_windows"](hd)
            bias_t[hd] = self.load(bias[:, s, :, :], src, *stored, *bias_free[s])

        fetch(0)
        fetch(1)
        scale = HD ** -0.5
        st = {}
        e_free = [(), ()]
        pT_free = ()

        def scores(hd):
            hs = slice(64 * (hd % 2), 64 * (hd % 2) + 64)
            s = hd % 2
            ch = [g * 8 + hd // 2 for g in range(3)]
            ba, bb, bc = (self.banks.take() for _ in range(3))
            for g in range(3):
                dst = ba[1][:, g * T:(g + 1) * T] if g < 2 else bb[1][:, 0:T]
                t = self.mm(dst, q[hs, ch[g], P:T], k[hs, ch[g], 0:T], True, True, *qt, *ba[2], *bb[2], signal=True)
            for g in range(3):
                t = self.mm(bc[1][:, g * P:(g + 1) * P], q[hs, ch[g], 0:P], k[hs, ch[g], 0:P], True, True, *bc[2], signal=True)
            E = e_[:, s, :]
            b_ = bias[:, s, :, ::-1]
            t1 = self.stt(E[:, 0:2 * T].rearrange("p (g c) -> p g c", g=2), ba[1][:, :].rearrange("p (g c) -> p g c", g=2),
                          scale, b_[:, 0:2, :], ALU.mult, ALU.add, t, bias_t[hd], *e_free[s])
            t2 = self.stt(E[:, 2 * T:3 * T], bb[1][:, 0:T], scale, b_[:, 2, :], ALU.mult, ALU.add, t, bias_t[hd])
            t3 = self.stt(E[:, 3 * T:].rearrange("p (g c) -> p g c", g=3), bc[1][:, 0:384].rearrange("p (g c) -> p g c", g=3),
                          scale, b_[:, :, P:T], ALU.mult, ALU.add, t, bias_t[hd])
            bias_free[s] = (t3,)
            for bk, tk in ((ba, t1), (bb, t2), (bc, t3)):
                self.banks.free(bk[0], tk)
            c = sc[:, hd, :]
            m1 = self.rmax(c[:, 1:2], E[:, 0:3 * T], t1, t2)
            m0 = self.rmax(c[:, 0:1], E[:, 3 * T:], t3)
            e1 = self.act(E[:, 0:3 * T], E[:, 0:3 * T], ACT.Exp, m1, bias=c[:, 1:2], accum=c[:, 3:4])
            e0 = self.act(E[:, 3 * T:], E[:, 3 * T:], ACT.Exp, m0, bias=c[:, 0:1], accum=c[:, 2:3])
            st[hd] = (e0, e1)
            if hd + 2 < ATT_HEADS:
                fetch(hd + 2)

        def turn(hd):
            s = hd % 2
            nonlocal pT_free
            c = sc[:, hd, :]
            st[hd, "r"] = self.recip(c[:, 4:6], c[:, 2:4], *st[hd])
            out = []
            for lo_, n_ in ((0, 4), (4, 4), (8, 1)):
                b, bank, free = self.banks.take()
                for i in range(n_):
                    t = self.transpose(bank[:, i * P:(i + 1) * P], e_[:, s, (lo_ + i) * P:(lo_ + i + 1) * P], *st[hd], *free,
                                       signal=i == n_ - 1)
                dst = pT[:, lo_:lo_ + n_, :]
                src = bank[:, 0:n_ * P].rearrange("p (a b) -> p a b", a=n_)
                if lo_ == 4:
                    e = self.copy(dst, src, t, *pT_free)
                else:
                    e = self.act(dst, src, ACT.Copy, t, *pT_free)
                self.banks.free(b, e)
                out.append(e)
            e_free[s] = (t,)
            st[hd] = out

        def values(hd):
            nonlocal pT_free
            c = sc[:, hd, :]
            b, bank, free = self.banks.take()
            vcol = lambda g: slice(g * D + hd * HD, g * D + hd * HD + HD)
            for g in range(3):
                for kb in range(2):
                    t = self.mm(bank[:, HD:2 * HD], pT[:, 2 * g + kb, :], v[:, kb, vcol(g)], g == 0 and kb == 0,
                                g == 2 and kb == 1, *st[hd], *vt, *free, signal=False)
            for g in range(3):
                t = self.mm(bank[:, 0:HD], pT[:, 6 + g, :], v[:, 0, vcol(g)], g == 0, g == 2, signal=g == 2)
            pT_free = (t,)
            d = self.ts(o[:, 0, hd * HD:(hd + 1) * HD], bank[:, 0:HD], c[:, 4:5], None, ALU.mult, None, t, st[hd, "r"])
            d = self.ts(o[:, 1, hd * HD:(hd + 1) * HD], bank[:, HD:2 * HD], c[:, 5:6], None, ALU.mult, None, t, st[hd, "r"])
            self.banks.free(b, d)

        for i in range(ATT_HEADS + 1):
            if i < ATT_HEADS:
                scores(i)
            if i >= 1:
                turn(i - 1)
                values(i - 1)
        bar = self.barrier()
        r = Unit()
        r.hi = self.place("at_hi", MID, [P, 8, T], F32R)
        r.lo = self.place("at_lo", MID + 8192, [P, 8, T], F32R)
        oT = self.place("at_oT", MID + 16384, [P, 8, T])
        r.ready = []
        for c in range(KC):
            b, bank, free = self.banks.take()
            for tb in range(TB):
                t = self.transpose(bank[:, tb * P:(tb + 1) * P], o[:, tb, c * P:(c + 1) * P], *free, signal=tb == 1)
            e = self.copy(oT[:, c, :], bank[:, 0:T], t)
            self.banks.free(b, e)
            r.ready.append(self.split_into(r.hi[:, c, :], r.lo[:, c, :], oT[:, c, :], e))
        return r

    def run(self, stop=99):
        h, io = self.h, self.io
        hT = h["hT"]
        self.acc_free = self.coef_free = self.gate_free = self.rs_free = self.x_free = ()
        self.sq_free = [(), ()]
        self.sq2_free = [(), ()]
        self.tmp_free = [(), ()]
        self.sg_free = [(), ()]
        self.diag_free = [(), (), (), ()]
        self.h_tok = [None] * KC
        self.rope_i = 0
        self.x = Unit()
        self.x.hi = self.place("x_hi", XN, [P, KC, 2 * T], F32R)
        self.x.lo = self.place("x_lo", XN + 16384, [P, KC, 2 * T], F32R)

        self.small_ready = self.load(h["small"][:, :], io["small"])
        hl = self.load(hT[:, :, :], io["hT"])
        ci = self.load(h["ident"][:, :], io["ident"])
        o1 = self.pool.do(lambda e: e.memset(h["ones"][:, :], 1.0))
        o2 = self.pool.do(lambda e: e.memset(h["mean"][:, :], 1.0 / D))
        o3 = self.pool.do(lambda e: e.memset(h["eps"][:, 0:1], EPS_RMS))
        o4 = self.pool.do(lambda e: e.memset(h["eps"][:, 1:2], EPS_LN))
        o5 = self.pool.do(lambda e: e.memset(h["one"][:, :], 1.0))
        self.cs_ready = self.act(h["cs"][:, :, :], self.small("cond").rearrange("p (k c) -> p k c", c=2), ACT.Silu,
                                 self.small_ready)
        self.h_ready = (hl,)
        for e in (self.pe, self.act_e, self.dve):
            e.first = [o5, ci, self.small_ready]
        for k in range(KC):
            self.square_sum(k, hT[:, k, :], 2 * T, hl)

        def layer(l, n2):
            x = self.prenorm(hT, 2 * T, l, "norm_ffn1", 0, self.h_ready, self.sum_tok)
            gate, upd = self.gated_update(l, 2, 0.5, 2 * T)
            self.ffn(io["ffn1_w_in"][l], io["ffn1_w_out"][l], x, 2 * T, upd, between=self.ada_step,
                     before_down=lambda half: gate() if half == 0 else None)
            self.h_ready = tuple(self.h_tok)
            if stop <= 10 * l + 1:
                return True
            x = self.prenorm(hT, 2 * T, l, "norm_mix", 3, self.h_ready, self.sum_tok)
            x = (self.even_mixer if l == 0 else self.odd_mixer)(x)
            gate, upd = self.gated_update(l, 5, 1.0, n2)
            gate()
            self.mix_out(io["mix_w_out"][l], x, n2, upd)
            self.h_ready = tuple(self.h_tok)
            if stop <= 10 * l + 2:
                return True
            x = self.prenorm(hT, n2, l, "norm_ffn2", 6, self.h_ready, self.sum_tok)
            gate, upd = self.gated_update(l, 8, 0.5, n2)
            self.ffn(io["ffn2_w_in"][l], io["ffn2_w_out"][l], x, n2, upd, between=self.ada_step,
                     before_down=lambda half: gate() if half == 0 else None)
            self.h_ready = tuple(self.h_tok)
            return stop <= 10 * l + 3

        if layer(0, 2 * T) or layer(1, T):
            return
        rb, rows, rt = self.rms_rows(T, D, EPS_RMS, self.sum_tok)
        x = self.x
        x.ready = []
        rd = []
        for k in range(KC):
            t = self.stt(hT[:, k, 0:T], hT[:, k, 0:T], self.small("final_norm", k, k + 1), rows[:, 0:T], ALU.mult, ALU.mult,
                         rt, *self.h_ready)
            x.ready.append(self.split_into(x.hi[:, k, 0:T], x.lo[:, k, 0:T], hT[:, k, 0:T], t, free=self.x_free))
            rd.append(t)
            rd += x.ready[-1]
        self.banks.free(rb, t)
        self.h_ready = tuple(rd)
        for l in range(2):
            if stop <= 21 + 10 * l:
                return
            upd = self.residual_update(1)
            r = self.retention(x) if l == 0 else self.dilated(x)
            save = self.x_free
            self.mix_out(io["ret_w_out" if l == 0 else "attn_w_out"], r, T, upd, kn=16 if l == 0 else KC)
            self.barrier()
            x = self.layer_norm(2 * l)
            upd = self.residual_update(0)
            self.ffn(io["ffn_w_up"][l], io["ffn_w_down"][l], x, T, upd)
            x = self.layer_norm(2 * l + 1, split=l == 0)

    def finish(self):
        t = [e.last() for e in (self.pe, self.act_e, self.dve, self.pool)]
        sem = self.h["out_sem"]
        hT, out = self.h["hT"], self.io["out"]
        self.sync.do(lambda e: e.dma_start(out, hT[:, :, 0:T]).then_inc(sem, 16), *t, signal=False)
        self.sync.do(lambda e: e.wait_ge(sem, 16), signal=False)


def build(nc, io, stop=99):
    with ExitStack() as ctx:
        def sb(name, shape, dt=F32):
            return ctx.enter_context(nc.sbuf_tensor(name, shape, dt))

        def sem(name):
            return ctx.enter_context(nc.semaphore(name))

        h = {
            "hT": sb("hT", [P, KC, 2 * T]), "small": sb("small", [P, SMALL_N]), "ident": sb("ident", [P, P]),
            "ones": sb("ones", [P, P]), "mean": sb("mean", [P, P]), "eps": sb("eps", [P, 2]), "one": sb("one", [P, 1]),
            "cs": sb("cs", [P, KC, 2]), "mod": sb("mod", [P, 2 * MODS * KC, 2]), "coef": sb("coef", [P, KC, 2]),
            "gate": sb("gate", [P, KC, 2]), "rs": sb("rs", [P, 24]), "rs2": sb("rs2", [P, 24]),
            "diag": sb("diag", [P, 4, P]), "lam": sb("lam", [P, 8]),
        }
        raw = sb("w_raw", [P, NRAW, UNIT])
        whi = sb("w_hi", [P, NSPLIT, UNIT], F32R)
        wlo = sb("w_lo", [P, NSPLIT, UNIT], F32R)
        h["work"] = (nc.sbuf_base + 31) // 32 * 32
        assert h["work"] + WORK <= nc.sbuf_top
        h["placed"] = {}
        h["psum"] = [ctx.enter_context(nc.psum_tensor(f"bank{i}", [P, 512], F32)) for i in range(8)]
        h["load_sems"] = [sem(f"s_load{i}") for i in range(48)]
        h["out_sem"] = sem("s_out")
        at = TEMPS

        def place(name, at, shape):
            return nc.alloc_sbuf_tensor_at(name, shape, F32, offset=h["work"] + at)
        h["acc"] = place("acc", at, [P, 2 * T])
        h["sq"] = place("sq", at + 2048, [P, 2, 2 * T])
        h["tmp"] = place("tmp", at + 6144, [P, 2, 2 * T])
        h["sg"] = place("sg", at + 10240, [P, 2, 2 * T])
        h["sq2"] = h["sg"]
        sems = {n: sem(f"s_{n}") for n in ("pe", "act", "dve", "pool")}
        raw_sems = [sem(f"s_raw{i}") for i in range(NRAW)]

        def engines():
            return [Engine(sems[n]) for n in ("pe", "act", "dve", "pool")] + [Engine(None)]

        rec = Recorder(whi, wlo, raw)
        Program(nc, io, h, engines(), rec).run(stop)
        eng = engines()
        stream = Weights(rec.plan, whi, wlo, raw, eng[4], raw_sems, eng[1], eng[2], eng[3])
        prog = Program(nc, io, h, eng, stream)
        prog.run(stop)
        prog.finish()

        block = ctx.enter_context(nc.Block())

        @block.sync
        def _(e):
            eng[4].emit(e)

        @block.tensor
        def _(e):
            eng[0].emit(e)

        @block.scalar
        def _(e):
            eng[1].emit(e)

        @block.vector
        def _(e):
            eng[2].emit(e)

        @block.gpsimd
        def _(e):
            eng[3].emit(e)


def shape_constants():
    f = np.float32
    out = {"ident": np.eye(P, dtype=f)}
    t = np.arange(T)
    ang = 2 * np.pi * np.outer(t, t) / T
    out["fourier_time"] = np.stack([np.concatenate([np.cos(ang), np.sin(ang)], 1)[b * P:(b + 1) * P] for b in range(TB)], 1)
    d = np.arange(HD)
    ang = 2 * np.pi * np.outer(d, d) / HD
    norm = 1.0 / math.sqrt(T * HD)
    two = np.eye(2)
    out["fourier_dim"] = np.stack([np.kron(two, np.cos(ang)) * norm, -np.kron(two, np.sin(ang)) * norm], 1)
    seg = np.ones((P, 2 * T))
    seg[:, ::GLA_CHUNK] = 0
    out["segments"] = seg
    big = 3.0e38
    j, i = np.meshgrid(np.arange(P), np.arange(P), indexing="ij")
    same = j // GLA_CHUNK == i // GLA_CHUNK
    lim = []
    for keep in (same & (j <= i), same & (j >= i)):
        lim += [np.where(keep, big, 0.0), np.where(keep, -big, 0.0)]
    out["limits"] = np.stack(lim, 1)[:, :, None, :]
    n = 16
    inv = (np.float32(10000.0) ** (-np.arange(n, dtype=f) / f(n))).astype(f)
    tok = np.arange(T)
    row, col = (tok // 64).astype(f), (tok % 64).astype(f)
    ang = np.concatenate([np.outer(inv, row)] * 2 + [np.outer(inv, col)] * 2, 0).astype(f)
    ang = np.concatenate([ang, ang], 0)
    out["axial"] = np.stack([np.cos(ang), np.sin(ang)], 1)
    rot = np.zeros((P, P))
    for m in range(P):
        if m % 32 < 16:
            rot[m + 16, m] = -1.0
        else:
            rot[m - 16, m] = 1.0
    out["axial_rot"] = rot
    rot = np.zeros((P, P))
    for m in range(0, P, 2):
        rot[m + 1, m] = -1.0
        rot[m, m + 1] = 1.0
    out["pair_rot"] = rot
    inv = (f(1.0) / (f(10000.0) ** np.linspace(0.0, 1.0, P, dtype=f))).astype(f)
    ang = (np.arange(T, dtype=f)[None, :] * np.repeat(inv, 2)[:, None]).astype(f).reshape(2, P, T)
    out["ret_rope"] = np.stack([np.cos(ang), np.sin(ang)], 0).transpose(2, 0, 1, 3)
    dec = []
    for hd in range(RET_HEADS):
        g = math.log(1.0 - 2.0 ** (-5.0 - hd))
        jj, ii = np.arange(P)[:, None], np.arange(T)[None, :]
        full = [np.where(ii >= jj + b * P, np.exp(np.maximum(ii - jj - b * P, 0) * g), 0.0) for b in range(2)]
        dec.append(np.concatenate([full[0], full[1][:, P:]], 1) * RET_DK ** -0.5)
    out["decay"] = np.stack(dec, 1)
    delta = np.arange(384) - 127
    onehot, mask = np.zeros((NUM_BUCKETS, 3, 384)), np.zeros((16, 3, 384))
    for g, (window, dil) in enumerate(DILATED):
        ok = (delta >= 0) & (delta <= window) & (delta % dil == 0)
        dist = np.maximum(delta, 0)
        exact = NUM_BUCKETS // 2
        large = exact + (np.log(np.maximum(dist, 1).astype(f) / f(exact)) / f(math.log(MAX_DISTANCE / exact))
                         * f(NUM_BUCKETS - exact)).astype(np.int32)
        bucket = np.where(dist < exact, dist, np.minimum(large, NUM_BUCKETS - 1))
        onehot[bucket[ok], g, np.arange(384)[ok]] = 1.0
        mask[:, g, ~ok] = NEG
    out["onehot"], out["dist_mask"] = onehot, mask
    return {k: np.ascontiguousarray(v, dtype=f) for k, v in out.items()}


def chunks(v):
    return v.reshape(-1, P).T


def tall(v):
    return np.concatenate([v, np.zeros((P - v.shape[0], v.shape[1]), v.dtype)], 0)


WEIGHTS = ["ada_w", "ffn1_w_in", "ffn1_w_out", "ffn2_w_in", "ffn2_w_out", "mix_w_out"]
PLAIN = {"even_w_in": "even_w_in", "odd_w_in": "odd_w_in", "ret_w_in": "ret_w_in_2", "ret_w_out": "ret_w_out_2",
         "attn_w_in": "attn_w_in_2", "attn_w_out": "attn_w_out_2"}
PAIRS = {"ffn_w_up": "ffn_w_up_2", "ffn_w_down": "ffn_w_down_2"}


def kernel(stop=99, **inp):
    import concourse.bacc as bacc
    from concourse.bass_utils import run_bass_kernel_spmd

    a = {k: np.asarray(v) for k, v in inp.items()}
    small = {
        "cond": np.stack([chunks(a["c"][0]), chunks(a["c_ctx"])], 2).reshape(P, -1),
        "ada_b": chunks(a["ada_b"]), "norm_ffn1": chunks(a["norm_ffn1"]), "norm_mix": chunks(a["norm_mix"]),
        "norm_ffn2": chunks(a["norm_ffn2"]), "final_norm": chunks(a["final_norm"]), "gate_b": chunks(a["gla_gate_b"]),
        "gla_norm": chunks(a["gla_norm"]), "conv_w": chunks(a["conv_w"]), "conv_b": chunks(a["conv_b"]),
        "lambdas": tall(np.concatenate([a["lambda_q1"], a["lambda_q2"], a["lambda_k1"], a["lambda_k2"]], 0).T),
        "diff_norm": chunks(a["diff_norm"]), "ln_gain": chunks(a["ln_gain_2"]), "ln_bias": chunks(a["ln_bias_2"]),
        "rel_bias": tall(a["rel_bias_2"].T),
    }
    arrays = {"small": np.ascontiguousarray(np.concatenate([small[n] for n, _ in SMALL], 1))}
    both = np.concatenate([a["x"][0], a["ctx"][0]], 0)
    arrays["hT"] = np.ascontiguousarray(both.reshape(2 * T, KC, P).transpose(2, 1, 0))
    arrays["gate_w"] = np.ascontiguousarray(a["gla_gate_w"][0])
    for n in WEIGHTS:
        arrays[n] = a[n]
    for n, src in PLAIN.items():
        arrays[n] = a[src][0]
    for n, src in PAIRS.items():
        arrays[n] = a[src]
    arrays.update(shape_constants())

    nc = bacc.Bacc("TRN2", target_bir_lowering=False, num_devices=1)
    io = {n: nc.dram_tensor("in_" + n, v.shape, F32, kind="ExternalInput").ap() for n, v in arrays.items()}
    out = nc.dram_tensor("out_T", [P, KC, T], F32, kind="ExternalOutput")
    io["out"] = out.ap()
    rows = nc.dram_tensor("bias_rows", [ATT_GROUPS, ATT_HEADS, 384], F32, kind="Internal")
    io["bias_rows"] = rows.ap()
    io["bias_windows"] = lambda hd: bass.AP(tensor=rows, offset=hd * 384, ap=[[1, P], [ATT_HEADS * 384, 3], [1, T]])
    build(nc, io, stop)
    r = run_bass_kernel_spmd(nc, [{"in_" + n: v for n, v in arrays.items()}], core_ids=[0])
    got = r.results[0]["out_T"]
    return np.ascontiguousarray(got.transpose(2, 1, 0)).reshape(1, T, D)
```

```python
import math
from contextlib import ExitStack

import numpy as np
import concourse.bass as bass
from concourse import mybir

P = 128
F32 = mybir.dt.float32
F32R = mybir.dt.float32r
ALU = mybir.AluOpType
ACT = mybir.ActivationFunctionType
AX = mybir.AxisListType.X

D = 1024
KC = D // P
T = 256
TB = T // P
FFN = 2816
FC = FFN // P
HALVES = ((0, 12), (12, 10))
EPS_RMS = 1e-6
EPS_LN = 1e-5
MODS = 9
GLA_HEADS, GLA_DK, GLA_DV, GLA_CHUNK, GLA_TAU = 6, 64, 128, 64, 16.0
NCH = 2 * T // GLA_CHUNK
DIFF_HEADS, HD = 6, 64
LAM_INIT = 0.8 - 0.6 * math.exp(-0.3)
RET_HEADS, RET_DK, RET_DV = 4, 256, 512
ATT_HEADS, ATT_GROUPS = 16, 3
DILATED = ((128, 1), (512, 4), (2048, 16))
NUM_BUCKETS, MAX_DISTANCE = 32, 2048
ALPHA = 4 ** 0.25
NEG = -1e30

SMALL = [("cond", 2 * KC), ("ada_b", 2 * MODS * KC), ("norm_ffn1", 2 * KC), ("norm_mix", 2 * KC),
         ("norm_ffn2", 2 * KC), ("final_norm", KC), ("gate_b", 6), ("gla_norm", 1), ("conv_w", 6),
         ("conv_b", 2), ("lambdas", 4), ("diff_norm", 1), ("ln_gain", 4 * KC), ("ln_bias", 4 * KC),
         ("rel_bias", 48)]
SMALL_AT = {}
_at = 0
for _name, _n in SMALL:
    SMALL_AT[_name] = (_at, _at + _n)
    _at += _n
SMALL_N = _at

XN, MID, TEMPS, WORK = 0, 32768, 90496, 106880
UNIT = 2048
NRAW, NSPLIT = 4, 3


class Engine:

    def __init__(self, sem):
        self.sem, self.count, self.steps, self.first = sem, 0, [], []

    def do(self, op, *after, signal=True):
        waits = [t for t in (*self.first, *after) if t is not None]
        self.first = []
        self.steps.append([waits, op, signal])
        if signal:
            self.count += 1
            return (self.sem, self.count)
        return None

    def last(self):
        if not self.steps:
            return None
        if not self.steps[-1][2]:
            self.steps[-1][2] = True
            self.count += 1
        return (self.sem, self.count)

    def emit(self, eng):
        seen = {}
        for waits, op, signal in self.steps:
            need = {}
            for sem, value in waits:
                if value > max(seen.get(sem.name, 0), need.get(sem.name, (None, 0))[1]):
                    need[sem.name] = (sem, value)
            for name, (sem, value) in need.items():
                eng.wait_ge(sem, value)
                seen[name] = value
            ins = op(eng)
            if signal:
                ins.then_inc(self.sem, 1)


class Banks:

    def __init__(self, tiles):
        self.tiles, self.order, self.readers = tiles, list(range(len(tiles))), [()] * len(tiles)

    def take(self):
        b = self.order.pop(0)
        return b, self.tiles[b], self.readers[b]

    def free(self, b, *readers):
        self.readers[b] = readers
        self.order.append(b)


class Unit:
    pass


class Recorder:

    def __init__(self, hi, lo, raw):
        self.plan, self.tiles = [], (hi, lo, raw)

    def take(self, w, k0, kn, c0, cn, split=True):
        self.plan.append((w, k0, kn, c0, cn, split))
        u = Unit()
        u.hi, u.lo, u.raw = (t[:, 0, 0:kn * cn].rearrange("p (k c) -> p k c", k=kn) for t in self.tiles)
        u.ready = ()
        return u

    def done(self, unit, token):
        pass


class Weights:

    def __init__(self, plan, hi, lo, raw, sync, sems, act, dve, pool):
        self.plan, self.hi, self.lo, self.raw = plan, hi, lo, raw
        self.sync, self.sems, self.act, self.dve, self.pool = sync, sems, act, dve, pool
        self.loaded = self.split = self.taken = 0
        self.raw_free = [()] * NRAW
        self.split_free = [()] * NSPLIT
        self.split_slot = 0
        self.units = []

    def load_tile(self):
        i = self.loaded
        w, k0, kn, c0, cn, split = self.plan[i]
        slot = i % NRAW
        u = Unit()
        u.index, u.slot, u.is_split = i, slot, split
        u.raw = self.raw[:, slot, 0:kn * cn].rearrange("p (k c) -> p k c", k=kn)
        src = w[k0 * P:(k0 + kn) * P, c0:c0 + cn].rearrange("(k p) c -> p k c", p=P)
        self.sync.do(lambda e: e.dma_start(u.raw, src).then_inc(self.sems[slot], 16), *self.raw_free[slot], signal=False)
        u.loaded = (self.sems[slot], 16 * (i // NRAW + 1))
        u.ready = (u.loaded,)
        self.raw_free[slot] = None
        self.units.append(u)
        self.loaded += 1

    def split_tile(self, u):
        s = self.split_slot
        _, k0, kn, c0, cn, _ = self.plan[u.index]
        n = kn * cn
        raw, hi, lo = self.raw[:, u.slot, 0:n], self.hi[:, s, 0:n], self.lo[:, s, 0:n]
        u.hi = hi.rearrange("p (k c) -> p k c", k=kn)
        u.lo = lo.rearrange("p (k c) -> p k c", k=kn)
        a = self.act.do(lambda e: e.activation(hi, raw, ACT.Copy), u.loaded, *self.split_free[s])
        b = self.dve.do(lambda e: e.tensor_tensor(lo, raw, hi.bitcast(F32), ALU.subtract), a, u.loaded,
                        *self.split_free[s])
        u.ready = (a, b)
        self.raw_free[u.slot] = (a, b)
        self.split_free[s] = None
        u.split_slot = s
        self.split_slot = (s + 1) % NSPLIT
        self.split += 1

    def pump(self):
        moved = True
        while moved:
            moved = False
            if self.loaded < len(self.plan) and self.raw_free[self.loaded % NRAW] is not None:
                self.load_tile()
                moved = True
            if self.split < self.loaded:
                u = self.units[self.split]
                if not u.is_split:
                    self.split += 1
                    moved = True
                elif self.split_free[self.split_slot] is not None:
                    self.split_tile(u)
                    moved = True

    def take(self, w, k0, kn, c0, cn, split=True):
        self.pump()
        u = self.units[self.taken]
        assert self.taken < self.split and self.plan[self.taken][1:] == (k0, kn, c0, cn, split)
        self.taken += 1
        return u

    def done(self, u, token):
        if u.is_split:
            self.split_free[u.split_slot] = (token,)
        else:
            self.raw_free[u.slot] = (token,)
        self.pump()


class Program:
    def __init__(self, nc, io, handles, engines, stream):
        self.nc, self.io, self.h = nc, io, handles
        self.pe, self.act_e, self.dve, self.pool, self.sync = engines
        self.w = stream
        self.banks = Banks(handles["psum"])
        self.ada_next = 0
        self.loads = 0
        self.mod_ready = {}

    def mm(self, out, lhsT, rhs, start, stop, *after, signal=False, loose=False):
        return self.pe.do(lambda e: e.matmul(out, lhsT, rhs, start=start, stop=stop,
                                             skip_group_check=loose), *after, signal=signal)

    def transpose(self, out, in_, *after, signal=False):
        ident = self.h["ident"]
        return self.pe.do(lambda e: e.transpose(out, in_, ident[:, :]), *after, signal=signal)

    def act(self, out, in_, func, *after, scale=1.0, bias=0.0, accum=None):
        if accum is None:
            return self.act_e.do(lambda e: e.activation(out, in_, func, bias=bias, scale=scale), *after)
        return self.act_e.do(lambda e: e.activation(out, in_, func, bias=bias, scale=scale,
                                                    accum_out=accum), *after)

    def tt(self, out, a, b, op, *after, eng=None):
        return (eng or self.dve).do(lambda e: e.tensor_tensor(out, a, b, op), *after)

    def ts(self, out, a, s1, s2, op0, op1, *after, eng=None):
        if s2 is None:
            return (eng or self.dve).do(lambda e: e.tensor_scalar(out, a, s1, None, op0), *after)
        return (eng or self.dve).do(lambda e: e.tensor_scalar(out, a, s1, s2, op0, op1), *after)

    def stt(self, out, a, s, b, op0, op1, *after):
        return self.dve.do(lambda e: e.scalar_tensor_tensor(out, a, s, b, op0, op1), *after)

    def scan(self, out, keep, a, *after):
        return self.dve.do(lambda e: e.tensor_tensor_scan(out, keep, a, 0.0, ALU.mult, ALU.add), *after)

    def recip(self, out, a, *after):
        return self.dve.do(lambda e: e.reciprocal(out, a), *after)

    def rmax(self, out, a, *after):
        return self.dve.do(lambda e: e.tensor_reduce(out, a, AX, ALU.max, negate=True), *after)

    def copy(self, out, a, *after):
        return self.dve.do(lambda e: e.tensor_copy(out, a), *after)

    def load(self, dst, src, *after):
        sem = self.h["load_sems"][self.loads]
        self.loads += 1
        self.sync.do(lambda e: e.dma_start(dst, src).then_inc(sem, 16), *after, signal=False)
        return (sem, 16)

    def place(self, name, at, shape, dtype=F32):
        key = (name, at)
        if key not in self.h["placed"]:
            self.h["placed"][key] = self.nc.alloc_sbuf_tensor_at(name, shape, dtype, offset=self.h["work"] + at)
        return self.h["placed"][key]

    def barrier(self):
        tokens = [e.last() for e in (self.pe, self.act_e, self.dve, self.pool)]
        for e in (self.pe, self.act_e, self.dve, self.pool):
            e.first = list(tokens)
        return tokens

    def small(self, name, a=0, b=None):
        s, e = SMALL_AT[name]
        return self.h["small"][:, s + a:(e if b is None else s + b)]

    def product3(self, out, a_hi, a_lo, b_hi, b_lo, start, stop, *after, signal=False):
        self.mm(out, a_hi, b_hi, start, False, *after)
        self.mm(out, a_hi, b_lo, False, False)
        return self.mm(out, a_lo, b_hi, False, stop, signal=signal)

    def project(self, u, c, x, n, bank, after, ks=range(KC), k0=0, start=True, stop=True, cols=0):
        ks = list(ks)
        for i, k in enumerate(ks):
            t = self.product3(bank[:, 0:n], u.hi[:, k - k0, c:c + P], u.lo[:, k - k0, c:c + P],
                              x.hi[:, k, cols:cols + n], x.lo[:, k, cols:cols + n],
                              start and i == 0, stop and i == len(ks) - 1,
                              *u.ready, *x.ready[k], *(after if i == 0 else ()), signal=i == len(ks) - 1)
        return t

    def project_first(self, units, x, n, **kw):
        jobs = [(u, c, *self.banks.take()) for u in units for c in (0, P)]
        for k in range(KC):
            out = []
            for u, c, b, bank, free in jobs:
                t = self.product3(bank[:, 0:n], u.hi[:, k, c:c + P], u.lo[:, k, c:c + P], x.hi[:, k, 0:n], x.lo[:, k, 0:n],
                                  k == 0, k == KC - 1, *u.ready, *x.ready[k], *free, signal=k == KC - 1)
                out.append((b, bank, t))
        return out

    def project_tiles(self, w, cols, x, n, between=lambda: None):
        for i in range(0, len(cols), 2):
            pair = cols[i:i + 2]
            if i == 0 and len(pair) == 2:
                us = [self.w.take(w, 0, KC, c, 256) for c in pair]
                done = self.project_first(us, x, n)
                for q, u in enumerate(us):
                    self.w.done(u, done[2 * q + 1][2])
                    yield done[2 * q:2 * q + 2]
                between()
            else:
                for c in pair:
                    u = self.w.take(w, 0, KC, c, 256)
                    done = []
                    for q in range(2):
                        b, bank, free = self.banks.take()
                        done.append((b, bank, self.project(u, q * P, x, n, bank, free)))
                    self.w.done(u, done[1][2])
                    yield done
                    between()

    def project_rows(self, u, cn, x, tb, bank, after):
        for k in range(KC):
            t = self.product3(bank[:, 0:cn], x.hi[:, k, tb * P:(tb + 1) * P], x.lo[:, k, tb * P:(tb + 1) * P],
                              u.hi[:, k, 0:cn], u.lo[:, k, 0:cn], k == 0, k == KC - 1,
                              *u.ready, *x.ready[k], *(after if k == 0 else ()), signal=k == KC - 1)
        return t

    def ada_step(self):
        if self.ada_next >= 2 * MODS * 4:
            self.ada_finish()
            return
        h = self.h
        i = self.ada_next
        self.ada_next += 1
        layer, c = divmod(i, MODS * 4)
        u = self.w.take(self.io["ada_w"][layer], 0, KC, c * 256, 256, split=False)
        b, bank, free = self.banks.take()
        for k in range(KC):
            g = k % 4
            t = self.mm(bank[32 * g:32 * g + 32, 0:256], h["cs"][:, k, :], u.raw[:, k, :], k < 4, k >= 4,
                        *u.ready, self.cs_ready, *free, signal=k >= 4)
        self.w.done(u, t)
        s = i % 2
        e = self.act(h["ada_rows"][:, s, :], bank[:, 0:256], ACT.Copy, t, *self.ada_free[s])
        self.banks.free(b, e)
        self.ada_finish()
        self.ada_open = (i, s, e, layer * MODS * KC + 2 * c)

    def ada_finish(self):
        if self.ada_open is None:
            return
        h = self.h
        i, s, e, at = self.ada_open
        self.ada_open = None
        b, bank, free = self.banks.take()
        for j in range(2):
            t = self.mm(bank[:, 2 * j:2 * j + 2], h["ada_rows"][:, s, j * P:(j + 1) * P], h["fold"][:, :], True, True,
                        e, self.fold_ready, *free, signal=j == 1)
        self.ada_free[s] = (t,)
        bias = self.small("ada_b", at, at + 2).rearrange("p (j o) -> p j o", o=1).broadcast_to([P, 2, 2])
        e = self.tt(h["mod"][:, at:at + 2, :], bank[:, 0:4].rearrange("p (j c) -> p j c", j=2), bias,
                    ALU.add, t, self.small_ready)
        self.mod_ready[i] = e
        self.banks.free(b, e)

    def ada_until(self, layer, part):
        last = (layer * MODS + part + 1) * 4
        while self.ada_next < last:
            self.ada_step()
        if last - 1 not in self.mod_ready:
            self.ada_finish()
        return self.mod_ready[last - 1]

    def mod(self, layer, part):
        at = (layer * MODS + part) * KC
        return self.h["mod"][:, at:at + KC, :]

    def square_sum(self, k, src, n, *after):
        h = self.h
        if k == 0:
            self.sum_tok = self.act(h["acc"][:, 0:n], src, ACT.Square, *after, *self.acc_free)
            return
        s = k % 2
        t = self.act(h["sq"][:, s, 0:n], src, ACT.Square, *after, *self.sq_free[s])
        self.sum_tok = self.tt(h["acc"][:, 0:n], h["acc"][:, 0:n], h["sq"][:, s, 0:n], ALU.add, t, self.sum_tok,
                               eng=self.pool)
        self.sq_free[s] = (self.sum_tok,)

    def columns_to_rows(self, stat_bank, stat_ready, ncol, width, eps, banks_out):
        h = self.h
        t = self.act(h["rs"][:, 0:ncol], stat_bank[:, 0:ncol], ACT.Sqrt, stat_ready, *self.rs_free,
                     scale=1.0 / width, bias=h["eps"][:, 0:1] if eps == EPS_RMS else h["eps"][:, 1:2])
        stat_read = t
        t = self.recip(h["rs2"][:, 0:ncol], h["rs"][:, 0:ncol], t, *self.rs_free)
        out = []
        for c in range(ncol):
            s = c % 4
            d = self.ts(h["diag"][:, s, :], h["ident"][:, :], h["rs2"][:, c:c + 1], None, ALU.mult, None, t,
                        *self.diag_free[s])
            bank, at, free = banks_out[c]
            m = self.mm(bank[:, at:at + P], h["ones"][:, :], h["diag"][:, s, :], True, True, d, *free, signal=True)
            self.diag_free[s] = (m,)
            out.append(m)
        self.rs_free = (d,)
        return stat_read, out

    def rms_rows(self, n, width, eps, sum_tok):
        h = self.h
        sb, stat, sfree = self.banks.take()
        for tb in range(n // P):
            t = self.mm(stat[:, tb:tb + 1], h["acc"][:, tb * P:(tb + 1) * P], h["ones"][:, 0:1], True, True,
                        sum_tok, *sfree, signal=True)
        self.acc_free = (t,)
        rb, rows, rfree = self.banks.take()
        read, toks = self.columns_to_rows(stat, t, n // P, width, eps, [(rows, tb * P, rfree) for tb in range(n // P)])
        self.banks.free(sb, read)
        return rb, rows, toks[-1]

    def prenorm(self, hT, n, layer, gain, shift_part, hT_ready, sum_tok):
        h = self.h
        mt = self.ada_until(layer, shift_part + 1)
        g = self.small(gain, layer * KC, (layer + 1) * KC).rearrange("p (k o) -> p k o", o=1).broadcast_to([P, KC, 2])
        a = self.stt(h["coef"][:, :, :], self.mod(layer, shift_part + 1), 1.0, g, ALU.add, ALU.mult, mt, self.small_ready,
                     *self.coef_free)
        rb, rows, rt = self.rms_rows(n, D, EPS_RMS, sum_tok)
        x = self.x
        x.ready = []
        for k in range(KC):
            ready = []
            s = k % 2
            for c in range(n // T):
                cs = slice(c * T, (c + 1) * T)
                t = self.stt(h["tmp"][:, s, cs], hT[:, k, cs], h["coef"][:, k, c:c + 1], rows[:, cs], ALU.mult, ALU.mult,
                             a, rt, *hT_ready, *self.tmp_free[s])
                shift = self.mod(layer, shift_part)[:, k, c:c + 1]
                e = self.act(x.hi[:, k, cs], h["tmp"][:, s, cs], ACT.Identity, t, mt, *self.x_free, bias=shift)
                f = self.stt(x.lo[:, k, cs], h["tmp"][:, s, cs], shift, x.hi[:, k, cs].bitcast(F32), ALU.add, ALU.subtract,
                             e, t, *self.x_free)
                ready += [e, f]
            self.tmp_free[s] = tuple(ready)
            x.ready.append(ready)
        self.banks.free(rb, f)
        self.coef_free = (f,)
        return x

    def split_into(self, hi, lo, src, *after, free=()):
        a = self.act(hi, src, ACT.Copy, *after, *free)
        b = self.tt(lo, src, hi.bitcast(F32), ALU.subtract, a, *after, *free)
        return [a, b]

    def ffn(self, w_in, w_out, x, n, update, between=lambda: None, before_down=lambda half: None):
        h = self.h
        hid_hi = self.place("hid_hi", MID, [P, 12, 2 * T], F32R)
        hid_lo = self.place("hid_lo", MID + 24576, [P, 12, 2 * T], F32R)
        hid_free = ()
        gates = [None, None]

        def gated(q, b, bank, t):
            gates[q] = self.act(h["sg"][:, q, 0:n], bank[:, 0:n], ACT.Silu, t, *self.sg_free[q])
            self.banks.free(b, gates[q])

        for half, (j0, jn) in enumerate(HALVES):
            ready = []
            for j in range(j0, j0 + jn, 2):
                if j == 0:
                    ug, uu = (self.w.take(w_in, 0, KC, base + j * P, 256) for base in (0, FFN))
                    done = self.project_first((ug, uu), x, n)
                    self.w.done(ug, done[3][2])
                    self.w.done(uu, done[3][2])
                else:
                    done = []
                    for base in (0, FFN):
                        u = self.w.take(w_in, 0, KC, base + j * P, 256)
                        for q in range(2):
                            b, bank, free = self.banks.take()
                            done.append((b, bank, self.project(u, q * P, x, n, bank, free)))
                            if base == 0:
                                gated(q, *done[-1])
                        self.w.done(u, done[-1][2])
                for q in range(2):
                    if j == 0:
                        gated(q, *done[q])
                    b, bank, t = done[2 + q]
                    d = self.tt(h["tmp"][:, q, 0:n], bank[:, 0:n], h["sg"][:, q, 0:n], ALU.mult, t, gates[q],
                                *self.tmp_free[q])
                    self.banks.free(b, d)
                    self.sg_free[q] = (d,)
                    r = self.split_into(hid_hi[:, j - j0 + q, 0:n], hid_lo[:, j - j0 + q, 0:n], h["tmp"][:, q, 0:n],
                                        d, free=hid_free)
                    self.tmp_free[q] = tuple(r)
                    ready.append(r)
                between()
            if half == 1:
                self.x_free = (t,)
            before_down(half)
            hid = Unit()
            hid.hi, hid.lo, hid.ready = hid_hi, hid_lo, ready
            hk = jn // 2
            for c in range(KC // 2):
                pair = [self.banks.take() for _ in range(2)]
                for part in range(2):
                    u = self.w.take(w_out, j0 + part * hk, hk, c * 256, 256)
                    ends = []
                    for q in range(2):
                        t = self.project(u, q * P, hid, n, pair[q][1], pair[q][2],
                                         ks=range(part * hk, part * hk + hk), k0=part * hk, start=part == 0, stop=part == 1)
                        ends.append(t)
                    self.w.done(u, t)
                for q in range(2):
                    d = update(2 * c + q, pair[q][1], ends[q], half)
                    self.banks.free(pair[q][0], d)
                between()
            hid_free = (t,)

    def gated_update(self, layer, part, factor, n, last_half=1):
        h = self.h
        hT = h["hT"]

        def gate():
            mt = self.ada_until(layer, part)
            self.gate_ready = self.ts(h["gate"][:, :, :], self.mod(layer, part), factor, None, ALU.mult, None, mt,
                                      *self.gate_free)

        def update(k, bank, ready, half):
            ends = []
            for c in range(n // T):
                cs = slice(c * T, (c + 1) * T)
                ends.append(self.stt(hT[:, k, cs], bank[:, cs], h["gate"][:, k, c:c + 1], hT[:, k, cs], ALU.mult, ALU.add,
                                     ready, self.gate_ready, *self.h_ready))
            self.gate_free = (ends[-1],)
            self.h_tok[k] = ends[-1]
            if half == last_half:
                self.square_sum(k, hT[:, k, 0:n], n, *ends)
            return ends[-1]

        return gate, update

    def mix_out(self, w_out, x, n, update, kn=KC):
        c = 0
        if kn == KC:
            for c, done in enumerate(self.project_tiles(w_out, [0, 256, 512, 768], x, n, self.ada_step)):
                for q, (b, bank, t) in enumerate(done):
                    self.banks.free(b, update(2 * c + q, bank, t, 1))
            self.x_free = (t,)
            return
        for c in range(KC // 2):
            pair = [self.banks.take() for _ in range(2)]
            for k0 in range(0, kn, KC):
                u = self.w.take(w_out, k0, KC, c * 256, 256)
                ends = []
                for q in range(2):
                    t = self.project(u, q * P, x, n, pair[q][1], pair[q][2], ks=range(k0, k0 + KC), k0=k0,
                                     start=k0 == 0, stop=k0 + KC == kn)
                    ends.append(t)
                self.w.done(u, t)
            for q in range(2):
                self.banks.free(pair[q][0], update(2 * c + q, pair[q][1], ends[q], 1))
        self.x_free = (t,)

    def evac(self, dst, bank, t, eng="act", func=ACT.Copy, scale=1.0, *after):
        if eng == "act":
            return self.act(dst, bank, func, t, *after, scale=scale)
        return self.copy(dst, bank, t, *after)

    def even_mixer(self, x):
        h, io, n = self.h, self.io, 2 * T
        w = io["even_w_in"]
        q = self.place("gla_q", MID, [P, 3, n])
        k = self.place("gla_k", MID + 6144, [P, 3, n])
        v = self.place("gla_v", MID + 12288, [P, 4, 768])
        r = self.place("gla_r", MID + 24576, [P, 6, n])
        zf = self.place("gla_zf", MID + 36864, [P, 4, 256])
        zg = self.place("gla_zg", MID + 40960, [P, n])
        gw = self.place("gla_gw", MID + 43008, [P, 2, 384])
        fy = self.place("four_y", MID + 46080, [P, 2, n])
        bar = self.barrier()
        z = self.pool.do(lambda e: e.memset(gw[96:128, :, :], 0.0), *bar)
        gwt = [self.load(gw[96 + 16 * d:112 + 16 * d, d, :], io["gate_w"][d], z, *bar) for d in range(2)]

        qk = []
        for c, done in enumerate(self.project_tiles(w, [256, 512, 768], x, n, self.ada_step)):
            for j, (b, bank, t) in enumerate(done):
                m = 2 * c + j
                dst = q[:, m, :] if m < 3 else k[:, m - 3, :]
                e = self.act(dst, bank[:, :], ACT.Copy, t, scale=GLA_DK ** -0.5 if m < 3 else 1.0)
                self.banks.free(b, e)
                qk.append(e)
        u = self.w.take(w, 0, KC, 2592 - P, P)
        b, bank, free = self.banks.take()
        t = self.project(u, 0, x, n, bank, free)
        self.w.done(u, t)
        zgt = self.act(zg[96:128, :], bank[96:128, :], ACT.Copy, t)
        self.banks.free(b, zgt)

        def rows(c0, dst, c):
            u = self.w.take(w, 0, KC, c0, 256)
            ends = []
            for tb in range(4):
                b, bank, free = self.banks.take()
                t = self.project_rows(u, 256, x, tb, bank, free)
                e = self.copy(dst[:, tb, c:c + 256], bank[:, 0:256], t)
                self.banks.free(b, e)
                ends.append(e)
            self.w.done(u, t)
            self.ada_step()
            return ends
        zft = rows(0, zf, 0)
        vt = [e for c in range(3) for e in rows(1024 + 256 * c, v, 256 * c)]
        rt = []
        for c in range(3):
            u = self.w.take(w, 0, KC, 1792 + 256 * c, 256)
            for j in range(2):
                b, bank, free = self.banks.take()
                t = self.project(u, j * P, x, n, bank, free)
                e = self.act(r[:, 2 * c + j, :], bank[:, :], ACT.Silu, t)
                self.banks.free(b, e)
                rt.append(e)
            self.w.done(u, t)
            self.ada_step()
        self.ada_finish()
        bar = self.barrier()

        ft = self.place("four_t", XN, [P, 2, 512])
        fd = self.place("four_d", XN + 8192, [P, 2, 128])
        seg = self.place("seg", XN + 9216, [P, n])
        lim = self.place("lim", XN + 11264, [P, 4, 1, P])
        fa = self.place("four_a", XN + 4096, [P, 2, 512])
        cft = self.load(ft[:, :, :], io["fourier_time"], *bar)
        cfd = self.load(fd[:, :, :], io["fourier_dim"], *bar)
        cseg = self.load(seg[:, :], io["segments"], *bar)
        clim = self.load(lim[:, :, :, :], io["limits"], *bar)

        def fourier():
          fa_free = [(), ()]
          for c in range(2):
            for part in range(2):
                b, bank, free = self.banks.take()
                for tb in range(2):
                    t = self.mm(bank[:, :], zf[:, 2 * part + tb, c * P:(c + 1) * P], ft[:, tb, :], tb == 0, tb == 1,
                                cft, *free, *zft, signal=True)
                s = part
                e = self.copy(fa[:, s, :], bank[:, :], t, *fa_free[s])
                self.banks.free(b, e)
                b, bank, free = self.banks.take()
                self.mm(bank[:, 0:T], fd[:, 0, :], fa[:, s, 0:T], True, False, e, cfd, *free)
                t = self.mm(bank[:, 0:T], fd[:, 1, :], fa[:, s, T:2 * T], False, True, signal=True)
                fa_free[s] = (t,)
                e = self.act(fy[:, c, part * T:(part + 1) * T], bank[:, 0:T], ACT.Copy, t)
                self.banks.free(b, e)

        spots = [TEMPS + 14336, TEMPS + 12288] + [XN + 13312 + 2048 * i for i in range(7)] + \
                [MID + 50176 + 2048 * i for i in range(6)] + [MID + 36864, MID + 38912]
        st_at = (XN + 27648, MID + 62464)
        dirs = []
        for d in range(2):
            o = Unit()
            o.ls = self.place(f"gla_ls{d}", spots.pop(0), [P, n])
            o.l = self.place(f"gla_l{d}", spots.pop(0), [P, n])
            o.order = [4, 5, 6, 7, 0, 1, 2, 3] if d == 0 else [7, 6, 5, 4, 3, 2, 1, 0]
            o.st = self.place(f"gla_st{d}", st_at[d], [P, 7, P])
            o.sets = []
            o.st_free = ()
            dirs.append(o)
        ksn = self.place("gla_ksn", spots.pop(0), [P, 4, P])
        for e in range(2):
            for d, o in enumerate(dirs):
                w_ = Unit()
                w_.qd = self.place(f"gla_qd{d}{e}", spots.pop(0), [P, n])
                w_.kd = self.place(f"gla_kd{d}{e}", spots.pop(0), [P, n])
                w_.ks = self.place(f"gla_ks{d}{e}", spots.pop(0), [P, n])
                w_.dec = self.place(f"gla_dec{d}{e}", XN + 31232 + 64 * d + 32 * e, [P, 8])
                w_.free = ()
                o.sets.append(w_)
        att = self.place("gla_att", XN, [P, 4, 4, P])
        sbank_b, sbank, sfree = self.banks.take()
        ksn_free = [()]
        att_free = [(), (), (), ()]
        inv = 1.0 / GLA_TAU
        by_chunk = lambda ap: ap.rearrange("p (c i) -> p c i", i=GLA_CHUNK)

        def gates(m):
            for d, o in enumerate(dirs):
                b, bank, free = self.banks.take()
                t = self.mm(bank[:, :], gw[96:128, d, m * P:(m + 1) * P], zg[96:128, :], True, True, zgt, *gwt, *free,
                            signal=True)
                gb = self.small("gate_b", d * 3 + m, d * 3 + m + 1)
                o.t1 = self.ts(o.ls[:, :], bank[:, :], gb, None, ALU.add, None, t)
                self.banks.free(b, o.t1)
            for o in dirs:
                o.t2 = self.stt(o.l[:, :], o.ls[:, :], -1.0, o.ls[:, :], ALU.mult, ALU.min, o.t1)
                o.t3 = self.act(o.l[:, :], o.l[:, :], ACT.Exp, o.t2)
                o.t4 = self.act(o.l[:, :], o.l[:, :], ACT.Ln, o.t3, bias=h["one"][:, 0:1])
            for o in dirs:
                o.t5 = self.stt(o.ls[:, :], o.ls[:, :], 0.0, o.l[:, :], ALU.min, ALU.subtract, o.t4, o.t1)

        def decays(m):
            for d, o in enumerate(dirs):
                w_ = o.sets[m % 2]
                line = o.ls[:, :] if d == 0 else o.ls[:, ::-1]
                o.t6 = self.scan(line, seg[:, :], line, o.t5, cseg)
                ends = by_chunk(o.ls[:, :])[:, :, 63:64] if d == 0 else by_chunk(o.ls[:, :])[:, :, 0:1]
                w_.dec_t = self.act(w_.dec[:, :], ends, ACT.Exp, o.t6, *w_.free, scale=inv)
                w_.e1 = self.act(w_.qd[:, :], o.ls[:, :], ACT.Exp, o.t6, *w_.free, scale=inv)
                w_.e2 = self.act(w_.kd[:, :], o.ls[:, :], ACT.Exp, o.t6, *w_.free, scale=-inv)
                o.d1 = self.tt(by_chunk(o.l[:, :]), ends.broadcast_to([P, NCH, GLA_CHUNK]), by_chunk(o.ls[:, :]),
                               ALU.subtract, o.t6, o.t5)
                w_.e3 = self.act(w_.ks[:, :], o.l[:, :], ACT.Exp, o.d1, *w_.free, scale=inv)

        def decayed(m):
            for o in dirs:
                w_ = o.sets[m % 2]
                w_.qd_t = self.tt(w_.qd[:, :], w_.qd[:, :], q[:, m, :], ALU.mult, w_.e1, *qk)
                w_.kd_t = self.tt(w_.kd[:, :], w_.kd[:, :], k[:, m, :], ALU.mult, w_.e2, *qk, eng=self.pool)
                w_.ks_t = self.tt(w_.ks[:, :], w_.ks[:, :], k[:, m, :], ALU.mult, w_.e3, *qk)

        def states(m):
            for d, o in enumerate(dirs):
                w_ = o.sets[m % 2]
                b, bank, free = self.banks.take()
                for tb in range(4):
                    t = self.transpose(bank[:, tb * P:(tb + 1) * P], w_.ks[:, tb * P:(tb + 1) * P], w_.ks_t, *free,
                                       signal=tb == 3)
                kst = self.act(ksn[:, :, :], bank[:, :].rearrange("p (a b) -> p a b", a=4), ACT.Copy, t, *ksn_free[0])
                self.banks.free(b, kst)
                ub = [self.banks.take() for _ in range(2)]
                for c in o.order[:7]:
                    pr, tb = 64 * (c % 2), c // 2
                    for hl in range(2):
                        t = self.mm(ub[c % 2][1][64 * hl:64 * hl + 64, tb * P:(tb + 1) * P],
                                    ksn[pr:pr + 64, tb, 64 * hl:64 * hl + 64],
                                    v[pr:pr + 64, tb, (2 * m + hl) * P:(2 * m + hl + 1) * P], True, True,
                                    kst, *vt, *ub[c % 2][2], signal=True)
                ksn_free[0] = (t,)
                for s, c in enumerate(o.order[:7]):
                    up = ub[c % 2][1][:, (c // 2) * P:(c // 2 + 1) * P]
                    if s == 0:
                        st = self.copy(o.st[:, 0, :], up, t, *o.st_free)
                    else:
                        st = self.stt(o.st[:, s, :], o.st[:, s - 1, :], w_.dec[:, c:c + 1], up, ALU.mult, ALU.add, st, t,
                                      w_.dec_t)
                o.st_t = st
                for bb in ub:
                    self.banks.free(bb[0], st)

        def inside(m):
            for d, o in enumerate(dirs):
                w_ = o.sets[m % 2]
                for hl in range(2):
                    b, bank, free = self.banks.take()
                    hs = slice(64 * hl, 64 * hl + 64)
                    for tb in range(4):
                        t = self.mm(bank[:, tb * P:(tb + 1) * P], w_.kd[hs, tb * P:(tb + 1) * P],
                                    w_.qd[hs, tb * P:(tb + 1) * P], True, True, w_.kd_t, w_.qd_t, *free, signal=tb == 3)
                    i = 2 * d + hl
                    a = att[:, i, :, :]
                    t1 = self.tt(a, bank[:, :].rearrange("p (a b) -> p a b", a=4),
                                 lim[:, 2 * d, :, :].broadcast_to([P, 4, P]), ALU.min, t, clim, *att_free[i])
                    self.banks.free(b, t1)
                    att_t[i] = self.tt(a, a, lim[:, 2 * d + 1, :, :].broadcast_to([P, 4, P]), ALU.max, t1)

        def outputs(m):
            for hl in range(2):
                hd = 2 * m + hl
                hs = slice(64 * hl, 64 * hl + 64)
                b, bank, free = self.banks.take()
                first = True
                for d, o in enumerate(dirs):
                    for tb in range(4):
                        self.mm(bank[:, tb * P:(tb + 1) * P], v[:, tb, hd * P:(hd + 1) * P], att[:, 2 * d + hl, tb, :],
                                first, False, att_t[2 * d + hl], *free, loose=True)
                        first = False
                for d, o in enumerate(dirs):
                    w_ = o.sets[m % 2]
                    for s, c in enumerate(o.order[1:]):
                        t = self.mm(bank[:, c * 64:(c + 1) * 64], o.st[hs, s, :], w_.qd[hs, c * 64:(c + 1) * 64], False,
                                    d == 1 and s == 6, o.st_t, w_.qd_t, loose=True, signal=d == 1 and s == 6)
                att_free[hl] = att_free[2 + hl] = (t,)
                y1 = self.tt(r[:, hd, :], r[:, hd, :], bank[:, :], ALU.mult, t, *rt)
                sq = h["sq2"]
                y2 = self.act(sq[:, 0, :], bank[:, :], ACT.Square, t, y1, *self.sq2_free[0])
                self.banks.free(b, y2)
                for tb in range(4):
                    t2 = self.mm(sbank[:, hd * 4 + tb:hd * 4 + tb + 1], sq[:, 0, tb * P:(tb + 1) * P], h["ones"][:, 0:1],
                                 True, True, y2, *sfree, signal=True)
                self.sq2_free[0] = (t2,)
                self.stat_t = t2
            for o in dirs:
                o.sets[m % 2].free = (t,)
                o.st_free = (t,)

        att_t = {}
        gates(0)
        fourier()
        decays(0)
        decayed(0)
        for m in range(3):
            if m < 2:
                gates(m + 1)
            inside(m)
            if m < 2:
                decays(m + 1)
            states(m)
            if m < 2:
                decayed(m + 1)
            outputs(m)
        t = self.stat_t
        bar = self.barrier()
        xh, xl = self.x.hi, self.x.lo
        self.x.ready = [self.split_into(xh[:, c, :], xl[:, c, :], fy[:, c, :]) for c in range(2)]
        outs, taken = [], []
        for hd in range(6):
            b, bank, free = self.banks.take()
            taken.append((b, bank))
            outs += [(bank, tb * P, free) for tb in range(4)]
            if len(taken) == 6:
                break
        read, toks = self.columns_to_rows(sbank, t, 24, GLA_DV, EPS_RMS, outs)
        self.banks.free(sbank_b, read)
        for hd in range(6):
            y = self.stt(r[:, hd, :], r[:, hd, :], self.small("gla_norm"), taken[hd][1][:, :], ALU.mult, ALU.mult,
                         toks[4 * hd + 3])
            self.banks.free(taken[hd][0], y)
            self.x.ready.append(self.split_into(xh[:, 2 + hd, :], xl[:, 2 + hd, :], r[:, hd, :], y))
        return self.x

    def rope(self, dst, src, cos, sin, rot, n, *after):
        b, bank, free = self.banks.take()
        t = self.mm(bank[:, 0:n], rot, src, True, True, *after, *free, signal=True)
        s = self.rope_i % 2
        self.rope_i += 1
        h = self.h
        t1 = self.tt(h["rt"][:, s, 0:n], bank[:, 0:n], sin, ALU.mult, t, *self.rt_free[s])
        self.banks.free(b, t1)
        t2 = self.tt(dst, src, cos, ALU.mult, t, *after, eng=self.pool)
        t3 = self.tt(dst, dst, h["rt"][:, s, 0:n], ALU.add, t1, t2)
        self.rt_free[s] = (t3,)
        return t3

    def odd_mixer(self, x):
        h, io = self.h, self.io
        w = io["odd_w_in"]
        q = self.place("df_q", MID, [P, 6, T])
        k = self.place("df_k", MID + 6144, [P, 6, 2 * T])
        v = self.place("df_v", MID + 18432, [P, 4, 768])
        z3 = self.place("df_z", MID + 30720, [P, 3, 2, T])
        cs = self.place("df_cs", MID + 36864, [P, 2, T])
        rot = self.place("df_rot", MID + 38912, [P, P])
        raw = self.place("df_raw", MID + 39424, [P, 4, T])
        h["rt"] = self.place("df_rt", MID + 43520, [P, 2, T])
        self.rt_free = [(), ()]
        y = self.place("df_y", MID + 45568, [P, 8, T])
        bar = self.barrier()
        ccs = self.load(cs[:, :, :], io["axial"], *bar)
        crot = self.load(rot[:, :], io["axial_rot"], *bar)

        lam = self.small("lambdas")
        lv = h["lam"]
        t = self.tt(lv[0:64, 0:2], lam[0:64, 0:2], lam[0:64, 2:4], ALU.mult)
        b, bank, free = self.banks.take()
        t = self.mm(bank[:, 0:2], h["ones"][0:64, :], lv[0:64, 0:2], True, True, t, *free, signal=True)
        t = self.act(lv[:, 2:4], bank[:, 0:2], ACT.Exp, t)
        self.banks.free(b, t)
        t = self.tt(lv[:, 4:5], lv[:, 3:4], lv[:, 2:3], ALU.subtract, t)
        lam_t = self.ts(lv[:, 5:6], lv[:, 4:5], -LAM_INIT, None, ALU.add, None, t)

        zt = []
        for c, done in enumerate(self.project_tiles(w, [0, 256, 512], x, T, self.ada_step)):
            for j, (b, bank, t) in enumerate(done):
                e = self.act(z3[:, c, j, :], bank[:, 0:T], ACT.Copy, t)
                self.banks.free(b, e)
                zt.append(e)
        qt, kt = [], []
        raw_free = [()] * 4
        i = 0
        for part, dst, toks in ((0, q, qt), (1, k, kt)):
            for c in range(3):
                u = self.w.take(w, 0, KC, 768 + 768 * part + 256 * c, 256)
                for j in range(2):
                    m = 2 * c + j
                    n = T * (1 + part)
                    b, bank, free = self.banks.take()
                    t = self.project(u, j * P, x, n, bank, free)
                    s = i % 4
                    i += 1
                    e = self.act(raw[:, s, :], bank[:, 0:T], ACT.Copy, t, *raw_free[s])
                    if part:
                        e2 = self.act(k[:, m, T:2 * T], bank[:, T:2 * T], ACT.Copy, t)
                        toks.append(e2)
                        self.banks.free(b, e2)
                    else:
                        self.banks.free(b, e)
                    e = self.rope(dst[:, m, 0:T], raw[:, s, :], cs[:, 0, :], cs[:, 1, :], rot[:, :], T, e, ccs, crot)
                    raw_free[s] = (e,)
                    toks.append(e)
                self.w.done(u, t)
                self.ada_step()
        vt = []
        for c in range(3):
            u = self.w.take(w, 0, KC, 2304 + 256 * c, 256)
            for tb in range(4):
                b, bank, free = self.banks.take()
                t = self.project_rows(u, 256, x, tb, bank, free)
                e = self.copy(v[:, tb, 256 * c:256 * c + 256], bank[:, 0:256], t)
                self.banks.free(b, e)
                vt.append(e)
            self.w.done(u, t)
            self.ada_step()

        conv_y = []
        for j in range(2):
            u_ = z3[:, 1, j, :]
            tap = [self.small("conv_w", 2 * a + j, 2 * a + j + 1) for a in range(3)]
            t = self.tt(u_, z3[:, 1, j, :], z3[:, 2, j, :], ALU.mult, *zt)
            t = self.ts(y[:, j, :], u_, tap[1], self.small("conv_b", j, j + 1), ALU.mult, ALU.add, t)
            t = self.stt(y[:, j, 1:T], u_[:, 0:T - 1], tap[0], y[:, j, 1:T], ALU.mult, ALU.add, t)
            t = self.stt(y[:, j, 0:T - 1], u_[:, 1:T], tap[2], y[:, j, 0:T - 1], ALU.mult, ALU.add, t)
            conv_y.append(self.tt(y[:, j, :], y[:, j, :], z3[:, 0, j, :], ALU.mult, t, *zt))
        bar = self.barrier()

        NS = 3
        e_ = self.place("df_e", XN, [P, NS, 2, 2 * T])
        aT = self.place("df_aT", XN + 12288, [P, NS, 4, P])
        sc = self.place("df_sc", XN + 12288 + 6144, [P, 12, 8])
        scale = HD ** -0.5
        sbank_b, sbank, sfree = self.banks.take()
        jobs = [(hd, qb) for hd in range(6) for qb in range(TB)]
        st = {}
        e_free = [()] * NS
        aT_free = [()] * NS
        obank = {}

        def scores(i):
            hd, qb = jobs[i]
            st[i] = []
            for s in range(2):
                b, bank, free = self.banks.take()
                t = self.mm(bank[:, :], q[64 * s:64 * s + 64, hd, qb * P:(qb + 1) * P], k[64 * s:64 * s + 64, hd, :],
                            True, True, *qt, *kt, *free, signal=True)
                c = sc[:, i, :]
                m = self.rmax(c[:, s:s + 1], bank[:, :], t)
                m = self.ts(c[:, 2 + s:3 + s], c[:, s:s + 1], scale, None, ALU.mult, None, m)
                e = self.act(e_[:, i % NS, s, :], bank[:, :], ACT.Exp, t, m, *e_free[i % NS], scale=scale,
                             bias=c[:, 2 + s:3 + s], accum=c[:, 4 + s:5 + s])
                self.banks.free(b, e)
                st[i].append(e)

        def combine(i):
            c = sc[:, i, :]
            a, e1 = e_[:, i % NS, 0, :], e_[:, i % NS, 1, :]
            t = self.recip(c[:, 6:8], c[:, 4:6], *st[i])
            t1 = self.tt(c[:, 7:8], c[:, 7:8], h["lam"][:, 5:6], ALU.mult, t, lam_t)
            t2 = self.ts(a, a, c[:, 6:7], None, ALU.mult, None, t, *st[i])
            t3 = self.stt(a, e1, c[:, 7:8], a, ALU.mult, ALU.add, t1, t2)
            st[i] = t3

        def turn(i):
            b, bank, free = self.banks.take()
            for kb in range(4):
                t = self.transpose(bank[:, kb * P:(kb + 1) * P], e_[:, i % NS, 0, kb * P:(kb + 1) * P], st[i], *free,
                                   signal=kb == 3)
            e_free[i % NS] = (t,)
            e = self.act(aT[:, i % NS, :, :], bank[:, :].rearrange("p (a b) -> p a b", a=4), ACT.Copy, t, *aT_free[i % NS])
            self.banks.free(b, e)
            st[i] = e

        def values(i):
            hd, qb = jobs[i]
            if qb == 0:
                obank[hd] = self.banks.take()
            b, bank, free = obank[hd]
            for kb in range(4):
                t = self.mm(bank[:, qb * P:(qb + 1) * P], v[:, kb, hd * P:(hd + 1) * P], aT[:, i % NS, kb, :], kb == 0,
                            kb == 3, st[i], *vt, *free, signal=kb == 3)
            aT_free[i % NS] = (t,)
            if qb == TB - 1:
                s = hd % 2
                y2 = self.act(h["sq2"][:, s, 0:T], bank[:, 0:T], ACT.Square, t, *self.sq2_free[s])
                y1 = self.copy(y[:, 2 + hd, :], bank[:, 0:T], t, y2)
                self.banks.free(b, y1)
                for tb in range(TB):
                    t = self.mm(sbank[:, hd * TB + tb:hd * TB + tb + 1], h["sq2"][:, s, tb * P:(tb + 1) * P],
                                h["ones"][:, 0:1], True, True, y2, *sfree, signal=True)
                self.sq2_free[s] = (t,)
                self.stat_t = t

        nj = len(jobs)
        for i in range(nj + 2):
            if i < nj:
                scores(i)
            if 0 <= i - 2 < nj:
                values(i - 2)
            if 0 <= i - 1 < nj:
                combine(i - 1)
                turn(i - 1)
        bar = self.barrier()
        xh, xl = self.x.hi, self.x.lo
        self.x.ready = [self.split_into(xh[:, c, 0:T], xl[:, c, 0:T], y[:, c, :]) for c in range(2)]
        outs, taken = [], []
        for hd in range(3):
            b, bank, free = self.banks.take()
            taken.append((b, bank))
            outs += [(bank, tb * P, free) for tb in range(4)]
        read, toks = self.columns_to_rows(sbank, self.stat_t, 12, DIFF_HEADS and 2 * HD, EPS_RMS, outs)
        self.banks.free(sbank_b, read)
        g = self.ts(h["lam"][:, 6:7], self.small("diff_norm"), 1.0 - LAM_INIT, None, ALU.mult, None)
        for hd in range(6):
            rows = taken[hd // 2][1][:, (hd % 2) * T:(hd % 2 + 1) * T]
            t = self.stt(y[:, 2 + hd, :], y[:, 2 + hd, :], h["lam"][:, 6:7], rows, ALU.mult, ALU.mult, g, toks[4 * (hd // 2) + 3])
            if hd % 2:
                self.banks.free(taken[hd // 2][0], t)
            self.x.ready.append(self.split_into(xh[:, 2 + hd, 0:T], xl[:, 2 + hd, 0:T], y[:, 2 + hd, :], t))
        return self.x

    def residual_update(self, first):
        hT = self.h["hT"]

        def update(k, bank, ready, half):
            if half == first:
                t = self.stt(hT[:, k, 0:T], hT[:, k, 0:T], ALPHA, bank[:, 0:T], ALU.mult, ALU.add, ready, *self.h_ready)
            else:
                t = self.tt(hT[:, k, 0:T], hT[:, k, 0:T], bank[:, 0:T], ALU.add, ready, self.h_tok[k])
            self.h_tok[k] = t
            if half == 1:
                acc = self.h["acc"]
                if k == 0:
                    self.sum_tok = self.pool.do(lambda e: e.tensor_copy(acc[:, 0:T], hT[:, 0, 0:T]), t, *self.acc_free)
                else:
                    self.sum_tok = self.tt(acc[:, 0:T], acc[:, 0:T], hT[:, k, 0:T], ALU.add, t, self.sum_tok, eng=self.pool)
            return t
        return update

    def layer_norm(self, which, split=True):
        h, hT = self.h, self.h["hT"]
        b, bank, free = self.banks.take()
        mt = self.mm(bank[:, 0:T], h["mean"][:, :], h["acc"][:, 0:T], True, True, self.sum_tok, *free, signal=True)
        self.acc_free = (mt,)
        d = []
        for k in range(KC):
            t = self.tt(hT[:, k, 0:T], hT[:, k, 0:T], bank[:, 0:T], ALU.subtract, mt, self.h_tok[k])
            self.square_sum(k, hT[:, k, 0:T], T, t)
            d.append(t)
        self.banks.free(b, t)
        rb, rows, rt = self.rms_rows(T, D, EPS_LN, self.sum_tok)
        x = self.x
        x.ready = []
        ready_h = []
        for k in range(KC):
            g = self.small("ln_gain", which * KC + k, which * KC + k + 1)
            bb = self.small("ln_bias", which * KC + k, which * KC + k + 1)
            s = k % 2
            t = self.stt(h["tmp"][:, s, 0:T], hT[:, k, 0:T], g, rows[:, 0:T], ALU.mult, ALU.mult, rt, d[k], *self.tmp_free[s])
            o = self.ts(hT[:, k, 0:T], h["tmp"][:, s, 0:T], bb, None, ALU.add, None, t, eng=self.pool)
            ready_h.append(o)
            if split:
                e = self.act(x.hi[:, k, 0:T], h["tmp"][:, s, 0:T], ACT.Identity, t, *self.x_free, bias=bb)
                f = self.stt(x.lo[:, k, 0:T], h["tmp"][:, s, 0:T], bb, x.hi[:, k, 0:T].bitcast(F32), ALU.add, ALU.subtract,
                             e, t, *self.x_free)
                self.tmp_free[s] = (o, e, f)
                x.ready.append([e, f])
            else:
                self.tmp_free[s] = (o,)
        self.banks.free(rb, t)
        self.h_ready = tuple(ready_h)
        return x

    def retention(self, x):
        h, io = self.h, self.io
        w = io["ret_w_in"]
        q = self.place("rt_q", MID, [P, 8, T])
        k = self.place("rt_k", MID + 8192, [P, 8, T])
        v = self.place("rt_v", MID + 16384, [P, TB, 2048])
        gate = self.place("rt_g", MID + 32768, [P, 16, T])
        cs = self.place("rt_cs", MID + 49152, [P, 2, 2, T])
        raw = self.place("rt_raw", MID + 53248, [P, 2, T])
        rot = self.place("rt_rot", MID + 55296, [P, P])
        h["rt"] = self.place("rt_rt", MID + 55808, [P, 2, T])
        self.rt_free = [(), ()]
        bar = self.barrier()
        ccs = self.load(cs[:, :, :, :], io["ret_rope"], *bar)
        crot = self.load(rot[:, :], io["pair_rot"], *bar)
        qk = []
        raw_free = [(), ()]
        for c, done in enumerate(self.project_tiles(w, [256 * c for c in range(8)], x, T)):
            for j, (b, bank, t) in enumerate(done):
                m = 2 * c + j
                e = self.act(raw[:, j, :], bank[:, 0:T], ACT.Copy, t, *raw_free[j])
                self.banks.free(b, e)
                dst = q[:, m, :] if m < 8 else k[:, m - 8, :]
                e = self.rope(dst, raw[:, j, :], cs[:, 0, m % 2, :], cs[:, 1, m % 2, :], rot[:, :], T, e, ccs, crot)
                raw_free[j] = (e,)
                qk.append(e)
        vt = []
        for c in range(8):
            u = self.w.take(w, 0, KC, 2048 + 256 * c, 256)
            for tb in range(TB):
                b, bank, free = self.banks.take()
                t = self.project_rows(u, 256, x, tb, bank, free)
                e = self.copy(v[:, tb, 256 * c:256 * c + 256], bank[:, 0:256], t)
                self.banks.free(b, e)
                vt.append(e)
            self.w.done(u, t)
        gt = []
        for c in range(8):
            u = self.w.take(w, 0, KC, 4096 + 256 * c, 256)
            for j in range(2):
                b, bank, free = self.banks.take()
                t = self.project(u, j * P, x, T, bank, free)
                e = self.act(gate[:, 2 * c + j, :], bank[:, 0:T], ACT.Silu, t)
                self.banks.free(b, e)
                gt.append(e)
            self.w.done(u, t)
        bar = self.barrier()
        dec = self.place("rt_dec", XN, [P, 4, 384])
        S = self.place("rt_S", XN + 6144, [P, 2, 384])
        yb = self.place("rt_y", XN + 9216, [P, 2, 4, T])
        sqr = self.place("rt_sq", XN + 17408, [P, 4, T])
        cdec = self.load(dec[:, :, :], io["decay"], *bar)
        s_free = [(), ()]
        y_free = [(), ()]
        sq_free = ()
        for hd in range(RET_HEADS):
            s = hd % 2
            b, bank, free = self.banks.take()
            for jb, (i0, i1, at) in enumerate(((0, T, 0), (P, T, T))):
                for c in range(2):
                    t = self.mm(bank[:, at:at + i1 - i0], k[:, 2 * hd + c, jb * P:(jb + 1) * P], q[:, 2 * hd + c, i0:i1],
                                c == 0, c == 1, *qk, *free, signal=c == 1)
            st = self.tt(S[:, s, :], bank[:, 0:384], dec[:, hd, :], ALU.mult, t, cdec, *s_free[s])
            self.banks.free(b, st)
            ys = []
            for c in range(4):
                e0 = hd * RET_DV + c * P
                b, bank, free = self.banks.take()
                self.mm(bank[:, 0:T], v[:, 0, e0:e0 + P], S[:, s, 0:T], True, False, st, *vt, *free, loose=True)
                t = self.mm(bank[:, P:T], v[:, 1, e0:e0 + P], S[:, s, T:384], False, True, loose=True, signal=True)
                e = self.act(yb[:, s, c, :], bank[:, 0:T], ACT.Copy, t, *y_free[s])
                self.banks.free(b, e)
                ys.append(e)
            s_free[s] = (t,)
            mb, mbank, mfree = self.banks.take()
            for c in range(4):
                t = self.mm(mbank[:, 0:T], h["ones"][:, :], yb[:, s, c, :], c == 0, c == 3, ys[c], *mfree, signal=c == 3)
            mu = self.act(h["tmp"][:, 0, 0:T], mbank[:, 0:T], ACT.Copy, t, *self.tmp_free[0], scale=1.0 / RET_DV)
            self.banks.free(mb, mu)
            sb_, sbank, sfree = self.banks.take()
            ds = []
            for c in range(4):
                d = self.tt(yb[:, s, c, :], yb[:, s, c, :], h["tmp"][:, 0, 0:T], ALU.subtract, mu, ys[c], t)
                e = self.act(sqr[:, c, :], yb[:, s, c, :], ACT.Square, d, *sq_free)
                ds.append((d, e))
            self.tmp_free[0] = (d,)
            for tb in range(TB):
                for c in range(4):
                    t = self.mm(sbank[:, tb:tb + 1], sqr[:, c, tb * P:(tb + 1) * P], h["ones"][:, 0:1], c == 0, c == 3,
                                ds[c][1], *sfree, signal=c == 3)
            sq_free = (t,)
            rb, rows, rfree = self.banks.take()
            read, toks = self.columns_to_rows(sbank, t, TB, RET_DV, EPS_LN, [(rows, tb * P, rfree) for tb in range(TB)])
            self.banks.free(sb_, read)
            for c in range(4):
                y = self.tt(yb[:, s, c, :], yb[:, s, c, :], rows[:, 0:T], ALU.mult, toks[-1], ds[c][0], ds[c][1])
                f = self.tt(gate[:, hd * 4 + c, :], gate[:, hd * 4 + c, :], yb[:, s, c, :], ALU.mult, y, *gt, eng=self.pool)
            y_free[s] = (f,)
            self.banks.free(rb, y)
        bar = self.barrier()
        r = Unit()
        r.hi = self.place("rt_hi", MID, [P, 16, T], F32R)
        r.lo = self.place("rt_lo", MID + 16384, [P, 16, T], F32R)
        r.ready = [self.split_into(r.hi[:, c, :], r.lo[:, c, :], gate[:, c, :]) for c in range(16)]
        return r

    def dilated(self, x):
        h, io = self.h, self.io
        w = io["attn_w_in"]
        NQ = ATT_GROUPS * 8
        q = self.place("at_q", MID, [P, NQ, T])
        k = self.place("at_k", MID + 24576, [P, NQ, T])
        v = self.place("at_v", MID + 49152, [P, TB, 3072])
        bar = self.barrier()
        qt = []
        for part, dst in ((0, q), (1, k)):
            for c, done in enumerate(self.project_tiles(w, [3072 * part + 256 * c for c in range(12)], x, T)):
                for j, (b, bank, t) in enumerate(done):
                    e = self.act(dst[:, 2 * c + j, :], bank[:, 0:T], ACT.Copy, t)
                    self.banks.free(b, e)
                    qt.append(e)
        vt = []
        for c in range(12):
            u = self.w.take(w, 0, KC, 6144 + 256 * c, 256)
            for tb in range(TB):
                b, bank, free = self.banks.take()
                t = self.project_rows(u, 256, x, tb, bank, free)
                e = self.copy(v[:, tb, 256 * c:256 * c + 256], bank[:, 0:256], t)
                self.banks.free(b, e)
                vt.append(e)
            self.w.done(u, t)
        bar = self.barrier()
        NB = 2
        bias = self.place("at_bias", XN, [P, NB, 3, T])
        e_ = self.place("at_e", XN + 6144, [P, 2, 3 * T + 3 * P])
        pT = self.place("at_pT", XN + 15360, [P, 9, P])
        o = self.place("at_o", XN + 19968, [P, TB, D])
        sc = self.place("at_sc", XN + 28160, [P, 16, 8])
        wide = self.place("at_wide", XN + 28672, [16, 2, 384])

        oh = self.place("at_onehot", XN, [32, 3, 384])
        mk = self.place("at_mask", XN + 6144, [16, 3, 384])
        coh = self.load(oh[:, :, :], io["onehot"], *bar)
        cmk = self.load(mk[:, :, :], io["dist_mask"], *bar)
        rel = self.small("rel_bias")
        toks = []
        stored = []
        for g in range(3):
            b, bank, free = self.banks.take()
            t = self.mm(bank[0:16, 0:384], rel[0:32, 16 * g:16 * g + 16], oh[:, g, :], True, True, coh, *free, signal=True)
            t = self.tt(wide[:, g % 2, :], bank[0:16, 0:384], mk[:, g, :], ALU.add, t, cmk, *(stored[g - 2:g - 1] if g >= 2 else ()))
            self.banks.free(b, t)
            stored.append(self.load(io["bias_rows"][g], wide[:, g % 2, :], t))
        nbar = self.barrier()
        bias_t = {}
        bias_free = [list(nbar)] * NB

        def fetch(hd):
            s = hd % NB
            src = self.io["bias_windows"](hd)
            bias_t[hd] = self.load(bias[:, s, :, :], src, *stored, *bias_free[s])

        fetch(0)
        fetch(1)
        scale = HD ** -0.5
        st = {}
        e_free = [(), ()]
        pT_free = ()

        def scores(hd):
            hs = slice(64 * (hd % 2), 64 * (hd % 2) + 64)
            s = hd % 2
            ch = [g * 8 + hd // 2 for g in range(3)]
            ba, bb, bc = (self.banks.take() for _ in range(3))
            for g in range(3):
                dst = ba[1][:, g * T:(g + 1) * T] if g < 2 else bb[1][:, 0:T]
                t = self.mm(dst, q[hs, ch[g], P:T], k[hs, ch[g], 0:T], True, True, *qt, *ba[2], *bb[2], signal=True)
            for g in range(3):
                t = self.mm(bc[1][:, g * P:(g + 1) * P], q[hs, ch[g], 0:P], k[hs, ch[g], 0:P], True, True, *bc[2], signal=True)
            E = e_[:, s, :]
            b_ = bias[:, s, :, ::-1]
            t1 = self.stt(E[:, 0:2 * T].rearrange("p (g c) -> p g c", g=2), ba[1][:, :].rearrange("p (g c) -> p g c", g=2),
                          scale, b_[:, 0:2, :], ALU.mult, ALU.add, t, bias_t[hd], *e_free[s])
            t2 = self.stt(E[:, 2 * T:3 * T], bb[1][:, 0:T], scale, b_[:, 2, :], ALU.mult, ALU.add, t, bias_t[hd])
            t3 = self.stt(E[:, 3 * T:].rearrange("p (g c) -> p g c", g=3), bc[1][:, 0:384].rearrange("p (g c) -> p g c", g=3),
                          scale, b_[:, :, P:T], ALU.mult, ALU.add, t, bias_t[hd])
            bias_free[s] = (t3,)
            for bk, tk in ((ba, t1), (bb, t2), (bc, t3)):
                self.banks.free(bk[0], tk)
            c = sc[:, hd, :]
            m1 = self.rmax(c[:, 1:2], E[:, 0:3 * T], t1, t2)
            m0 = self.rmax(c[:, 0:1], E[:, 3 * T:], t3)
            e1 = self.act(E[:, 0:3 * T], E[:, 0:3 * T], ACT.Exp, m1, bias=c[:, 1:2], accum=c[:, 3:4])
            e0 = self.act(E[:, 3 * T:], E[:, 3 * T:], ACT.Exp, m0, bias=c[:, 0:1], accum=c[:, 2:3])
            st[hd] = (e0, e1)
            if hd + 2 < ATT_HEADS:
                fetch(hd + 2)

        def turn(hd):
            s = hd % 2
            nonlocal pT_free
            c = sc[:, hd, :]
            st[hd, "r"] = self.recip(c[:, 4:6], c[:, 2:4], *st[hd])
            out = []
            for lo_, n_ in ((0, 4), (4, 4), (8, 1)):
                b, bank, free = self.banks.take()
                for i in range(n_):
                    t = self.transpose(bank[:, i * P:(i + 1) * P], e_[:, s, (lo_ + i) * P:(lo_ + i + 1) * P], *st[hd], *free,
                                       signal=i == n_ - 1)
                dst = pT[:, lo_:lo_ + n_, :]
                src = bank[:, 0:n_ * P].rearrange("p (a b) -> p a b", a=n_)
                if lo_ == 4:
                    e = self.copy(dst, src, t, *pT_free)
                else:
                    e = self.act(dst, src, ACT.Copy, t, *pT_free)
                self.banks.free(b, e)
                out.append(e)
            e_free[s] = (t,)
            st[hd] = out

        def values(hd):
            nonlocal pT_free
            c = sc[:, hd, :]
            b, bank, free = self.banks.take()
            vcol = lambda g: slice(g * D + hd * HD, g * D + hd * HD + HD)
            for g in range(3):
                for kb in range(2):
                    t = self.mm(bank[:, HD:2 * HD], pT[:, 2 * g + kb, :], v[:, kb, vcol(g)], g == 0 and kb == 0,
                                g == 2 and kb == 1, *st[hd], *vt, *free, signal=False)
            for g in range(3):
                t = self.mm(bank[:, 0:HD], pT[:, 6 + g, :], v[:, 0, vcol(g)], g == 0, g == 2, signal=g == 2)
            pT_free = (t,)
            d = self.ts(o[:, 0, hd * HD:(hd + 1) * HD], bank[:, 0:HD], c[:, 4:5], None, ALU.mult, None, t, st[hd, "r"])
            d = self.ts(o[:, 1, hd * HD:(hd + 1) * HD], bank[:, HD:2 * HD], c[:, 5:6], None, ALU.mult, None, t, st[hd, "r"])
            self.banks.free(b, d)

        for i in range(ATT_HEADS + 1):
            if i < ATT_HEADS:
                scores(i)
            if i >= 1:
                turn(i - 1)
                values(i - 1)
        bar = self.barrier()
        r = Unit()
        r.hi = self.place("at_hi", MID, [P, 8, T], F32R)
        r.lo = self.place("at_lo", MID + 8192, [P, 8, T], F32R)
        oT = self.place("at_oT", MID + 16384, [P, 8, T])
        r.ready = []
        for c in range(KC):
            b, bank, free = self.banks.take()
            for tb in range(TB):
                t = self.transpose(bank[:, tb * P:(tb + 1) * P], o[:, tb, c * P:(c + 1) * P], *free, signal=tb == 1)
            e = self.copy(oT[:, c, :], bank[:, 0:T], t)
            self.banks.free(b, e)
            r.ready.append(self.split_into(r.hi[:, c, :], r.lo[:, c, :], oT[:, c, :], e))
        return r

    def run(self, stop=99):
        h, io = self.h, self.io
        hT = h["hT"]
        self.acc_free = self.coef_free = self.gate_free = self.rs_free = self.x_free = ()
        self.sq_free = [(), ()]
        self.sq2_free = [(), ()]
        self.tmp_free = [(), ()]
        self.sg_free = [(), ()]
        self.diag_free = [(), (), (), ()]
        self.ada_free = [(), ()]
        self.ada_open = None
        self.h_tok = [None] * KC
        self.rope_i = 0
        self.x = Unit()
        self.x.hi = self.place("x_hi", XN, [P, KC, 2 * T], F32R)
        self.x.lo = self.place("x_lo", XN + 16384, [P, KC, 2 * T], F32R)

        self.small_ready = self.load(h["small"][:, :], io["small"])
        hl = self.load(hT[:, :, :], io["hT"])
        ci = self.load(h["ident"][:, :], io["ident"])
        o1 = self.pool.do(lambda e: e.memset(h["ones"][:, :], 1.0))
        o2 = self.pool.do(lambda e: e.memset(h["mean"][:, :], 1.0 / D))
        o3 = self.pool.do(lambda e: e.memset(h["eps"][:, 0:1], EPS_RMS))
        o4 = self.pool.do(lambda e: e.memset(h["eps"][:, 1:2], EPS_LN))
        o5 = self.pool.do(lambda e: e.memset(h["one"][:, :], 1.0))
        z = self.pool.do(lambda e: e.memset(h["cs"][:, :, :], 0.0))
        self.fold_ready = self.load(h["fold"][:, :], io["fold"])
        self.cs_ready = self.act(h["cs"][:, :, 0:2], self.small("cond").rearrange("p (k c) -> p k c", c=2), ACT.Silu,
                                 self.small_ready, z)
        self.h_ready = (hl,)
        for e in (self.pe, self.act_e, self.dve):
            e.first = [o5, ci, self.small_ready]
        for k in range(KC):
            self.square_sum(k, hT[:, k, :], 2 * T, hl)

        def layer(l, n2):
            x = self.prenorm(hT, 2 * T, l, "norm_ffn1", 0, self.h_ready, self.sum_tok)
            gate, upd = self.gated_update(l, 2, 0.5, 2 * T)
            self.ffn(io["ffn1_w_in"][l], io["ffn1_w_out"][l], x, 2 * T, upd, between=self.ada_step,
                     before_down=lambda half: gate() if half == 0 else None)
            self.h_ready = tuple(self.h_tok)
            if stop <= 10 * l + 1:
                return True
            x = self.prenorm(hT, 2 * T, l, "norm_mix", 3, self.h_ready, self.sum_tok)
            x = (self.even_mixer if l == 0 else self.odd_mixer)(x)
            gate, upd = self.gated_update(l, 5, 1.0, n2)
            gate()
            self.mix_out(io["mix_w_out"][l], x, n2, upd)
            self.h_ready = tuple(self.h_tok)
            if stop <= 10 * l + 2:
                return True
            x = self.prenorm(hT, n2, l, "norm_ffn2", 6, self.h_ready, self.sum_tok)
            gate, upd = self.gated_update(l, 8, 0.5, n2)
            self.ffn(io["ffn2_w_in"][l], io["ffn2_w_out"][l], x, n2, upd, between=self.ada_step,
                     before_down=lambda half: gate() if half == 0 else None)
            self.h_ready = tuple(self.h_tok)
            return stop <= 10 * l + 3

        if layer(0, 2 * T) or layer(1, T):
            return
        rb, rows, rt = self.rms_rows(T, D, EPS_RMS, self.sum_tok)
        x = self.x
        x.ready = []
        rd = []
        for k in range(KC):
            t = self.stt(hT[:, k, 0:T], hT[:, k, 0:T], self.small("final_norm", k, k + 1), rows[:, 0:T], ALU.mult, ALU.mult,
                         rt, *self.h_ready)
            x.ready.append(self.split_into(x.hi[:, k, 0:T], x.lo[:, k, 0:T], hT[:, k, 0:T], t, free=self.x_free))
            rd.append(t)
            rd += x.ready[-1]
        self.banks.free(rb, t)
        self.h_ready = tuple(rd)
        for l in range(2):
            if stop <= 21 + 10 * l:
                return
            upd = self.residual_update(1)
            r = self.retention(x) if l == 0 else self.dilated(x)
            save = self.x_free
            self.mix_out(io["ret_w_out" if l == 0 else "attn_w_out"], r, T, upd, kn=16 if l == 0 else KC)
            self.barrier()
            x = self.layer_norm(2 * l)
            upd = self.residual_update(0)
            self.ffn(io["ffn_w_up"][l], io["ffn_w_down"][l], x, T, upd)
            x = self.layer_norm(2 * l + 1, split=l == 0)

    def finish(self):
        t = [e.last() for e in (self.pe, self.act_e, self.dve, self.pool)]
        sem = self.h["out_sem"]
        hT, out = self.h["hT"], self.io["out"]
        self.sync.do(lambda e: e.dma_start(out, hT[:, :, 0:T]).then_inc(sem, 16), *t, signal=False)
        self.sync.do(lambda e: e.wait_ge(sem, 16), signal=False)


def build(nc, io, stop=99):
    with ExitStack() as ctx:
        def sb(name, shape, dt=F32):
            return ctx.enter_context(nc.sbuf_tensor(name, shape, dt))

        def sem(name):
            return ctx.enter_context(nc.semaphore(name))

        h = {
            "hT": sb("hT", [P, KC, 2 * T]), "small": sb("small", [P, SMALL_N]), "ident": sb("ident", [P, P]),
            "ones": sb("ones", [P, P]), "mean": sb("mean", [P, P]), "eps": sb("eps", [P, 2]), "one": sb("one", [P, 1]),
            "cs": sb("cs", [P, KC, 32]), "fold": sb("fold", [P, 2]), "mod": sb("mod", [P, 2 * MODS * KC, 2]), "coef": sb("coef", [P, KC, 2]),
            "gate": sb("gate", [P, KC, 2]), "rs": sb("rs", [P, 24]), "rs2": sb("rs2", [P, 24]),
            "diag": sb("diag", [P, 4, P]), "lam": sb("lam", [P, 8]),
        }
        raw = sb("w_raw", [P, NRAW, UNIT])
        whi = sb("w_hi", [P, NSPLIT, UNIT], F32R)
        wlo = sb("w_lo", [P, NSPLIT, UNIT], F32R)
        h["work"] = (nc.sbuf_base + 31) // 32 * 32
        assert h["work"] + WORK <= nc.sbuf_top
        h["placed"] = {}
        h["psum"] = [ctx.enter_context(nc.psum_tensor(f"bank{i}", [P, 512], F32)) for i in range(8)]
        h["load_sems"] = [sem(f"s_load{i}") for i in range(48)]
        h["out_sem"] = sem("s_out")
        at = TEMPS

        def place(name, at, shape):
            return nc.alloc_sbuf_tensor_at(name, shape, F32, offset=h["work"] + at)
        h["acc"] = place("acc", at, [P, 2 * T])
        h["sq"] = place("sq", at + 2048, [P, 2, 2 * T])
        h["tmp"] = place("tmp", at + 6144, [P, 2, 2 * T])
        h["sg"] = place("sg", at + 10240, [P, 2, 2 * T])
        h["sq2"] = h["sg"]
        h["ada_rows"] = place("ada_rows", at + 14336, [P, 2, 256])
        sems = {n: sem(f"s_{n}") for n in ("pe", "act", "dve", "pool")}
        raw_sems = [sem(f"s_raw{i}") for i in range(NRAW)]

        def engines():
            return [Engine(sems[n]) for n in ("pe", "act", "dve", "pool")] + [Engine(None)]

        rec = Recorder(whi, wlo, raw)
        Program(nc, io, h, engines(), rec).run(stop)
        eng = engines()
        stream = Weights(rec.plan, whi, wlo, raw, eng[4], raw_sems, eng[1], eng[2], eng[3])
        prog = Program(nc, io, h, eng, stream)
        prog.run(stop)
        prog.finish()

        block = ctx.enter_context(nc.Block())

        @block.sync
        def _(e):
            eng[4].emit(e)

        @block.tensor
        def _(e):
            eng[0].emit(e)

        @block.scalar
        def _(e):
            eng[1].emit(e)

        @block.vector
        def _(e):
            eng[2].emit(e)

        @block.gpsimd
        def _(e):
            eng[3].emit(e)


def shape_constants():
    f = np.float32
    out = {"ident": np.eye(P, dtype=f)}
    out["fold"] = np.tile(np.eye(32, 2), (4, 1))
    t = np.arange(T)
    ang = 2 * np.pi * np.outer(t, t) / T
    out["fourier_time"] = np.stack([np.concatenate([np.cos(ang), np.sin(ang)], 1)[b * P:(b + 1) * P] for b in range(TB)], 1)
    d = np.arange(HD)
    ang = 2 * np.pi * np.outer(d, d) / HD
    norm = 1.0 / math.sqrt(T * HD)
    two = np.eye(2)
    out["fourier_dim"] = np.stack([np.kron(two, np.cos(ang)) * norm, -np.kron(two, np.sin(ang)) * norm], 1)
    seg = np.ones((P, 2 * T))
    seg[:, ::GLA_CHUNK] = 0
    out["segments"] = seg
    big = 3.0e38
    j, i = np.meshgrid(np.arange(P), np.arange(P), indexing="ij")
    same = j // GLA_CHUNK == i // GLA_CHUNK
    lim = []
    for keep in (same & (j <= i), same & (j >= i)):
        lim += [np.where(keep, big, 0.0), np.where(keep, -big, 0.0)]
    out["limits"] = np.stack(lim, 1)[:, :, None, :]
    n = 16
    inv = (np.float32(10000.0) ** (-np.arange(n, dtype=f) / f(n))).astype(f)
    tok = np.arange(T)
    row, col = (tok // 64).astype(f), (tok % 64).astype(f)
    ang = np.concatenate([np.outer(inv, row)] * 2 + [np.outer(inv, col)] * 2, 0).astype(f)
    ang = np.concatenate([ang, ang], 0)
    out["axial"] = np.stack([np.cos(ang), np.sin(ang)], 1)
    rot = np.zeros((P, P))
    for m in range(P):
        if m % 32 < 16:
            rot[m + 16, m] = -1.0
        else:
            rot[m - 16, m] = 1.0
    out["axial_rot"] = rot
    rot = np.zeros((P, P))
    for m in range(0, P, 2):
        rot[m + 1, m] = -1.0
        rot[m, m + 1] = 1.0
    out["pair_rot"] = rot
    inv = (f(1.0) / (f(10000.0) ** np.linspace(0.0, 1.0, P, dtype=f))).astype(f)
    ang = (np.arange(T, dtype=f)[None, :] * np.repeat(inv, 2)[:, None]).astype(f).reshape(2, P, T)
    out["ret_rope"] = np.stack([np.cos(ang), np.sin(ang)], 0).transpose(2, 0, 1, 3)
    dec = []
    for hd in range(RET_HEADS):
        g = math.log(1.0 - 2.0 ** (-5.0 - hd))
        jj, ii = np.arange(P)[:, None], np.arange(T)[None, :]
        full = [np.where(ii >= jj + b * P, np.exp(np.maximum(ii - jj - b * P, 0) * g), 0.0) for b in range(2)]
        dec.append(np.concatenate([full[0], full[1][:, P:]], 1) * RET_DK ** -0.5)
    out["decay"] = np.stack(dec, 1)
    delta = np.arange(384) - 127
    onehot, mask = np.zeros((NUM_BUCKETS, 3, 384)), np.zeros((16, 3, 384))
    for g, (window, dil) in enumerate(DILATED):
        ok = (delta >= 0) & (delta <= window) & (delta % dil == 0)
        dist = np.maximum(delta, 0)
        exact = NUM_BUCKETS // 2
        large = exact + (np.log(np.maximum(dist, 1).astype(f) / f(exact)) / f(math.log(MAX_DISTANCE / exact))
                         * f(NUM_BUCKETS - exact)).astype(np.int32)
        bucket = np.where(dist < exact, dist, np.minimum(large, NUM_BUCKETS - 1))
        onehot[bucket[ok], g, np.arange(384)[ok]] = 1.0
        mask[:, g, ~ok] = NEG
    out["onehot"], out["dist_mask"] = onehot, mask
    return {k: np.ascontiguousarray(v, dtype=f) for k, v in out.items()}


def chunks(v):
    return v.reshape(-1, P).T


def tall(v):
    return np.concatenate([v, np.zeros((P - v.shape[0], v.shape[1]), v.dtype)], 0)


WEIGHTS = ["ada_w", "ffn1_w_in", "ffn1_w_out", "ffn2_w_in", "ffn2_w_out", "mix_w_out"]
PLAIN = {"even_w_in": "even_w_in", "odd_w_in": "odd_w_in", "ret_w_in": "ret_w_in_2", "ret_w_out": "ret_w_out_2",
         "attn_w_in": "attn_w_in_2", "attn_w_out": "attn_w_out_2"}
PAIRS = {"ffn_w_up": "ffn_w_up_2", "ffn_w_down": "ffn_w_down_2"}


def kernel(stop=99, **inp):
    import concourse.bacc as bacc
    from concourse.bass_utils import run_bass_kernel_spmd

    a = {k: np.asarray(v) for k, v in inp.items()}
    small = {
        "cond": np.stack([chunks(a["c"][0]), chunks(a["c_ctx"])], 2).reshape(P, -1),
        "ada_b": chunks(a["ada_b"]), "norm_ffn1": chunks(a["norm_ffn1"]), "norm_mix": chunks(a["norm_mix"]),
        "norm_ffn2": chunks(a["norm_ffn2"]), "final_norm": chunks(a["final_norm"]), "gate_b": chunks(a["gla_gate_b"]),
        "gla_norm": chunks(a["gla_norm"]), "conv_w": chunks(a["conv_w"]), "conv_b": chunks(a["conv_b"]),
        "lambdas": tall(np.concatenate([a["lambda_q1"], a["lambda_q2"], a["lambda_k1"], a["lambda_k2"]], 0).T),
        "diff_norm": chunks(a["diff_norm"]), "ln_gain": chunks(a["ln_gain_2"]), "ln_bias": chunks(a["ln_bias_2"]),
        "rel_bias": tall(a["rel_bias_2"].T),
    }
    arrays = {"small": np.ascontiguousarray(np.concatenate([small[n] for n, _ in SMALL], 1))}
    both = np.concatenate([a["x"][0], a["ctx"][0]], 0)
    arrays["hT"] = np.ascontiguousarray(both.reshape(2 * T, KC, P).transpose(2, 1, 0))
    arrays["gate_w"] = np.ascontiguousarray(a["gla_gate_w"][0])
    for n in WEIGHTS:
        arrays[n] = a[n]
    for n, src in PLAIN.items():
        arrays[n] = a[src][0]
    for n, src in PAIRS.items():
        arrays[n] = a[src]
    arrays.update(shape_constants())

    nc = bacc.Bacc("TRN2", target_bir_lowering=False, num_devices=1)
    io = {n: nc.dram_tensor("in_" + n, v.shape, F32, kind="ExternalInput").ap() for n, v in arrays.items()}
    out = nc.dram_tensor("out_T", [P, KC, T], F32, kind="ExternalOutput")
    io["out"] = out.ap()
    rows = nc.dram_tensor("bias_rows", [ATT_GROUPS, ATT_HEADS, 384], F32, kind="Internal")
    io["bias_rows"] = rows.ap()
    io["bias_windows"] = lambda hd: bass.AP(tensor=rows, offset=hd * 384, ap=[[1, P], [ATT_HEADS * 384, 3], [1, T]])
    build(nc, io, stop)
    r = run_bass_kernel_spmd(nc, [{"in_" + n: v for n, v in arrays.items()}], core_ids=[0])
    got = r.results[0]["out_T"]
    return np.ascontiguousarray(got.transpose(2, 1, 0)).reshape(1, T, D)
```

```python
import math
from contextlib import ExitStack

import numpy as np
import concourse.bass as bass
from concourse import mybir

P = 128
F32 = mybir.dt.float32
F32R = mybir.dt.float32r
ALU = mybir.AluOpType
ACT = mybir.ActivationFunctionType
AX = mybir.AxisListType.X

D = 1024
KC = D // P
T = 256
TB = T // P
FFN = 2816
FC = FFN // P
HALVES = ((0, 12), (12, 10))
EPS_RMS = 1e-6
EPS_LN = 1e-5
MODS = 9
GLA_HEADS, GLA_DK, GLA_DV, GLA_CHUNK, GLA_TAU = 6, 64, 128, 64, 16.0
NCH = 2 * T // GLA_CHUNK
DIFF_HEADS, HD = 6, 64
LAM_INIT = 0.8 - 0.6 * math.exp(-0.3)
RET_HEADS, RET_DK, RET_DV = 4, 256, 512
ATT_HEADS, ATT_GROUPS = 16, 3
DILATED = ((128, 1), (512, 4), (2048, 16))
NUM_BUCKETS, MAX_DISTANCE = 32, 2048
ALPHA = 4 ** 0.25
NEG = -1e30

SMALL = [("cond", 2 * KC), ("ada_b", 2 * MODS * KC), ("norm_ffn1", 2 * KC), ("norm_mix", 2 * KC),
         ("norm_ffn2", 2 * KC), ("final_norm", KC), ("gate_b", 6), ("gla_norm", 1), ("conv_w", 6),
         ("conv_b", 2), ("lambdas", 4), ("diff_norm", 1), ("ln_gain", 4 * KC), ("ln_bias", 4 * KC),
         ("rel_bias", 48)]
SMALL_AT = {}
_at = 0
for _name, _n in SMALL:
    SMALL_AT[_name] = (_at, _at + _n)
    _at += _n
SMALL_N = _at

XN, MID, TEMPS, WORK = 0, 32768, 90496, 106880
UNIT = 2048
NRAW, NSPLIT = 4, 3


class Engine:

    def __init__(self, sem):
        self.sem, self.count, self.steps, self.first = sem, 0, [], []

    def do(self, op, *after, signal=True):
        waits = [t for t in (*self.first, *after) if t is not None]
        self.first = []
        self.steps.append([waits, op, signal])
        if signal:
            self.count += 1
            return (self.sem, self.count)
        return None

    def last(self):
        if not self.steps:
            return None
        if not self.steps[-1][2]:
            self.steps[-1][2] = True
            self.count += 1
        return (self.sem, self.count)

    def emit(self, eng):
        seen = {}
        for waits, op, signal in self.steps:
            need = {}
            for sem, value in waits:
                if value > max(seen.get(sem.name, 0), need.get(sem.name, (None, 0))[1]):
                    need[sem.name] = (sem, value)
            for name, (sem, value) in need.items():
                eng.wait_ge(sem, value)
                seen[name] = value
            ins = op(eng)
            if signal:
                ins.then_inc(self.sem, 1)


class Banks:

    def __init__(self, tiles):
        self.tiles, self.order, self.readers = tiles, list(range(len(tiles))), [()] * len(tiles)

    def take(self):
        b = self.order.pop(0)
        return b, self.tiles[b], self.readers[b]

    def free(self, b, *readers):
        self.readers[b] = readers
        self.order.append(b)


class Unit:
    pass


class Recorder:

    def __init__(self, hi, lo, raw):
        self.plan, self.tiles = [], (hi, lo, raw)

    def take(self, w, k0, kn, c0, cn, split=True):
        self.plan.append((w, k0, kn, c0, cn, split))
        u = Unit()
        u.hi, u.lo, u.raw = (t[:, 0, 0:kn * cn].rearrange("p (k c) -> p k c", k=kn) for t in self.tiles)
        u.ready = ()
        return u

    def done(self, unit, token):
        pass

    def pump(self):
        pass


class Weights:

    def __init__(self, plan, hi, lo, raw, sync, sems, act, dve, pool):
        self.plan, self.hi, self.lo, self.raw = plan, hi, lo, raw
        self.sync, self.sems, self.act, self.dve, self.pool = sync, sems, act, dve, pool
        self.loaded = self.split = self.taken = 0
        self.raw_free = [()] * NRAW
        self.split_free = [()] * NSPLIT
        self.split_slot = 0
        self.units = []

    def load_tile(self):
        i = self.loaded
        w, k0, kn, c0, cn, split = self.plan[i]
        slot = i % NRAW
        u = Unit()
        u.index, u.slot, u.is_split = i, slot, split
        u.raw = self.raw[:, slot, 0:kn * cn].rearrange("p (k c) -> p k c", k=kn)
        src = w[k0 * P:(k0 + kn) * P, c0:c0 + cn].rearrange("(k p) c -> p k c", p=P)
        self.sync.do(lambda e: e.dma_start(u.raw, src).then_inc(self.sems[slot], 16), *self.raw_free[slot], signal=False)
        u.loaded = (self.sems[slot], 16 * (i // NRAW + 1))
        u.ready = (u.loaded,)
        self.raw_free[slot] = None
        self.units.append(u)
        self.loaded += 1

    def split_tile(self, u):
        s = self.split_slot
        _, k0, kn, c0, cn, _ = self.plan[u.index]
        n = kn * cn
        raw, hi, lo = self.raw[:, u.slot, 0:n], self.hi[:, s, 0:n], self.lo[:, s, 0:n]
        u.hi = hi.rearrange("p (k c) -> p k c", k=kn)
        u.lo = lo.rearrange("p (k c) -> p k c", k=kn)
        a = self.act.do(lambda e: e.activation(hi, raw, ACT.Copy), u.loaded, *self.split_free[s])
        b = self.dve.do(lambda e: e.tensor_tensor(lo, raw, hi.bitcast(F32), ALU.subtract), a, u.loaded,
                        *self.split_free[s])
        u.ready = (a, b)
        self.raw_free[u.slot] = (a, b)
        self.split_free[s] = None
        u.split_slot = s
        self.split_slot = (s + 1) % NSPLIT
        self.split += 1

    def pump(self, splits=True):
        moved = True
        while moved:
            moved = False
            if self.loaded < len(self.plan) and self.raw_free[self.loaded % NRAW] is not None:
                self.load_tile()
                moved = True
            if self.split < self.loaded:
                u = self.units[self.split]
                if u.is_split and not splits:
                    continue
                if not u.is_split:
                    self.split += 1
                    moved = True
                elif self.split_free[self.split_slot] is not None:
                    self.split_tile(u)
                    moved = True

    def take(self, w, k0, kn, c0, cn, split=True):
        self.pump(splits=split)
        u = self.units[self.taken]
        assert self.taken < self.split and self.plan[self.taken][1:] == (k0, kn, c0, cn, split)
        self.taken += 1
        return u

    def done(self, u, token):
        if u.is_split:
            self.split_free[u.split_slot] = (token,)
        else:
            self.raw_free[u.slot] = (token,)


class Program:
    def __init__(self, nc, io, handles, engines, stream):
        self.nc, self.io, self.h = nc, io, handles
        self.pe, self.act_e, self.dve, self.pool, self.sync = engines
        self.w = stream
        self.banks = Banks(handles["psum"])
        self.ada_next = 0
        self.loads = 0
        self.mod_ready = {}

    def mm(self, out, lhsT, rhs, start, stop, *after, signal=False, loose=False):
        return self.pe.do(lambda e: e.matmul(out, lhsT, rhs, start=start, stop=stop,
                                             skip_group_check=loose), *after, signal=signal)

    def transpose(self, out, in_, *after, signal=False):
        ident = self.h["ident"]
        return self.pe.do(lambda e: e.transpose(out, in_, ident[:, :]), *after, signal=signal)

    def act(self, out, in_, func, *after, scale=1.0, bias=0.0, accum=None):
        if accum is None:
            return self.act_e.do(lambda e: e.activation(out, in_, func, bias=bias, scale=scale), *after)
        return self.act_e.do(lambda e: e.activation(out, in_, func, bias=bias, scale=scale,
                                                    accum_out=accum), *after)

    def tt(self, out, a, b, op, *after, eng=None):
        return (eng or self.dve).do(lambda e: e.tensor_tensor(out, a, b, op), *after)

    def ts(self, out, a, s1, s2, op0, op1, *after, eng=None):
        if s2 is None:
            return (eng or self.dve).do(lambda e: e.tensor_scalar(out, a, s1, None, op0), *after)
        return (eng or self.dve).do(lambda e: e.tensor_scalar(out, a, s1, s2, op0, op1), *after)

    def stt(self, out, a, s, b, op0, op1, *after):
        return self.dve.do(lambda e: e.scalar_tensor_tensor(out, a, s, b, op0, op1), *after)

    def scan(self, out, keep, a, *after):
        return self.dve.do(lambda e: e.tensor_tensor_scan(out, keep, a, 0.0, ALU.mult, ALU.add), *after)

    def recip(self, out, a, *after):
        return self.dve.do(lambda e: e.reciprocal(out, a), *after)

    def rmax(self, out, a, *after):
        return self.dve.do(lambda e: e.tensor_reduce(out, a, AX, ALU.max, negate=True), *after)

    def copy(self, out, a, *after):
        return self.dve.do(lambda e: e.tensor_copy(out, a), *after)

    def load(self, dst, src, *after):
        sem = self.h["load_sems"][self.loads]
        self.loads += 1
        self.sync.do(lambda e: e.dma_start(dst, src).then_inc(sem, 16), *after, signal=False)
        return (sem, 16)

    def place(self, name, at, shape, dtype=F32):
        key = (name, at)
        if key not in self.h["placed"]:
            self.h["placed"][key] = self.nc.alloc_sbuf_tensor_at(name, shape, dtype, offset=self.h["work"] + at)
        return self.h["placed"][key]

    def barrier(self):
        tokens = [e.last() for e in (self.pe, self.act_e, self.dve, self.pool)]
        for e in (self.pe, self.act_e, self.dve, self.pool):
            e.first = list(tokens)
        return tokens

    def small(self, name, a=0, b=None):
        s, e = SMALL_AT[name]
        return self.h["small"][:, s + a:(e if b is None else s + b)]

    def product3(self, out, a_hi, a_lo, b_hi, b_lo, start, stop, *after, signal=False):
        self.mm(out, a_hi, b_hi, start, False, *after)
        self.mm(out, a_hi, b_lo, False, False)
        return self.mm(out, a_lo, b_hi, False, stop, signal=signal)

    def project(self, u, c, x, n, bank, after, ks=range(KC), k0=0, start=True, stop=True, cols=0):
        ks = list(ks)
        for i, k in enumerate(ks):
            t = self.product3(bank[:, 0:n], u.hi[:, k - k0, c:c + P], u.lo[:, k - k0, c:c + P],
                              x.hi[:, k, cols:cols + n], x.lo[:, k, cols:cols + n],
                              start and i == 0, stop and i == len(ks) - 1,
                              *u.ready, *x.ready[k], *(after if i == 0 else ()), signal=i == len(ks) - 1)
        return t

    def project_first(self, units, x, n, **kw):
        jobs = [(u, c, *self.banks.take()) for u in units for c in (0, P)]
        for k in range(KC):
            out = []
            for u, c, b, bank, free in jobs:
                t = self.product3(bank[:, 0:n], u.hi[:, k, c:c + P], u.lo[:, k, c:c + P], x.hi[:, k, 0:n], x.lo[:, k, 0:n],
                                  k == 0, k == KC - 1, *u.ready, *x.ready[k], *free, signal=k == KC - 1)
                out.append((b, bank, t))
        return out

    def project_tiles(self, w, cols, x, n, between=lambda: None):
        for i in range(0, len(cols), 2):
            pair = cols[i:i + 2]
            if i == 0 and len(pair) == 2:
                us = [self.w.take(w, 0, KC, c, 256) for c in pair]
                done = self.project_first(us, x, n)
                for q, u in enumerate(us):
                    self.w.done(u, done[2 * q + 1][2])
                    yield done[2 * q:2 * q + 2]
                between()
            else:
                for c in pair:
                    u = self.w.take(w, 0, KC, c, 256)
                    done = []
                    for q in range(2):
                        b, bank, free = self.banks.take()
                        done.append((b, bank, self.project(u, q * P, x, n, bank, free)))
                    self.w.done(u, done[1][2])
                    yield done
                    between()

    def project_rows(self, u, cn, x, tb, bank, after):
        for k in range(KC):
            t = self.product3(bank[:, 0:cn], x.hi[:, k, tb * P:(tb + 1) * P], x.lo[:, k, tb * P:(tb + 1) * P],
                              u.hi[:, k, 0:cn], u.lo[:, k, 0:cn], k == 0, k == KC - 1,
                              *u.ready, *x.ready[k], *(after if k == 0 else ()), signal=k == KC - 1)
        return t

    def ada_step(self):
        if self.ada_next >= 2 * MODS * 4:
            self.ada_finish()
            return
        h = self.h
        i = self.ada_next
        self.ada_next += 1
        layer, c = divmod(i, MODS * 4)
        u = self.w.take(self.io["ada_w"][layer], 0, KC, c * 256, 256, split=False)
        b, bank, free = self.banks.take()
        for k in range(KC):
            g = k % 4
            t = self.mm(bank[32 * g:32 * g + 32, 0:256], h["cs"][:, k, :], u.raw[:, k, :], k < 4, k >= 4,
                        *u.ready, self.cs_ready, *free, signal=k >= 4)
        self.w.done(u, t)
        s = i % 2
        e = self.act(h["ada_rows"][:, s, :], bank[:, 0:256], ACT.Copy, t, *self.ada_free[s])
        self.banks.free(b, e)
        self.ada_finish()
        self.ada_open = (i, s, e, layer * MODS * KC + 2 * c)

    def ada_finish(self):
        if self.ada_open is None:
            return
        h = self.h
        i, s, e, at = self.ada_open
        self.ada_open = None
        b, bank, free = self.banks.take()
        for j in range(2):
            t = self.mm(bank[:, 2 * j:2 * j + 2], h["ada_rows"][:, s, j * P:(j + 1) * P], h["fold"][:, :], True, True,
                        e, self.fold_ready, *free, signal=j == 1)
        self.ada_free[s] = (t,)
        bias = self.small("ada_b", at, at + 2).rearrange("p (j o) -> p j o", o=1).broadcast_to([P, 2, 2])
        e = self.tt(h["mod"][:, at:at + 2, :], bank[:, 0:4].rearrange("p (j c) -> p j c", j=2), bias,
                    ALU.add, t, self.small_ready)
        self.mod_ready[i] = e
        self.banks.free(b, e)

    def ada_until(self, layer, part):
        last = (layer * MODS + part + 1) * 4
        while self.ada_next < last:
            self.ada_step()
        if last - 1 not in self.mod_ready:
            self.ada_finish()
        return self.mod_ready[last - 1]

    def mod(self, layer, part):
        at = (layer * MODS + part) * KC
        return self.h["mod"][:, at:at + KC, :]

    def square_sum(self, k, src, n, *after):
        h = self.h
        if k == 0:
            self.sum_tok = self.act(h["acc"][:, 0:n], src, ACT.Square, *after, *self.acc_free)
            return
        s = k % 2
        t = self.act(h["sq"][:, s, 0:n], src, ACT.Square, *after, *self.sq_free[s])
        self.sum_tok = self.tt(h["acc"][:, 0:n], h["acc"][:, 0:n], h["sq"][:, s, 0:n], ALU.add, t, self.sum_tok,
                               eng=self.pool)
        self.sq_free[s] = (self.sum_tok,)

    def columns_to_rows(self, stat_bank, stat_ready, ncol, width, eps, banks_out):
        h = self.h
        t = self.act(h["rs"][:, 0:ncol], stat_bank[:, 0:ncol], ACT.Sqrt, stat_ready, *self.rs_free,
                     scale=1.0 / width, bias=h["eps"][:, 0:1] if eps == EPS_RMS else h["eps"][:, 1:2])
        stat_read = t
        t = self.recip(h["rs2"][:, 0:ncol], h["rs"][:, 0:ncol], t, *self.rs_free)
        out = []
        for c in range(ncol):
            s = c % 4
            d = self.ts(h["diag"][:, s, :], h["ident"][:, :], h["rs2"][:, c:c + 1], None, ALU.mult, None, t,
                        *self.diag_free[s])
            bank, at, free = banks_out[c]
            m = self.mm(bank[:, at:at + P], h["ones"][:, :], h["diag"][:, s, :], True, True, d, *free, signal=True)
            self.diag_free[s] = (m,)
            out.append(m)
        self.rs_free = (d,)
        return stat_read, out

    def rstd(self, dst, bank, ready, width, eps, *after):
        bias = self.h["eps"][:, 0:1] if eps == EPS_RMS else self.h["eps"][:, 1:2]
        t = self.act(dst, bank, ACT.Sqrt, ready, *after, scale=1.0 / width, bias=bias)
        return t, self.recip(dst, dst, t)

    def rms_rows(self, n, width, eps, sum_tok):
        h = self.h
        sb, stat, sfree = self.banks.take()
        for tb in range(n // P):
            t = self.mm(stat[:, tb:tb + 1], h["acc"][:, tb * P:(tb + 1) * P], h["ones"][:, 0:1], True, True,
                        sum_tok, *sfree, signal=True)
        self.acc_free = (t,)
        rb, rows, rfree = self.banks.take()
        read, toks = self.columns_to_rows(stat, t, n // P, width, eps, [(rows, tb * P, rfree) for tb in range(n // P)])
        self.banks.free(sb, read)
        return rb, rows, toks[-1]

    def prenorm(self, hT, n, layer, gain, shift_part, hT_ready, sum_tok):
        h = self.h
        self.ada_until(layer, shift_part)
        rb, rows, rt = self.rms_rows(n, D, EPS_RMS, sum_tok)
        mt = self.ada_until(layer, shift_part + 1)
        g = self.small(gain, layer * KC, (layer + 1) * KC).rearrange("p (k o) -> p k o", o=1).broadcast_to([P, KC, 2])
        a = self.stt(h["coef"][:, :, :], self.mod(layer, shift_part + 1), 1.0, g, ALU.add, ALU.mult, mt, self.small_ready,
                     *self.coef_free)
        x = self.x
        x.ready = []
        ahead = {}

        def scaled(k):
            s = k % 2
            for c in range(n // T):
                cs = slice(c * T, (c + 1) * T)
                ahead[k, c] = self.stt(h["tmp"][:, s, cs], hT[:, k, cs], h["coef"][:, k, c:c + 1], rows[:, cs],
                                       ALU.mult, ALU.mult, a, rt, *hT_ready, *self.tmp_free[s])

        scaled(0)
        for k in range(KC):
            s = k % 2
            shift = [self.mod(layer, shift_part)[:, k, c:c + 1] for c in range(2)]
            hi, lo = [], []
            for c in range(n // T):
                cs = slice(c * T, (c + 1) * T)
                hi.append(self.act(x.hi[:, k, cs], h["tmp"][:, s, cs], ACT.Identity, ahead[k, c], mt, *self.x_free,
                                   bias=shift[c]))
            if k + 1 < KC:
                scaled(k + 1)
            for c in range(n // T):
                cs = slice(c * T, (c + 1) * T)
                lo.append(self.stt(x.lo[:, k, cs], h["tmp"][:, s, cs], shift[c], x.hi[:, k, cs].bitcast(F32),
                                   ALU.add, ALU.subtract, hi[c], ahead[k, c], *self.x_free))
            self.tmp_free[s] = (*hi, *lo)
            x.ready.append([*hi, *lo])
            if k == 1:
                self.w.pump()
        f = lo[-1]
        self.banks.free(rb, f)
        self.coef_free = (f,)
        return x

    def split_into(self, hi, lo, src, *after, free=()):
        a = self.act(hi, src, ACT.Copy, *after, *free)
        b = self.tt(lo, src, hi.bitcast(F32), ALU.subtract, a, *after, *free)
        return [a, b]

    def ffn(self, w_in, w_out, x, n, update, between=lambda: None, before_down=lambda half: None):
        h = self.h
        hid_hi = self.place("hid_hi", MID, [P, 12, 2 * T], F32R)
        hid_lo = self.place("hid_lo", MID + 24576, [P, 12, 2 * T], F32R)
        hid_free = ()
        gates = [None, None]

        def gated(q, b, bank, t):
            gates[q] = self.act(h["sg"][:, q, 0:n], bank[:, 0:n], ACT.Silu, t, *self.sg_free[q])
            self.banks.free(b, gates[q])

        for half, (j0, jn) in enumerate(HALVES):
            ready = []
            for j in range(j0, j0 + jn, 2):
                if j == 0:
                    ug, uu = (self.w.take(w_in, 0, KC, base + j * P, 256) for base in (0, FFN))
                    done = self.project_first((ug, uu), x, n)
                    self.w.done(ug, done[3][2])
                    self.w.done(uu, done[3][2])
                else:
                    done = []
                    for base in (0, FFN):
                        u = self.w.take(w_in, 0, KC, base + j * P, 256)
                        for q in range(2):
                            b, bank, free = self.banks.take()
                            done.append((b, bank, self.project(u, q * P, x, n, bank, free)))
                            if base == 0:
                                gated(q, *done[-1])
                        self.w.done(u, done[-1][2])
                for q in range(2):
                    if j == 0:
                        gated(q, *done[q])
                    b, bank, t = done[2 + q]
                    d = self.tt(h["tmp"][:, q, 0:n], bank[:, 0:n], h["sg"][:, q, 0:n], ALU.mult, t, gates[q],
                                *self.tmp_free[q])
                    self.banks.free(b, d)
                    self.sg_free[q] = (d,)
                    r = self.split_into(hid_hi[:, j - j0 + q, 0:n], hid_lo[:, j - j0 + q, 0:n], h["tmp"][:, q, 0:n],
                                        d, free=hid_free)
                    self.tmp_free[q] = tuple(r)
                    ready.append(r)
                between()
            if half == 1:
                self.x_free = (t,)
            before_down(half)
            hid = Unit()
            hid.hi, hid.lo, hid.ready = hid_hi, hid_lo, ready
            hk = jn // 2
            for c in range(KC // 2):
                pair = [self.banks.take() for _ in range(2)]
                for part in range(2):
                    u = self.w.take(w_out, j0 + part * hk, hk, c * 256, 256)
                    ends = []
                    for q in range(2):
                        t = self.project(u, q * P, hid, n, pair[q][1], pair[q][2],
                                         ks=range(part * hk, part * hk + hk), k0=part * hk, start=part == 0, stop=part == 1)
                        ends.append(t)
                    self.w.done(u, t)
                for q in range(2):
                    d = update(2 * c + q, pair[q][1], ends[q], half)
                    self.banks.free(pair[q][0], d)
                between()
            hid_free = (t,)
        self.mid_free = (t,)

    def gated_update(self, layer, part, factor, n, last_half=1):
        h = self.h
        hT = h["hT"]

        def gate():
            mt = self.ada_until(layer, part)
            self.gate_ready = self.ts(h["gate"][:, :, :], self.mod(layer, part), factor, None, ALU.mult, None, mt,
                                      *self.gate_free)

        def update(k, bank, ready, half):
            ends = []
            for c in range(n // T):
                cs = slice(c * T, (c + 1) * T)
                ends.append(self.stt(hT[:, k, cs], bank[:, cs], h["gate"][:, k, c:c + 1], hT[:, k, cs], ALU.mult, ALU.add,
                                     ready, self.gate_ready, *self.h_ready))
            self.gate_free = (ends[-1],)
            self.h_tok[k] = ends[-1]
            if half == last_half:
                self.square_sum(k, hT[:, k, 0:n], n, *ends)
            return ends[-1]

        return gate, update

    def mix_out(self, w_out, x, n, update, kn=KC):
        c = 0
        if kn == KC:
            for c, done in enumerate(self.project_tiles(w_out, [0, 256, 512, 768], x, n, self.ada_step)):
                for q, (b, bank, t) in enumerate(done):
                    self.banks.free(b, update(2 * c + q, bank, t, 1))
            self.x_free = (t,)
            return
        for c in range(KC // 2):
            pair = [self.banks.take() for _ in range(2)]
            for k0 in range(0, kn, KC):
                u = self.w.take(w_out, k0, KC, c * 256, 256)
                ends = []
                for q in range(2):
                    t = self.project(u, q * P, x, n, pair[q][1], pair[q][2], ks=range(k0, k0 + KC), k0=k0,
                                     start=k0 == 0, stop=k0 + KC == kn)
                    ends.append(t)
                self.w.done(u, t)
            for q in range(2):
                self.banks.free(pair[q][0], update(2 * c + q, pair[q][1], ends[q], 1))
        self.x_free = (t,)

    def evac(self, dst, bank, t, eng="act", func=ACT.Copy, scale=1.0, *after):
        if eng == "act":
            return self.act(dst, bank, func, t, *after, scale=scale)
        return self.copy(dst, bank, t, *after)

    def even_mixer(self, x):
        h, io, n = self.h, self.io, 2 * T
        w = io["even_w_in"]
        q = self.place("gla_q", MID, [P, 3, n])
        k = self.place("gla_k", MID + 6144, [P, 3, n])
        v = self.place("gla_v", MID + 12288, [P, 4, 768])
        r = self.place("gla_r", MID + 24576, [P, 6, n])
        zf = self.place("gla_zf", MID + 36864, [P, 4, 256])
        zg = self.place("gla_zg", MID + 40960, [P, n])
        gw = self.place("gla_gw", MID + 43008, [P, 2, 384])
        fy = self.place("four_y", MID + 46080, [P, 2, n])
        bar = self.mid_free
        z = self.pool.do(lambda e: e.memset(gw[96:128, :, :], 0.0), *bar, self.pool.last())
        self.pool.first = [z]
        gwt = [self.load(gw[96 + 16 * d:112 + 16 * d, d, :], io["gate_w"][d], z, *bar) for d in range(2)]

        qk = []
        for c, done in enumerate(self.project_tiles(w, [256, 512, 768], x, n, self.ada_step)):
            for j, (b, bank, t) in enumerate(done):
                m = 2 * c + j
                dst = q[:, m, :] if m < 3 else k[:, m - 3, :]
                e = self.act(dst, bank[:, :], ACT.Copy, t, scale=GLA_DK ** -0.5 if m < 3 else 1.0)
                self.banks.free(b, e)
                qk.append(e)
        u = self.w.take(w, 0, KC, 2592 - P, P)
        b, bank, free = self.banks.take()
        t = self.project(u, 0, x, n, bank, free)
        self.w.done(u, t)
        zgt = self.act(zg[96:128, :], bank[96:128, :], ACT.Copy, t)
        self.banks.free(b, zgt)

        def rows(c0, dst, c):
            u = self.w.take(w, 0, KC, c0, 256)
            ends = []
            for tb in range(4):
                b, bank, free = self.banks.take()
                t = self.project_rows(u, 256, x, tb, bank, free)
                e = self.copy(dst[:, tb, c:c + 256], bank[:, 0:256], t)
                self.banks.free(b, e)
                ends.append(e)
            self.w.done(u, t)
            self.ada_step()
            return ends
        zft = rows(0, zf, 0)
        vt = [e for c in range(3) for e in rows(1024 + 256 * c, v, 256 * c)]
        spots = [MID + 50176 + 2048 * i for i in range(6)] + [TEMPS + 14336, TEMPS + 12288] + \
                [XN + 9216] + [XN + 13312 + 2048 * i for i in range(7)] + [MID + 36864, MID + 38912]
        st_at = (XN + 27648, MID + 62464)
        dirs = []
        for d in range(2):
            o = Unit()
            o.ls = self.place(f"gla_ls{d}", spots.pop(0), [P, n])
            o.l = self.place(f"gla_l{d}", spots.pop(0), [P, n])
            o.order = [4, 5, 6, 7, 0, 1, 2, 3] if d == 0 else [7, 6, 5, 4, 3, 2, 1, 0]
            o.st = self.place(f"gla_st{d}", st_at[d], [P, 7, P])
            o.sets = []
            o.st_free = ()
            dirs.append(o)
        seg = self.place("seg", spots.pop(0), [P, n])
        cseg = self.load(seg[:, :], io["segments"], *self.mid_free, *self.x.ready[KC - 1])
        ksn = self.place("gla_ksn", spots.pop(0), [P, 4, P])
        for e in range(2):
            for d, o in enumerate(dirs):
                w_ = Unit()
                w_.qd = self.place(f"gla_qd{d}{e}", spots.pop(0), [P, n])
                w_.kd = self.place(f"gla_kd{d}{e}", spots.pop(0), [P, n])
                w_.ks = self.place(f"gla_ks{d}{e}", spots.pop(0), [P, n])
                w_.dec = self.place(f"gla_dec{d}{e}", XN + 31232 + 64 * d + 32 * e, [P, 8])
                w_.free = ()
                o.sets.append(w_)
        att = self.place("gla_att", XN, [P, 4, 4, P])
        ksn_free = [()]
        att_free = [(), (), (), ()]
        inv = 1.0 / GLA_TAU
        by_chunk = lambda ap: ap.rearrange("p (c i) -> p c i", i=GLA_CHUNK)

        def gates(m):
            for d, o in enumerate(dirs):
                b, bank, free = self.banks.take()
                t = self.mm(bank[:, :], gw[96:128, d, m * P:(m + 1) * P], zg[96:128, :], True, True, zgt, *gwt, *free,
                            signal=True)
                gb = self.small("gate_b", d * 3 + m, d * 3 + m + 1)
                o.t1 = self.ts(o.ls[:, :], bank[:, :], gb, None, ALU.add, None, t)
                self.banks.free(b, o.t1)
            for o in dirs:
                o.t2 = self.stt(o.l[:, :], o.ls[:, :], -1.0, o.ls[:, :], ALU.mult, ALU.min, o.t1)
                o.t3 = self.act(o.l[:, :], o.l[:, :], ACT.Exp, o.t2)
            for o in dirs:
                o.t4 = self.act(o.l[:, :], o.l[:, :], ACT.Ln, o.t3, bias=h["one"][:, 0:1])
            for o in dirs:
                o.t5 = self.stt(o.ls[:, :], o.ls[:, :], 0.0, o.l[:, :], ALU.min, ALU.subtract, o.t4, o.t1)

        gates(0)
        rt = []
        for c in range(3):
            u = self.w.take(w, 0, KC, 1792 + 256 * c, 256)
            for j in range(2):
                b, bank, free = self.banks.take()
                t = self.project(u, j * P, x, n, bank, free)
                e = self.act(r[:, 2 * c + j, :], bank[:, :], ACT.Silu, t)
                self.banks.free(b, e)
                rt.append(e)
            self.w.done(u, t)
            self.ada_step()
        self.ada_finish()
        bar = (self.pe.last(),)
        for e in (self.act_e, self.dve, self.pool):
            e.first = list(bar)
        sbank_b, sbank, sfree = self.banks.take()

        ft = self.place("four_t", XN, [P, 2, 512])
        fd = self.place("four_d", XN + 8192, [P, 2, 128])
        lim = self.place("lim", XN + 11264, [P, 4, 1, P])
        fa = self.place("four_a", XN + 4096, [P, 2, 512])
        cft = self.load(ft[:, :, :], io["fourier_time"], *bar)
        cfd = self.load(fd[:, :, :], io["fourier_dim"], *bar)
        clim = self.load(lim[:, :, :, :], io["limits"], *bar)

        fa_free = [(), ()]
        fa_t = [None, None]

        def fourier_time(c, s):
            b, bank, free = self.banks.take()
            for tb in range(2):
                t = self.mm(bank[:, :], zf[:, 2 * s + tb, c * P:(c + 1) * P], ft[:, tb, :], tb == 0, tb == 1,
                            cft, *free, *zft, signal=tb == 1)
            fa_t[s] = self.copy(fa[:, s, :], bank[:, :], t, *fa_free[s])
            self.banks.free(b, fa_t[s])

        def fourier_dim(c, s):
            b, bank, free = self.banks.take()
            self.mm(bank[:, 0:T], fd[:, 0, :], fa[:, s, 0:T], True, False, fa_t[s], cfd, *free)
            t = self.mm(bank[:, 0:T], fd[:, 1, :], fa[:, s, T:2 * T], False, True, signal=True)
            fa_free[s] = (t,)
            e = self.act(fy[:, c, s * T:(s + 1) * T], bank[:, 0:T], ACT.Copy, t)
            self.banks.free(b, e)

        def decays(m):
            for d, o in enumerate(dirs):
                w_ = o.sets[m % 2]
                line = o.ls[:, :] if d == 0 else o.ls[:, ::-1]
                o.t6 = self.scan(line, seg[:, :], line, o.t5, cseg)
                ends = by_chunk(o.ls[:, :])[:, :, 63:64] if d == 0 else by_chunk(o.ls[:, :])[:, :, 0:1]
                w_.dec_t = self.act(w_.dec[:, :], ends, ACT.Exp, o.t6, *w_.free, scale=inv)
                w_.e1 = self.act(w_.qd[:, :], o.ls[:, :], ACT.Exp, o.t6, *w_.free, scale=inv)
                w_.e2 = self.act(w_.kd[:, :], o.ls[:, :], ACT.Exp, o.t6, *w_.free, scale=-inv)
                o.d1 = self.tt(by_chunk(o.l[:, :]), ends.broadcast_to([P, NCH, GLA_CHUNK]), by_chunk(o.ls[:, :]),
                               ALU.subtract, o.t6, o.t5)
                w_.e3 = self.act(w_.ks[:, :], o.l[:, :], ACT.Exp, o.d1, *w_.free, scale=inv)

        def decayed(m):
            for o in dirs:
                w_ = o.sets[m % 2]
                w_.qd_t = self.tt(w_.qd[:, :], w_.qd[:, :], q[:, m, :], ALU.mult, w_.e1, *qk)
                w_.kd_t = self.tt(w_.kd[:, :], w_.kd[:, :], k[:, m, :], ALU.mult, w_.e2, *qk, eng=self.pool)
                w_.ks_t = self.tt(w_.ks[:, :], w_.ks[:, :], k[:, m, :], ALU.mult, w_.e3, *qk)

        def keys(m, d):
            w_ = dirs[d].sets[m % 2]
            b, bank, free = self.banks.take()
            for tb in range(4):
                t = self.transpose(bank[:, tb * P:(tb + 1) * P], w_.ks[:, tb * P:(tb + 1) * P], w_.ks_t, *free,
                                   signal=tb == 3)
            dirs[d].kst = self.act(ksn[:, :, :], bank[:, :].rearrange("p (a b) -> p a b", a=4), ACT.Copy, t, *ksn_free[0])
            self.banks.free(b, dirs[d].kst)

        def states(m, d):
            o = dirs[d]
            kst = o.kst
            w_ = o.sets[m % 2]
            ub = [self.banks.take() for _ in range(2)]
            for c in o.order[:7]:
                pr, tb = 64 * (c % 2), c // 2
                for hl in range(2):
                    t = self.mm(ub[c % 2][1][64 * hl:64 * hl + 64, tb * P:(tb + 1) * P],
                                ksn[pr:pr + 64, tb, 64 * hl:64 * hl + 64],
                                v[pr:pr + 64, tb, (2 * m + hl) * P:(2 * m + hl + 1) * P], True, True,
                                kst, *vt, *ub[c % 2][2], signal=True)
            ksn_free[0] = (t,)
            for s, c in enumerate(o.order[:7]):
                up = ub[c % 2][1][:, (c // 2) * P:(c // 2 + 1) * P]
                if s == 0:
                    st = self.copy(o.st[:, 0, :], up, t, *o.st_free)
                else:
                    st = self.stt(o.st[:, s, :], o.st[:, s - 1, :], w_.dec[:, c:c + 1], up, ALU.mult, ALU.add, st, t,
                                  w_.dec_t)
            o.st_t = st
            for bb in ub:
                self.banks.free(bb[0], st)

        def inside(m, d):
            o = dirs[d]
            w_ = o.sets[m % 2]
            for hl in range(2):
                b, bank, free = self.banks.take()
                hs = slice(64 * hl, 64 * hl + 64)
                for tb in range(4):
                    t = self.mm(bank[:, tb * P:(tb + 1) * P], w_.kd[hs, tb * P:(tb + 1) * P],
                                w_.qd[hs, tb * P:(tb + 1) * P], True, True, w_.kd_t, w_.qd_t, *free, signal=tb == 3)
                i = 2 * d + hl
                a = att[:, i, :, :]
                t1 = self.tt(a, bank[:, :].rearrange("p (a b) -> p a b", a=4),
                             lim[:, 2 * d, :, :].broadcast_to([P, 4, P]), ALU.min, t, clim, *att_free[i])
                self.banks.free(b, t1)
                att_t[i] = self.tt(a, a, lim[:, 2 * d + 1, :, :].broadcast_to([P, 4, P]), ALU.max, t1)

        squares = {}

        def square_sums(hd):
            if hd not in squares:
                return
            for tb in range(4):
                t = self.mm(sbank[:, hd * 4 + tb:hd * 4 + tb + 1], h["sq2"][:, 0, tb * P:(tb + 1) * P], h["ones"][:, 0:1],
                            True, True, squares[hd], *sfree, signal=True)
            self.sq2_free[0] = (t,)

        def outputs(m):
            for hl in range(2):
                hd = 2 * m + hl
                hs = slice(64 * hl, 64 * hl + 64)
                b, bank, free = self.banks.take()
                first = True
                for d, o in enumerate(dirs):
                    for tb in range(4):
                        self.mm(bank[:, tb * P:(tb + 1) * P], v[:, tb, hd * P:(hd + 1) * P], att[:, 2 * d + hl, tb, :],
                                first, False, att_t[2 * d + hl], *free, loose=True)
                        first = False
                for d, o in enumerate(dirs):
                    w_ = o.sets[m % 2]
                    for s, c in enumerate(o.order[1:]):
                        t = self.mm(bank[:, c * 64:(c + 1) * 64], o.st[hs, s, :], w_.qd[hs, c * 64:(c + 1) * 64], False,
                                    d == 1 and s == 6, o.st_t, w_.qd_t, loose=True, signal=d == 1 and s == 6)
                att_free[hl] = att_free[2 + hl] = (t,)
                square_sums(hd - 1)
                y1 = self.tt(r[:, hd, :], r[:, hd, :], bank[:, :], ALU.mult, t, *rt)
                y2 = self.act(h["sq2"][:, 0, :], bank[:, :], ACT.Square, t, y1, *self.sq2_free[0])
                self.banks.free(b, y2)
                squares[hd] = y2
            for o in dirs:
                o.sets[m % 2].free = (t,)
                o.st_free = (t,)

        att_t = {}
        decays(0)
        decayed(0)
        parts = [(c, s) for c in range(2) for s in range(2)]
        for i in range(len(parts) + 1):
            if i < len(parts):
                fourier_time(*parts[i])
            if i:
                fourier_dim(*parts[i - 1])
        for m in range(3):
            for d in range(2):
                keys(m, d)
                inside(m, d)
                states(m, d)
            if m < 2:
                gates(m + 1)
                decays(m + 1)
            outputs(m)
            if m < 2:
                decayed(m + 1)
        square_sums(5)
        t = self.pe.last()
        bar = self.barrier()
        xh, xl = self.x.hi, self.x.lo
        self.x.ready = [self.split_into(xh[:, c, :], xl[:, c, :], fy[:, c, :]) for c in range(2)]
        outs, taken = [], []
        for hd in range(6):
            b, bank, free = self.banks.take()
            taken.append((b, bank))
            outs += [(bank, tb * P, free) for tb in range(4)]
            if len(taken) == 6:
                break
        read, toks = self.columns_to_rows(sbank, t, 24, GLA_DV, EPS_RMS, outs)
        self.banks.free(sbank_b, read)
        for hd in range(6):
            y = self.stt(r[:, hd, :], r[:, hd, :], self.small("gla_norm"), taken[hd][1][:, :], ALU.mult, ALU.mult,
                         toks[4 * hd + 3])
            self.banks.free(taken[hd][0], y)
            self.x.ready.append(self.split_into(xh[:, 2 + hd, :], xl[:, 2 + hd, :], r[:, hd, :], y))
        return self.x

    def rope(self, dst, src, cos, sin, rot, n, *after):
        b, bank, free = self.banks.take()
        t = self.mm(bank[:, 0:n], rot, src, True, True, *after, *free, signal=True)
        s = self.rope_i % 2
        self.rope_i += 1
        h = self.h
        t1 = self.tt(h["rt"][:, s, 0:n], bank[:, 0:n], sin, ALU.mult, t, *self.rt_free[s])
        self.banks.free(b, t1)
        t2 = self.tt(dst, src, cos, ALU.mult, t, *after, eng=self.pool)
        t3 = self.tt(dst, dst, h["rt"][:, s, 0:n], ALU.add, t1, t2)
        self.rt_free[s] = (t3,)
        return t3

    def rope_later(self, done, *args):
        self.rope_open.append((done, args))
        self.rope_flush(2)

    def rope_flush(self, keep=0):
        while len(self.rope_open) > keep:
            done, args = self.rope_open.pop(0)
            done(self.rope(*args))

    def odd_mixer(self, x):
        h, io = self.h, self.io
        w = io["odd_w_in"]
        q = self.place("df_q", MID, [P, 6, T])
        k = self.place("df_k", MID + 6144, [P, 6, 2 * T])
        v = self.place("df_v", MID + 18432, [P, 4, 768])
        z3 = self.place("df_z", MID + 30720, [P, 3, 2, T])
        cs = self.place("df_cs", MID + 36864, [P, 2, T])
        rot = self.place("df_rot", MID + 38912, [P, P])
        raw = self.place("df_raw", MID + 39424, [P, 4, T])
        h["rt"] = self.place("df_rt", MID + 43520, [P, 2, T])
        self.rt_free = [(), ()]
        y = self.place("df_y", MID + 45568, [P, 8, T])
        bar = self.mid_free
        ccs = self.load(cs[:, :, :], io["axial"], *bar)
        crot = self.load(rot[:, :], io["axial_rot"], *bar)

        zt = []
        for c, done in enumerate(self.project_tiles(w, [0, 256, 512], x, T, self.ada_step)):
            for j, (b, bank, t) in enumerate(done):
                e = self.act(z3[:, c, j, :], bank[:, 0:T], ACT.Copy, t)
                self.banks.free(b, e)
                zt.append(e)
        qt, kt = [], []
        raw_free = [()] * 4
        i = 0
        conv_y = []
        lam_t = None
        for part, dst, toks in ((0, q, qt), (1, k, kt)):
            if part:
                lam = self.small("lambdas")
                lv = h["lam"]
                t = self.tt(lv[0:64, 0:2], lam[0:64, 0:2], lam[0:64, 2:4], ALU.mult)
                b, bank, free = self.banks.take()
                t = self.mm(bank[:, 0:2], h["ones"][0:64, :], lv[0:64, 0:2], True, True, t, *free, signal=True)
                t = self.act(lv[:, 2:4], bank[:, 0:2], ACT.Exp, t)
                self.banks.free(b, t)
                t = self.tt(lv[:, 4:5], lv[:, 3:4], lv[:, 2:3], ALU.subtract, t)
                lam_t = self.ts(lv[:, 5:6], lv[:, 4:5], -LAM_INIT, None, ALU.add, None, t)

                for j in range(2):
                    u_ = z3[:, 1, j, :]
                    tap = [self.small("conv_w", 2 * a + j, 2 * a + j + 1) for a in range(3)]
                    t = self.tt(u_, z3[:, 1, j, :], z3[:, 2, j, :], ALU.mult, *zt)
                    t = self.ts(y[:, j, :], u_, tap[1], self.small("conv_b", j, j + 1), ALU.mult, ALU.add, t)
                    t = self.stt(y[:, j, 1:T], u_[:, 0:T - 1], tap[0], y[:, j, 1:T], ALU.mult, ALU.add, t)
                    t = self.stt(y[:, j, 0:T - 1], u_[:, 1:T], tap[2], y[:, j, 0:T - 1], ALU.mult, ALU.add, t)
                    conv_y.append(self.tt(y[:, j, :], y[:, j, :], z3[:, 0, j, :], ALU.mult, t, *zt))
            for c in range(3):
                u = self.w.take(w, 0, KC, 768 + 768 * part + 256 * c, 256)
                for j in range(2):
                    m = 2 * c + j
                    n = T * (1 + part)
                    b, bank, free = self.banks.take()
                    t = self.project(u, j * P, x, n, bank, free)
                    s = i % 4
                    i += 1
                    e = self.act(raw[:, s, :], bank[:, 0:T], ACT.Copy, t, *raw_free[s])
                    if part:
                        e2 = self.act(k[:, m, T:2 * T], bank[:, T:2 * T], ACT.Copy, t)
                        toks.append(e2)
                        self.banks.free(b, e2)
                    else:
                        self.banks.free(b, e)

                    def turned(t, s=s, toks=toks):
                        raw_free[s] = (t,)
                        toks.append(t)
                    self.rope_later(turned, dst[:, m, 0:T], raw[:, s, :], cs[:, 0, :], cs[:, 1, :], rot[:, :], T, e, ccs,
                                    crot)
                self.w.done(u, t)
                self.ada_step()
        vt = []
        for c in range(3):
            u = self.w.take(w, 0, KC, 2304 + 256 * c, 256)
            for tb in range(4):
                b, bank, free = self.banks.take()
                t = self.project_rows(u, 256, x, tb, bank, free)
                e = self.copy(v[:, tb, 256 * c:256 * c + 256], bank[:, 0:256], t)
                self.banks.free(b, e)
                vt.append(e)
            self.w.done(u, t)
            self.rope_flush()
            self.ada_step()

        bar = self.barrier()

        NS = 3
        e_ = self.place("df_e", XN, [P, NS, 2, 2 * T])
        aT = self.place("df_aT", XN + 12288, [P, NS, 4, P])
        sc = self.place("df_sc", XN + 12288 + 6144, [P, 12, 8])
        scale = HD ** -0.5
        sbank_b, sbank, sfree = self.banks.take()
        jobs = [(hd, qb) for hd in range(6) for qb in range(TB)]
        st = {}
        e_free = [()] * NS
        aT_free = [()] * NS
        obank = {}

        def scores(i):
            hd, qb = jobs[i]
            st[i] = []
            for s in range(2):
                b, bank, free = self.banks.take()
                t = self.mm(bank[:, :], q[64 * s:64 * s + 64, hd, qb * P:(qb + 1) * P], k[64 * s:64 * s + 64, hd, :],
                            True, True, *qt, *kt, *free, signal=True)
                c = sc[:, i, :]
                m = self.rmax(c[:, s:s + 1], bank[:, :], t)
                m = self.ts(c[:, 2 + s:3 + s], c[:, s:s + 1], scale, None, ALU.mult, None, m)
                e = self.act(e_[:, i % NS, s, :], bank[:, :], ACT.Exp, t, m, *e_free[i % NS], scale=scale,
                             bias=c[:, 2 + s:3 + s], accum=c[:, 4 + s:5 + s])
                self.banks.free(b, e)
                st[i].append(e)

        def combine(i):
            c = sc[:, i, :]
            a, e1 = e_[:, i % NS, 0, :], e_[:, i % NS, 1, :]
            t = self.recip(c[:, 6:8], c[:, 4:6], *st[i])
            t1 = self.tt(c[:, 7:8], c[:, 7:8], h["lam"][:, 5:6], ALU.mult, t, lam_t)
            t2 = self.ts(a, a, c[:, 6:7], None, ALU.mult, None, t, *st[i])
            t3 = self.stt(a, e1, c[:, 7:8], a, ALU.mult, ALU.add, t1, t2)
            st[i] = t3

        def turn(i):
            b, bank, free = self.banks.take()
            for kb in range(4):
                t = self.transpose(bank[:, kb * P:(kb + 1) * P], e_[:, i % NS, 0, kb * P:(kb + 1) * P], st[i], *free,
                                   signal=kb == 3)
            e_free[i % NS] = (t,)
            e = self.act(aT[:, i % NS, :, :], bank[:, :].rearrange("p (a b) -> p a b", a=4), ACT.Copy, t, *aT_free[i % NS])
            self.banks.free(b, e)
            st[i] = e

        def values(i):
            hd, qb = jobs[i]
            if qb == 0:
                obank[hd] = self.banks.take()
            b, bank, free = obank[hd]
            for kb in range(4):
                t = self.mm(bank[:, qb * P:(qb + 1) * P], v[:, kb, hd * P:(hd + 1) * P], aT[:, i % NS, kb, :], kb == 0,
                            kb == 3, st[i], *vt, *free, signal=kb == 3)
            aT_free[i % NS] = (t,)
            if qb == TB - 1:
                s = hd % 2
                y2 = self.act(h["sq2"][:, s, 0:T], bank[:, 0:T], ACT.Square, t, *self.sq2_free[s])
                y1 = self.copy(y[:, 2 + hd, :], bank[:, 0:T], t, y2)
                self.banks.free(b, y1)
                squares[hd] = y2

        squares = {}

        def square_sums(hd):
            s = hd % 2
            for tb in range(TB):
                t = self.mm(sbank[:, hd * TB + tb:hd * TB + tb + 1], h["sq2"][:, s, tb * P:(tb + 1) * P],
                            h["ones"][:, 0:1], True, True, squares.pop(hd) if tb == 0 else None, *sfree, signal=True)
            self.sq2_free[s] = (t,)
            self.stat_t = t

        nj = len(jobs)
        for i in range(nj + 2):
            if 0 <= i - 1 < nj:
                combine(i - 1)
            if i < nj:
                scores(i)
            if 0 <= i - 2 < nj:
                values(i - 2)
            if 0 <= i - 1 < nj:
                turn(i - 1)
            for hd in [hd for hd in squares if i > (hd + 1) * TB + 1 or i == nj + 1]:
                square_sums(hd)
        bar = self.barrier()
        xh, xl = self.x.hi, self.x.lo
        self.x.ready = [self.split_into(xh[:, c, 0:T], xl[:, c, 0:T], y[:, c, :]) for c in range(2)]
        outs, taken = [], []
        for hd in range(3):
            b, bank, free = self.banks.take()
            taken.append((b, bank))
            outs += [(bank, tb * P, free) for tb in range(4)]
        read, toks = self.columns_to_rows(sbank, self.stat_t, 12, 2 * HD, EPS_RMS, outs)
        self.banks.free(sbank_b, read)
        g = self.ts(h["lam"][:, 6:7], self.small("diff_norm"), 1.0 - LAM_INIT, None, ALU.mult, None)
        for hd in range(6):
            rows = taken[hd // 2][1][:, (hd % 2) * T:(hd % 2 + 1) * T]
            t = self.stt(y[:, 2 + hd, :], y[:, 2 + hd, :], h["lam"][:, 6:7], rows, ALU.mult, ALU.mult, g, toks[4 * (hd // 2) + 3])
            if hd % 2:
                self.banks.free(taken[hd // 2][0], t)
            self.x.ready.append(self.split_into(xh[:, 2 + hd, 0:T], xl[:, 2 + hd, 0:T], y[:, 2 + hd, :], t))
        return self.x

    def residual_update(self, first):
        hT = self.h["hT"]

        def update(k, bank, ready, half):
            if half == first:
                t = self.stt(hT[:, k, 0:T], hT[:, k, 0:T], ALPHA, bank[:, 0:T], ALU.mult, ALU.add, ready, *self.h_ready)
            else:
                t = self.tt(hT[:, k, 0:T], hT[:, k, 0:T], bank[:, 0:T], ALU.add, ready, self.h_tok[k])
            self.h_tok[k] = t
            if half == 1:
                acc = self.h["acc"]
                if k == 0:
                    self.sum_tok = self.pool.do(lambda e: e.tensor_copy(acc[:, 0:T], hT[:, 0, 0:T]), t, *self.acc_free)
                else:
                    self.sum_tok = self.tt(acc[:, 0:T], acc[:, 0:T], hT[:, k, 0:T], ALU.add, t, self.sum_tok, eng=self.pool)
            return t
        return update

    def layer_norm(self, which, split=True):
        h, hT = self.h, self.h["hT"]
        b, bank, free = self.banks.take()
        mt = self.mm(bank[:, 0:T], h["mean"][:, :], h["acc"][:, 0:T], True, True, self.sum_tok, *free, signal=True)
        self.acc_free = (mt,)
        d = []
        mean = bank[:, 0:T].rearrange("p (o n) -> p o n", o=1).broadcast_to([P, 2, T])
        sb, stat, sfree = self.banks.take()
        for k in range(0, KC, 2):
            s = k // 2 % 2
            t = self.tt(hT[:, k:k + 2, 0:T], hT[:, k:k + 2, 0:T], mean, ALU.subtract, mt, self.h_tok[k], self.h_tok[k + 1])
            d += [t, t]
            e = self.act(h["sq"][:, s, :].rearrange("p (k n) -> p k n", k=2), hT[:, k:k + 2, 0:T], ACT.Square, t,
                         *self.sq_free[s])
            for j in range(2):
                m = self.mm(stat[:, 0:T], h["ones"][:, :], h["sq"][:, s, j * T:(j + 1) * T], k + j == 0, k + j == KC - 1,
                            e, *sfree, signal=j == 1)
            self.sq_free[s] = (m,)
        self.banks.free(b, t)
        rows = h["acc"]
        read, rt = self.rstd(rows[:, 0:T], stat[:, 0:T], m, D, EPS_LN, *self.acc_free)
        self.banks.free(sb, read)
        x = self.x
        x.ready = []
        ready_h = []
        for k in range(KC):
            g = self.small("ln_gain", which * KC + k, which * KC + k + 1)
            bb = self.small("ln_bias", which * KC + k, which * KC + k + 1)
            s = k % 2
            t = self.stt(h["tmp"][:, s, 0:T], hT[:, k, 0:T], g, rows[:, 0:T], ALU.mult, ALU.mult, rt, d[k], *self.tmp_free[s])
            if split:
                o = self.ts(hT[:, k, 0:T], h["tmp"][:, s, 0:T], bb, None, ALU.add, None, t, eng=self.pool)
            else:
                o = self.act(hT[:, k, 0:T], h["tmp"][:, s, 0:T], ACT.Identity, t, bias=bb)
            ready_h.append(o)
            if split:
                e = self.act(x.hi[:, k, 0:T], h["tmp"][:, s, 0:T], ACT.Identity, t, *self.x_free, bias=bb)
                f = self.stt(x.lo[:, k, 0:T], h["tmp"][:, s, 0:T], bb, x.hi[:, k, 0:T].bitcast(F32), ALU.add, ALU.subtract,
                             e, t, *self.x_free)
                self.tmp_free[s] = (o, e, f)
                x.ready.append([e, f])
            else:
                self.tmp_free[s] = (o,)
        self.acc_free = (t,)
        self.h_ready = tuple(ready_h)
        return x

    def retention(self, x):
        h, io = self.h, self.io
        w = io["ret_w_in"]
        q = self.place("rt_q", MID, [P, 8, T])
        k = self.place("rt_k", MID + 8192, [P, 8, T])
        v = self.place("rt_v", MID + 16384, [P, TB, 2048])
        gate = self.place("rt_g", MID + 32768, [P, 16, T])
        cs = self.place("rt_cs", MID + 49152, [P, 2, 2, T])
        rot = self.place("rt_rot", MID + 53248, [P, P])
        h["rt"] = self.place("rt_rt", MID + 53760, [P, 2, T])
        raw = self.place("rt_raw", TEMPS + 2048, [P, 4, T])
        self.rt_free = [(), ()]
        bar = self.mid_free
        dec = self.place("rt_dec", TEMPS + 10240, [P, 4, 384])
        cdec = self.load(dec[:, :, :], io["decay"], *bar)
        ccs = self.load(cs[:, :, :, :], io["ret_rope"], *bar)
        crot = self.load(rot[:, :], io["pair_rot"], *bar)
        qk = []
        raw_free = [()] * 4
        for c, done in enumerate(self.project_tiles(w, [256 * c for c in range(8)], x, T)):
            for j, (b, bank, t) in enumerate(done):
                m = 2 * c + j
                e = self.act(raw[:, m % 4, :], bank[:, 0:T], ACT.Copy, t, *raw_free[m % 4])
                self.banks.free(b, e)
                dst = q[:, m, :] if m < 8 else k[:, m - 8, :]

                def turned(t, s=m % 4):
                    raw_free[s] = (t,)
                    qk.append(t)
                self.rope_later(turned, dst, raw[:, m % 4, :], cs[:, 0, m % 2, :], cs[:, 1, m % 2, :], rot[:, :], T, e, ccs,
                                crot)
        vt = []
        for c in range(8):
            u = self.w.take(w, 0, KC, 2048 + 256 * c, 256)
            for tb in range(TB):
                b, bank, free = self.banks.take()
                t = self.project_rows(u, 256, x, tb, bank, free)
                e = self.copy(v[:, tb, 256 * c:256 * c + 256], bank[:, 0:256], t)
                self.banks.free(b, e)
                vt.append(e)
            self.w.done(u, t)
            self.rope_flush()
        gt = []
        for c in range(8):
            u = self.w.take(w, 0, KC, 4096 + 256 * c, 256)
            for j in range(2):
                b, bank, free = self.banks.take()
                t = self.project(u, j * P, x, T, bank, free)
                e = self.act(gate[:, 2 * c + j, :], bank[:, 0:T], ACT.Silu, t)
                self.banks.free(b, e)
                gt.append(e)
            self.w.done(u, t)
        bar = (self.pe.last(),)
        S = self.place("rt_S", XN + 6144, [P, 2, 384])
        yb = self.place("rt_y", XN + 9216, [P, 2, 4, T])
        sqr = self.place("rt_sq", XN + 17408, [P, 4, T])
        r = Unit()
        r.hi = self.place("rt_hi", MID, [P, 16, T], F32R)
        r.lo = self.place("rt_lo", MID + 32768, [P, 16, T], F32R)
        r.ready = []
        s_free = [bar, bar]
        y_free = [bar, bar]
        sq_free = [bar]
        st, ys, centred = {}, {}, {}

        def scores(hd):
            s = hd % 2
            b, bank, free = self.banks.take()
            for jb, (i0, i1, at) in enumerate(((0, T, 0), (P, T, T))):
                for c in range(2):
                    t = self.mm(bank[:, at:at + i1 - i0], k[:, 2 * hd + c, jb * P:(jb + 1) * P], q[:, 2 * hd + c, i0:i1],
                                c == 0, c == 1, *qk, *free, signal=c == 1)
            st[hd] = self.tt(S[:, s, :], bank[:, 0:384], dec[:, hd, :], ALU.mult, t, cdec, *s_free[s])
            self.banks.free(b, st[hd])

        def outputs(hd):
            s = hd % 2
            ys[hd] = []
            for c in range(4):
                e0 = hd * RET_DV + c * P
                b, bank, free = self.banks.take()
                self.mm(bank[:, 0:T], v[:, 0, e0:e0 + P], S[:, s, 0:T], True, False, st[hd], *vt, *free, loose=True)
                t = self.mm(bank[:, P:T], v[:, 1, e0:e0 + P], S[:, s, T:384], False, True, loose=True, signal=True)
                e = self.act(yb[:, s, c, :], bank[:, 0:T], ACT.Copy, t, *y_free[s])
                self.banks.free(b, e)
                ys[hd].append(e)
            s_free[s] = (t,)

        def centre(hd):
            s = hd % 2
            b, bank, free = self.banks.take()
            for c in range(4):
                t = self.mm(bank[:, 0:T], h["ones"][:, :], yb[:, s, c, :], c == 0, c == 3, ys[hd][c], *free, signal=c == 3)
            mu = self.act(h["tmp"][:, 0, 0:T], bank[:, 0:T], ACT.Copy, t, *self.tmp_free[0], scale=1.0 / RET_DV)
            self.banks.free(b, mu)
            centred[hd] = []
            for c in range(4):
                d = self.tt(yb[:, s, c, :], yb[:, s, c, :], h["tmp"][:, 0, 0:T], ALU.subtract, mu, ys[hd][c], t)
                centred[hd].append((d, self.act(sqr[:, c, :], yb[:, s, c, :], ACT.Square, d, *sq_free[0])))
            self.tmp_free[0] = (d,)

        def gated(hd):
            s = hd % 2
            b, bank, free = self.banks.take()
            for tb in range(TB):
                for c in range(4):
                    t = self.mm(bank[:, tb:tb + 1], sqr[:, c, tb * P:(tb + 1) * P], h["ones"][:, 0:1], c == 0, c == 3,
                                centred[hd][c][1], *free, signal=c == 3)
            sq_free[0] = (t,)
            rb, rows, rfree = self.banks.take()
            read, rt = self.columns_to_rows(bank, t, TB, RET_DV, EPS_LN, [(rows, tb * P, rfree) for tb in range(TB)])
            self.banks.free(b, read)
            fs = []
            for c in range(4):
                m = hd * 4 + c
                y = self.tt(yb[:, s, c, :], yb[:, s, c, :], rows[:, 0:T], ALU.mult, rt[-1], *centred[hd][c])
                fs.append(self.tt(gate[:, m, :], gate[:, m, :], yb[:, s, c, :], ALU.mult, y, *gt, eng=self.pool))
            self.banks.free(rb, y)
            y_free[s] = (fs[-1],)
            for c in range(4):
                m = hd * 4 + c
                r.ready.append(self.split_into(r.hi[:, m, :], r.lo[:, m, :], gate[:, m, :], fs[c]))

        for i in range(RET_HEADS + 2):
            if i < RET_HEADS:
                scores(i)
            if i >= 2:
                centre(i - 2)
            if 1 <= i <= RET_HEADS:
                outputs(i - 1)
            if i >= 2:
                gated(i - 2)
        return r

    def bias_tables(self, at, *after):
        io = self.io
        oh = self.place("at_onehot", at, [32, 3, 384])
        mk = self.place("at_mask", at + 4608, [16, 3, 384])
        wide = self.place("at_wide", at + 9216, [16, 3, 384])
        coh = self.load(oh[:, :, :], io["onehot"], *after, *self.h_ready)
        cmk = self.load(mk[:, :, :], io["dist_mask"], *after, *self.h_ready)
        return oh, mk, wide, coh, cmk

    def bias_rows(self, oh, mk, wide, coh, cmk):
        io = self.io
        rel = self.small("rel_bias")
        stored = []
        for g in range(3):
            b, bank, free = self.banks.take()
            t = self.mm(bank[0:16, 0:384], rel[0:32, 16 * g:16 * g + 16], oh[:, g, :], True, True, coh, *free, signal=True)
            t = self.tt(wide[:, g, :], bank[0:16, 0:384], mk[:, g, :], ALU.add, t, cmk)
            self.banks.free(b, t)
            stored.append(self.load(io["bias_rows"][g], wide[:, g, :], t))
        return stored

    def dilated(self, x):
        h, io = self.h, self.io
        w = io["attn_w_in"]
        NQ = ATT_GROUPS * 8
        q = self.place("at_q", MID, [P, NQ, T])
        k = self.place("at_k", MID + 24576, [P, NQ, T])
        v = self.place("at_v", MID + 49152, [P, TB, 3072])
        qt = []
        for part, dst in ((0, q), (1, k)):
            for c, done in enumerate(self.project_tiles(w, [3072 * part + 256 * c for c in range(12)], x, T)):
                for j, (b, bank, t) in enumerate(done):
                    e = self.act(dst[:, 2 * c + j, :], bank[:, 0:T], ACT.Copy, t)
                    self.banks.free(b, e)
                    qt.append(e)
            if part == 0:
                tables = self.bias_tables(MID + 49152, *qt)
        stored = self.bias_rows(*tables)
        vt = []
        for c in range(12):
            u = self.w.take(w, 0, KC, 6144 + 256 * c, 256)
            for tb in range(TB):
                b, bank, free = self.banks.take()
                t = self.project_rows(u, 256, x, tb, bank, free)
                e = self.copy(v[:, tb, 256 * c:256 * c + 256], bank[:, 0:256], t, *self.h_ready, *stored)
                self.banks.free(b, e)
                vt.append(e)
            self.w.done(u, t)
        x_read = (self.pe.last(),)
        NB = 2
        bias = self.place("at_bias", XN, [P, NB, 3, T])
        e_ = self.place("at_e", XN + 6144, [P, 2, 3 * T + 3 * P])
        pT = self.place("at_pT", XN + 15360, [P, 2, 9, P])
        o = self.place("at_o", XN + 24576, [P, TB, D])
        sc = self.place("at_sc", MID + 73728, [P, 16, 6])
        bias_t = {}
        bias_free = [x_read] * NB

        def fetch(hd):
            s = hd % NB
            src = self.io["bias_windows"](hd)
            bias_t[hd] = self.load(bias[:, s, :, :], src, *stored, *bias_free[s])

        fetch(0)
        fetch(1)
        scale = HD ** -0.5
        st = {}
        e_free = [x_read, x_read]
        pT_free = [(), ()]

        def scores(hd):
            hs = slice(64 * (hd % 2), 64 * (hd % 2) + 64)
            s = hd % 2
            ch = [g * 8 + hd // 2 for g in range(3)]
            ba, bb, bc = (self.banks.take() for _ in range(3))
            for g in range(3):
                dst = ba[1][:, g * T:(g + 1) * T] if g < 2 else bb[1][:, 0:T]
                t = self.mm(dst, q[hs, ch[g], P:T], k[hs, ch[g], 0:T], True, True, *qt, *ba[2], *bb[2], signal=True)
            for g in range(3):
                t = self.mm(bc[1][:, g * P:(g + 1) * P], q[hs, ch[g], 0:P], k[hs, ch[g], 0:P], True, True, *bc[2], signal=True)
            E = e_[:, s, :]
            b_ = bias[:, s, :, ::-1]
            t1 = self.stt(E[:, 0:2 * T].rearrange("p (g c) -> p g c", g=2), ba[1][:, :].rearrange("p (g c) -> p g c", g=2),
                          scale, b_[:, 0:2, :], ALU.mult, ALU.add, t, bias_t[hd], *e_free[s])
            t2 = self.stt(E[:, 2 * T:3 * T], bb[1][:, 0:T], scale, b_[:, 2, :], ALU.mult, ALU.add, t, bias_t[hd])
            t3 = self.stt(E[:, 3 * T:].rearrange("p (g c) -> p g c", g=3), bc[1][:, 0:384].rearrange("p (g c) -> p g c", g=3),
                          scale, b_[:, :, P:T], ALU.mult, ALU.add, t, bias_t[hd])
            bias_free[s] = (t3,)
            for bk, tk in ((ba, t1), (bb, t2), (bc, t3)):
                self.banks.free(bk[0], tk)
            c = sc[:, hd, :]
            m1 = self.rmax(c[:, 1:2], E[:, 0:3 * T], t1, t2)
            m0 = self.rmax(c[:, 0:1], E[:, 3 * T:], t3)
            e1 = self.act(E[:, 0:3 * T], E[:, 0:3 * T], ACT.Exp, m1, bias=c[:, 1:2], accum=c[:, 3:4])
            e0 = self.act(E[:, 3 * T:], E[:, 3 * T:], ACT.Exp, m0, bias=c[:, 0:1], accum=c[:, 2:3])
            st[hd] = (e0, e1)
            if hd + 2 < ATT_HEADS:
                fetch(hd + 2)

        def turn(hd):
            s = hd % 2
            c = sc[:, hd, :]
            st[hd, "r"] = self.recip(c[:, 4:6], c[:, 2:4], *st[hd])
            out = []
            for lo_, n_ in ((0, 4), (4, 4), (8, 1)):
                b, bank, free = self.banks.take()
                for i in range(n_):
                    t = self.transpose(bank[:, i * P:(i + 1) * P], e_[:, s, (lo_ + i) * P:(lo_ + i + 1) * P], *st[hd], *free,
                                       signal=i == n_ - 1)
                dst = pT[:, s, lo_:lo_ + n_, :]
                src = bank[:, 0:n_ * P].rearrange("p (a b) -> p a b", a=n_)
                if lo_ == 4:
                    e = self.copy(dst, src, t, *pT_free[s])
                else:
                    e = self.act(dst, src, ACT.Copy, t, *pT_free[s])
                self.banks.free(b, e)
                out.append(e)
            e_free[s] = (t,)
            st[hd] = out

        def values(hd):
            s = hd % 2
            c = sc[:, hd, :]
            b, bank, free = self.banks.take()
            vcol = lambda g: slice(g * D + hd * HD, g * D + hd * HD + HD)
            for g in range(3):
                for kb in range(2):
                    t = self.mm(bank[:, HD:2 * HD], pT[:, s, 2 * g + kb, :], v[:, kb, vcol(g)], g == 0 and kb == 0,
                                g == 2 and kb == 1, *st[hd], *vt, *free, signal=False)
            for g in range(3):
                t = self.mm(bank[:, 0:HD], pT[:, s, 6 + g, :], v[:, 0, vcol(g)], g == 0, g == 2, signal=g == 2)
            pT_free[s] = (t,)
            d = self.ts(o[:, 0, hd * HD:(hd + 1) * HD], bank[:, 0:HD], c[:, 4:5], None, ALU.mult, None, t, st[hd, "r"])
            d = self.ts(o[:, 1, hd * HD:(hd + 1) * HD], bank[:, HD:2 * HD], c[:, 5:6], None, ALU.mult, None, t, st[hd, "r"])
            self.banks.free(b, d)

        for i in range(ATT_HEADS + 2):
            if i < ATT_HEADS:
                scores(i)
            if 1 <= i <= ATT_HEADS:
                turn(i - 1)
            if i >= 2:
                values(i - 2)
        bar = self.barrier()
        r = Unit()
        r.hi = self.place("at_hi", MID, [P, 8, T], F32R)
        r.lo = self.place("at_lo", MID + 8192, [P, 8, T], F32R)
        oT = self.place("at_oT", MID + 16384, [P, 8, T])
        r.ready = []
        for c in range(KC):
            b, bank, free = self.banks.take()
            for tb in range(TB):
                t = self.transpose(bank[:, tb * P:(tb + 1) * P], o[:, tb, c * P:(c + 1) * P], *free, signal=tb == 1)
            e = self.copy(oT[:, c, :], bank[:, 0:T], t)
            self.banks.free(b, e)
            r.ready.append(self.split_into(r.hi[:, c, :], r.lo[:, c, :], oT[:, c, :], e))
        return r

    def run(self):
        h, io = self.h, self.io
        hT = h["hT"]
        self.acc_free = self.coef_free = self.gate_free = self.rs_free = self.x_free = ()
        self.sq_free = [(), ()]
        self.sq2_free = [(), ()]
        self.tmp_free = [(), ()]
        self.sg_free = [(), ()]
        self.diag_free = [(), (), (), ()]
        self.ada_free = [(), ()]
        self.ada_open = None
        self.h_tok = [None] * KC
        self.rope_i = 0
        self.rope_open = []
        self.x = Unit()
        self.x.hi = self.place("x_hi", XN, [P, KC, 2 * T], F32R)
        self.x.lo = self.place("x_lo", XN + 16384, [P, KC, 2 * T], F32R)

        self.small_ready = self.load(h["small"][:, :], io["small"])
        hl = self.load(hT[:, :, :], io["hT"])
        ci = self.load(h["ident"][:, :], io["ident"])
        o1 = self.pool.do(lambda e: e.memset(h["ones"][:, :], 1.0))
        o2 = self.pool.do(lambda e: e.memset(h["mean"][:, :], 1.0 / D))
        o3 = self.pool.do(lambda e: e.memset(h["eps"][:, 0:1], EPS_RMS))
        o4 = self.pool.do(lambda e: e.memset(h["eps"][:, 1:2], EPS_LN))
        o5 = self.pool.do(lambda e: e.memset(h["one"][:, :], 1.0))
        z = self.pool.do(lambda e: e.memset(h["cs"][:, :, :], 0.0))
        self.fold_ready = self.load(h["fold"][:, :], io["fold"])
        self.cs_ready = self.act(h["cs"][:, :, 0:2], self.small("cond").rearrange("p (k c) -> p k c", c=2), ACT.Silu,
                                 self.small_ready, z)
        self.h_ready = (hl,)
        for e in (self.pe, self.act_e, self.dve):
            e.first = [o5, ci, self.small_ready]
        for k in range(KC):
            self.square_sum(k, hT[:, k, :], 2 * T, hl)

        def layer(l, n2):
            x = self.prenorm(hT, 2 * T, l, "norm_ffn1", 0, self.h_ready, self.sum_tok)
            gate, upd = self.gated_update(l, 2, 0.5, 2 * T)
            self.ffn(io["ffn1_w_in"][l], io["ffn1_w_out"][l], x, 2 * T, upd, between=self.ada_step,
                     before_down=lambda half: gate() if half == 0 else None)
            self.h_ready = tuple(self.h_tok)
            x = self.prenorm(hT, 2 * T, l, "norm_mix", 3, self.h_ready, self.sum_tok)
            x = (self.even_mixer if l == 0 else self.odd_mixer)(x)
            gate, upd = self.gated_update(l, 5, 1.0, n2)
            gate()
            self.mix_out(io["mix_w_out"][l], x, n2, upd)
            self.h_ready = tuple(self.h_tok)
            x = self.prenorm(hT, n2, l, "norm_ffn2", 6, self.h_ready, self.sum_tok)
            gate, upd = self.gated_update(l, 8, 0.5, n2)
            self.ffn(io["ffn2_w_in"][l], io["ffn2_w_out"][l], x, n2, upd, between=self.ada_step,
                     before_down=lambda half: gate() if half == 0 else None)
            self.h_ready = tuple(self.h_tok)

        layer(0, 2 * T)
        layer(1, T)
        rb, rows, rt = self.rms_rows(T, D, EPS_RMS, self.sum_tok)
        x = self.x
        x.ready = []
        rd = []
        for k in range(KC):
            t = self.stt(hT[:, k, 0:T], hT[:, k, 0:T], self.small("final_norm", k, k + 1), rows[:, 0:T], ALU.mult, ALU.mult,
                         rt, *self.h_ready)
            x.ready.append(self.split_into(x.hi[:, k, 0:T], x.lo[:, k, 0:T], hT[:, k, 0:T], t, free=self.x_free))
            rd.append(t)
            rd += x.ready[-1]
        self.banks.free(rb, t)
        self.h_ready = tuple(rd)
        for l in range(2):
            upd = self.residual_update(1)
            r = self.retention(x) if l == 0 else self.dilated(x)
            self.mix_out(io["ret_w_out" if l == 0 else "attn_w_out"], r, T, upd, kn=16 if l == 0 else KC)
            self.barrier()
            x = self.layer_norm(2 * l)
            upd = self.residual_update(0)
            self.ffn(io["ffn_w_up"][l], io["ffn_w_down"][l], x, T, upd)
            x = self.layer_norm(2 * l + 1, split=l == 0)

    def finish(self):
        sem = self.h["out_sem"]
        hT, out = self.h["hT"], self.io["out"]
        for k in range(0, KC, 2):
            self.sync.do(lambda e, k=k: e.dma_start(out[:, k:k + 2, :], hT[:, k:k + 2, 0:T]).then_inc(sem, 16),
                         self.h_ready[k], self.h_ready[k + 1], signal=False)
        self.sync.do(lambda e: e.wait_ge(sem, 16 * KC // 2), signal=False)


def build(nc, io):
    with ExitStack() as ctx:
        def sb(name, shape, dt=F32):
            return ctx.enter_context(nc.sbuf_tensor(name, shape, dt))

        def sem(name):
            return ctx.enter_context(nc.semaphore(name))

        h = {
            "hT": sb("hT", [P, KC, 2 * T]), "small": sb("small", [P, SMALL_N]), "ident": sb("ident", [P, P]),
            "ones": sb("ones", [P, P]), "mean": sb("mean", [P, P]), "eps": sb("eps", [P, 2]), "one": sb("one", [P, 1]),
            "cs": sb("cs", [P, KC, 32]), "fold": sb("fold", [P, 2]), "mod": sb("mod", [P, 2 * MODS * KC, 2]), "coef": sb("coef", [P, KC, 2]),
            "gate": sb("gate", [P, KC, 2]), "rs": sb("rs", [P, 24]), "rs2": sb("rs2", [P, 24]),
            "diag": sb("diag", [P, 4, P]), "lam": sb("lam", [P, 8]),
        }
        raw = sb("w_raw", [P, NRAW, UNIT])
        whi = sb("w_hi", [P, NSPLIT, UNIT], F32R)
        wlo = sb("w_lo", [P, NSPLIT, UNIT], F32R)
        h["work"] = (nc.sbuf_base + 31) // 32 * 32
        assert h["work"] + WORK <= nc.sbuf_top
        h["placed"] = {}
        h["psum"] = [ctx.enter_context(nc.psum_tensor(f"bank{i}", [P, 512], F32)) for i in range(8)]
        h["load_sems"] = [sem(f"s_load{i}") for i in range(48)]
        h["out_sem"] = sem("s_out")
        at = TEMPS

        def place(name, at, shape):
            return nc.alloc_sbuf_tensor_at(name, shape, F32, offset=h["work"] + at)
        h["acc"] = place("acc", at, [P, 2 * T])
        h["sq"] = place("sq", at + 2048, [P, 2, 2 * T])
        h["tmp"] = place("tmp", at + 6144, [P, 2, 2 * T])
        h["sg"] = place("sg", at + 10240, [P, 2, 2 * T])
        h["sq2"] = h["sg"]
        h["ada_rows"] = place("ada_rows", at + 14336, [P, 2, 256])
        sems = {n: sem(f"s_{n}") for n in ("pe", "act", "dve", "pool")}
        raw_sems = [sem(f"s_raw{i}") for i in range(NRAW)]

        def engines():
            return [Engine(sems[n]) for n in ("pe", "act", "dve", "pool")] + [Engine(None)]

        rec = Recorder(whi, wlo, raw)
        Program(nc, io, h, engines(), rec).run()
        eng = engines()
        stream = Weights(rec.plan, whi, wlo, raw, eng[4], raw_sems, eng[1], eng[2], eng[3])
        prog = Program(nc, io, h, eng, stream)
        prog.run()
        prog.finish()

        block = ctx.enter_context(nc.Block())

        @block.sync
        def _(e):
            eng[4].emit(e)

        @block.tensor
        def _(e):
            eng[0].emit(e)

        @block.scalar
        def _(e):
            eng[1].emit(e)

        @block.vector
        def _(e):
            eng[2].emit(e)

        @block.gpsimd
        def _(e):
            eng[3].emit(e)


def shape_constants():
    f = np.float32
    out = {"ident": np.eye(P, dtype=f)}
    out["fold"] = np.tile(np.eye(32, 2), (4, 1))
    t = np.arange(T)
    ang = 2 * np.pi * np.outer(t, t) / T
    out["fourier_time"] = np.stack([np.concatenate([np.cos(ang), np.sin(ang)], 1)[b * P:(b + 1) * P] for b in range(TB)], 1)
    d = np.arange(HD)
    ang = 2 * np.pi * np.outer(d, d) / HD
    norm = 1.0 / math.sqrt(T * HD)
    two = np.eye(2)
    out["fourier_dim"] = np.stack([np.kron(two, np.cos(ang)) * norm, -np.kron(two, np.sin(ang)) * norm], 1)
    seg = np.ones((P, 2 * T))
    seg[:, ::GLA_CHUNK] = 0
    out["segments"] = seg
    big = 3.0e38
    j, i = np.meshgrid(np.arange(P), np.arange(P), indexing="ij")
    same = j // GLA_CHUNK == i // GLA_CHUNK
    lim = []
    for keep in (same & (j <= i), same & (j >= i)):
        lim += [np.where(keep, big, 0.0), np.where(keep, -big, 0.0)]
    out["limits"] = np.stack(lim, 1)[:, :, None, :]
    n = 16
    inv = (np.float32(10000.0) ** (-np.arange(n, dtype=f) / f(n))).astype(f)
    tok = np.arange(T)
    row, col = (tok // 64).astype(f), (tok % 64).astype(f)
    ang = np.concatenate([np.outer(inv, row)] * 2 + [np.outer(inv, col)] * 2, 0).astype(f)
    ang = np.concatenate([ang, ang], 0)
    out["axial"] = np.stack([np.cos(ang), np.sin(ang)], 1)
    rot = np.zeros((P, P))
    for m in range(P):
        if m % 32 < 16:
            rot[m + 16, m] = -1.0
        else:
            rot[m - 16, m] = 1.0
    out["axial_rot"] = rot
    rot = np.zeros((P, P))
    for m in range(0, P, 2):
        rot[m + 1, m] = -1.0
        rot[m, m + 1] = 1.0
    out["pair_rot"] = rot
    inv = (f(1.0) / (f(10000.0) ** np.linspace(0.0, 1.0, P, dtype=f))).astype(f)
    ang = (np.arange(T, dtype=f)[None, :] * np.repeat(inv, 2)[:, None]).astype(f).reshape(2, P, T)
    out["ret_rope"] = np.stack([np.cos(ang), np.sin(ang)], 0).transpose(2, 0, 1, 3)
    dec = []
    for hd in range(RET_HEADS):
        g = math.log(1.0 - 2.0 ** (-5.0 - hd))
        jj, ii = np.arange(P)[:, None], np.arange(T)[None, :]
        full = [np.where(ii >= jj + b * P, np.exp(np.maximum(ii - jj - b * P, 0) * g), 0.0) for b in range(2)]
        dec.append(np.concatenate([full[0], full[1][:, P:]], 1) * RET_DK ** -0.5)
    out["decay"] = np.stack(dec, 1)
    delta = np.arange(384) - 127
    onehot, mask = np.zeros((NUM_BUCKETS, 3, 384)), np.zeros((16, 3, 384))
    for g, (window, dil) in enumerate(DILATED):
        ok = (delta >= 0) & (delta <= window) & (delta % dil == 0)
        dist = np.maximum(delta, 0)
        exact = NUM_BUCKETS // 2
        large = exact + (np.log(np.maximum(dist, 1).astype(f) / f(exact)) / f(math.log(MAX_DISTANCE / exact))
                         * f(NUM_BUCKETS - exact)).astype(np.int32)
        bucket = np.where(dist < exact, dist, np.minimum(large, NUM_BUCKETS - 1))
        onehot[bucket[ok], g, np.arange(384)[ok]] = 1.0
        mask[:, g, ~ok] = NEG
    out["onehot"], out["dist_mask"] = onehot, mask
    return {k: np.ascontiguousarray(v, dtype=f) for k, v in out.items()}


def chunks(v):
    return v.reshape(-1, P).T


def tall(v):
    return np.concatenate([v, np.zeros((P - v.shape[0], v.shape[1]), v.dtype)], 0)


WEIGHTS = ["ada_w", "ffn1_w_in", "ffn1_w_out", "ffn2_w_in", "ffn2_w_out", "mix_w_out"]
PLAIN = {"even_w_in": "even_w_in", "odd_w_in": "odd_w_in", "ret_w_in": "ret_w_in_2", "ret_w_out": "ret_w_out_2",
         "attn_w_in": "attn_w_in_2", "attn_w_out": "attn_w_out_2"}
PAIRS = {"ffn_w_up": "ffn_w_up_2", "ffn_w_down": "ffn_w_down_2"}


def kernel(**inp):
    import concourse.bacc as bacc
    from concourse.bass_utils import run_bass_kernel_spmd

    a = {k: np.asarray(v) for k, v in inp.items()}
    small = {
        "cond": np.stack([chunks(a["c"][0]), chunks(a["c_ctx"])], 2).reshape(P, -1),
        "ada_b": chunks(a["ada_b"]), "norm_ffn1": chunks(a["norm_ffn1"]), "norm_mix": chunks(a["norm_mix"]),
        "norm_ffn2": chunks(a["norm_ffn2"]), "final_norm": chunks(a["final_norm"]), "gate_b": chunks(a["gla_gate_b"]),
        "gla_norm": chunks(a["gla_norm"]), "conv_w": chunks(a["conv_w"]), "conv_b": chunks(a["conv_b"]),
        "lambdas": tall(np.concatenate([a["lambda_q1"], a["lambda_q2"], a["lambda_k1"], a["lambda_k2"]], 0).T),
        "diff_norm": chunks(a["diff_norm"]), "ln_gain": chunks(a["ln_gain_2"]), "ln_bias": chunks(a["ln_bias_2"]),
        "rel_bias": tall(a["rel_bias_2"].T),
    }
    arrays = {"small": np.ascontiguousarray(np.concatenate([small[n] for n, _ in SMALL], 1))}
    both = np.concatenate([a["x"][0], a["ctx"][0]], 0)
    arrays["hT"] = np.ascontiguousarray(both.reshape(2 * T, KC, P).transpose(2, 1, 0))
    arrays["gate_w"] = np.ascontiguousarray(a["gla_gate_w"][0])
    for n in WEIGHTS:
        arrays[n] = a[n]
    for n, src in PLAIN.items():
        arrays[n] = a[src][0]
    for n, src in PAIRS.items():
        arrays[n] = a[src]
    arrays.update(shape_constants())

    nc = bacc.Bacc("TRN2", target_bir_lowering=False, num_devices=1)
    io = {n: nc.dram_tensor("in_" + n, v.shape, F32, kind="ExternalInput").ap() for n, v in arrays.items()}
    out = nc.dram_tensor("out_T", [P, KC, T], F32, kind="ExternalOutput")
    io["out"] = out.ap()
    rows = nc.dram_tensor("bias_rows", [ATT_GROUPS, ATT_HEADS, 384], F32, kind="Internal")
    io["bias_rows"] = rows.ap()
    io["bias_windows"] = lambda hd: bass.AP(tensor=rows, offset=hd * 384, ap=[[1, P], [ATT_HEADS * 384, 3], [1, T]])
    build(nc, io)
    r = run_bass_kernel_spmd(nc, [{"in_" + n: v for n, v in arrays.items()}], core_ids=[0])
    got = r.results[0]["out_T"]
    return np.ascontiguousarray(got.transpose(2, 1, 0)).reshape(1, T, D)
```
